# Optimizing a Trainium2 kernel written in Bass

```python
import math
import jax, jax.numpy as jnp
from jax import lax
import numpy as np

D_MODEL = 1024
BATCH = 1
SEQ = 128
DEPTH = 2
DEC_BATCH = 1
DEC_SEQ = 512
PAST_LEN = 128

GRID_W = 64
HEAD_DIM = 64
GQA_HEADS = 8
GQA_KV_HEADS = 2
GQA_GROUP = GQA_HEADS // GQA_KV_HEADS
GLA_HEADS = 4
GLA_DK = 64
GLA_DV = 128
GLA_RANK = 16
GLA_TAU = 16.0
GLA_CHUNK = 64
DIFF_HEADS = 4
DIFF_DV = 2 * HEAD_DIM
N_BRANCH = 3
BRANCH_W = 512
FFN_HIDDEN = ((8 * D_MODEL + 3 * 256 - 1) // (3 * 256)) * 256
ROPE_THETA = 10000.0
Q_BLOCK = 128
EPS = 1e-6
SPLIT_SIZES = (
    GQA_HEADS * HEAD_DIM, GQA_KV_HEADS * HEAD_DIM, GQA_KV_HEADS * HEAD_DIM,
    GLA_HEADS * GLA_DK, GLA_HEADS * GLA_DK, GLA_HEADS * GLA_DV, 2 * GLA_RANK, GLA_HEADS * GLA_DV,
    DIFF_HEADS * 2 * HEAD_DIM, DIFF_HEADS * 2 * HEAD_DIM, DIFF_HEADS * DIFF_DV,
    N_BRANCH * D_MODEL,
)
N_IN = sum(SPLIT_SIZES)

kernel_name = 'hybrid_diffusion_gqa_gla_diffattn_step'

def rms_norm(x, g):
    x32 = x.astype(jnp.float32)
    y = x32 * lax.rsqrt(jnp.mean(x32 * x32, axis=-1, keepdims=True) + EPS)
    return (y * g.astype(jnp.float32)).astype(x.dtype)

def split_columns(z):
    points, acc = [], 0
    for s in SPLIT_SIZES[:-1]:
        acc += s
        points.append(acc)
    return jnp.split(z, points, axis=-1)

def axial_rope_angles(n_tokens):
    n_rows = n_tokens // GRID_W
    row = jnp.repeat(jnp.arange(n_rows, dtype=jnp.float32), GRID_W)
    col = jnp.tile(jnp.arange(GRID_W, dtype=jnp.float32), n_rows)
    n_freq = HEAD_DIM // 4
    freqs = ROPE_THETA ** (-jnp.arange(n_freq, dtype=jnp.float32) / n_freq)
    return row[:, None] * freqs, col[:, None] * freqs

def rope_half(x, ang):
    ang = ang.reshape((1, ang.shape[0]) + (1,) * (x.ndim - 3) + (ang.shape[-1],))
    cos, sin = jnp.cos(ang), jnp.sin(ang)
    x1, x2 = jnp.split(x, 2, axis=-1)
    return jnp.concatenate([x1 * cos - x2 * sin, x2 * cos + x1 * sin], axis=-1)

def apply_axial_rope(x, angles):
    ang_row, ang_col = angles
    x32 = x.astype(jnp.float32)
    half = HEAD_DIM // 2
    out = jnp.concatenate([rope_half(x32[..., :half], ang_row), rope_half(x32[..., half:], ang_col)], axis=-1)
    return out.astype(x.dtype)

def sweep_query_blocks(fn, q):
    b, n = q.shape[:2]
    nb = n // Q_BLOCK
    blocks = jnp.moveaxis(q.reshape((b, nb, Q_BLOCK) + q.shape[2:]), 1, 0)
    out = lax.map(fn, blocks)
    return jnp.moveaxis(out, 0, 1).reshape((b, n) + out.shape[3:])

def gqa_block(q, k, v):
    s = jnp.einsum('bqkgd,bskd->bkgqs', q, k).astype(jnp.float32) * (HEAD_DIM ** -0.5)
    p = jax.nn.softmax(s, axis=-1).astype(v.dtype)
    return jnp.einsum('bkgqs,bskd->bqkgd', p, v)

def diff_block(q, k, v, lam):
    s = jnp.einsum('bqhmd,bshmd->bhmqs', q, k).astype(jnp.float32) * (HEAD_DIM ** -0.5)
    p = jax.nn.softmax(s, axis=-1)
    p = p[:, :, 0] - lam * p[:, :, 1]
    return jnp.einsum('bhqs,bshe->bqhe', p.astype(v.dtype), v)

def gla_chunked(q, k, v, log_a, s0):
    b, n, h, dk = q.shape
    dv = v.shape[-1]
    nc = n // GLA_CHUNK
    f32 = jnp.float32
    q = q.astype(f32).reshape(b, nc, GLA_CHUNK, h, dk)
    k = k.astype(f32).reshape(b, nc, GLA_CHUNK, h, dk)
    v = v.astype(f32).reshape(b, nc, GLA_CHUNK, h, dv)
    cum = jnp.cumsum(log_a.astype(f32).reshape(b, nc, GLA_CHUNK, h, dk), axis=2)
    last = cum[:, :, -1]
    q_dec = q * jnp.exp(cum)
    k_inv = k * jnp.exp(-cum)
    k_to_end = k * jnp.exp(last[:, :, None] - cum)
    mask = jnp.tril(jnp.ones((GLA_CHUNK, GLA_CHUNK), dtype=bool))
    a = jnp.where(mask, jnp.einsum('bcihd,bcjhd->bchij', q_dec, k_inv), 0.0)
    o_intra = jnp.einsum('bchij,bcjhe->bcihe', a, v)
    ds = jnp.einsum('bcjhd,bcjhe->bchde', k_to_end, v)

    def step(s, inp):
        decay, d = inp
        return decay[..., None] * s + d, s

    s_final, s_prev = lax.scan(step, s0.astype(f32), (jnp.moveaxis(jnp.exp(last), 1, 0), jnp.moveaxis(ds, 1, 0)))
    s_prev = jnp.moveaxis(s_prev, 0, 1)
    o_inter = jnp.einsum('bcihd,bchde->bcihe', q_dec, s_prev)
    return (o_intra + o_inter).reshape(b, n, h, dv), s_final

def gla_bidirectional(q, k, v, log_a, s0):
    o_f, s_f = gla_chunked(q, k, v, log_a[:, :, 0], s0[:, 0])
    flip = lambda t: jnp.flip(t, axis=1)
    o_b, s_b = gla_chunked(flip(q), flip(k), flip(v), flip(log_a[:, :, 1]), s0[:, 1])
    return o_f + flip(o_b), jnp.stack([s_f, s_b], axis=1)

def token_mixers(h, p, l, angles, ctx):
    b, n = h.shape[:2]
    (gq, gk, gv, lq, lk, lv, lr, lgo, dq, dk, dv, merge) = split_columns(h @ p['w_in'][l])
    gq = rms_norm(gq.reshape(b, n, GQA_HEADS, HEAD_DIM), p['gqa_q_norm'][l])
    gk = rms_norm(gk.reshape(b, n, GQA_KV_HEADS, HEAD_DIM), p['gqa_k_norm'][l])
    gv = gv.reshape(b, n, GQA_KV_HEADS, HEAD_DIM)
    dq = rms_norm(dq.reshape(b, n, DIFF_HEADS, 2, HEAD_DIM), p['diff_q_norm'][l])
    dk = rms_norm(dk.reshape(b, n, DIFF_HEADS, 2, HEAD_DIM), p['diff_k_norm'][l])
    dv = dv.reshape(b, n, DIFF_HEADS, DIFF_DV)
    if angles is not None:
        gq, gk = apply_axial_rope(gq, angles), apply_axial_rope(gk, angles)
        dq, dk = apply_axial_rope(dq, angles), apply_axial_rope(dk, angles)
    if ctx is None:
        gk_all, gv_all, dk_all, dv_all = gk, gv, dk, dv
        s0 = jnp.zeros((b, 2, GLA_HEADS, GLA_DK, GLA_DV), jnp.float32)
    else:
        c_gk, c_gv, c_state, c_dk, c_dv = ctx
        gk_all = jnp.concatenate([gk, c_gk.astype(gk.dtype)], axis=1)
        gv_all = jnp.concatenate([gv, c_gv.astype(gv.dtype)], axis=1)
        dk_all = jnp.concatenate([dk, c_dk.astype(dk.dtype)], axis=1)
        dv_all = jnp.concatenate([dv, c_dv.astype(dv.dtype)], axis=1)
        s0 = c_state
    gqa_out = sweep_query_blocks(lambda qb: gqa_block(qb, gk_all, gv_all),
                                 gq.reshape(b, n, GQA_KV_HEADS, GQA_GROUP, HEAD_DIM)).reshape(b, n, BRANCH_W)
    lq = lq.reshape(b, n, GLA_HEADS, GLA_DK) * (GLA_DK ** -0.5)
    lk = lk.reshape(b, n, GLA_HEADS, GLA_DK)
    lv = lv.reshape(b, n, GLA_HEADS, GLA_DV)
    z = jnp.einsum('bnzr,zrf->bnzf', lr.reshape(b, n, 2, GLA_RANK), p['gla_alpha_up'][l]) + p['gla_alpha_bias'][l]
    log_a = (jax.nn.log_sigmoid(z.astype(jnp.float32)) / GLA_TAU).reshape(b, n, 2, GLA_HEADS, GLA_DK)
    o_gla, s_new = gla_bidirectional(lq, lk, lv, log_a, s0)
    gla_out = rms_norm(o_gla.astype(h.dtype), p['gla_out_norm'][l]) * jax.nn.silu(lgo.reshape(b, n, GLA_HEADS, GLA_DV))
    gla_out = gla_out.reshape(b, n, BRANCH_W)
    lam_init = 0.8 - 0.6 * math.exp(-0.3 * l)
    lp = p['diff_lambda'][l].astype(jnp.float32)
    lam = jnp.exp(jnp.sum(lp[0] * lp[1])) - jnp.exp(jnp.sum(lp[2] * lp[3])) + lam_init
    d_out = sweep_query_blocks(lambda qb: diff_block(qb, dk_all, dv_all, lam), dq)
    diff_out = (rms_norm(d_out, p['diff_sub_norm'][l]) * (1.0 - lam_init)).reshape(b, n, BRANCH_W)
    outs = jnp.stack([gqa_out, gla_out, diff_out], axis=2)
    y = jnp.einsum('bnie,ied->bnid', outs, p['w_branch'][l])
    gates = jax.nn.sigmoid(merge.reshape(b, n, N_BRANCH, D_MODEL))
    mixed = jnp.sum(gates * y, axis=2) @ p['w_out'][l]
    return mixed, (gk, gv, s_new.astype(h.dtype), dk, dv)

def layer(x, cond, p, l, angles, ctx):
    mod = jax.nn.silu(cond) @ p['w_mod'][l] + p['b_mod'][l]
    sh1, sc1, g1, sh2, sc2, g2 = jnp.split(mod, 6, axis=-1)
    h = rms_norm(x, p['norm1'][l]) * (1.0 + sc1) + sh1
    mixed, ctx_out = token_mixers(h, p, l, angles, ctx)
    x = x + g1 * mixed
    h = rms_norm(x, p['norm2'][l]) * (1.0 + sc2) + sh2
    a, u = jnp.split(h @ p['w_ffn_in'][l], 2, axis=-1)
    x = x + g2 * ((jax.nn.silu(a) * u) @ p['w_ffn_out'][l])
    return x, ctx_out

def setup_inputs(seed: int = 0) -> dict:
    key = jax.random.key(seed)
    ks = jax.random.split(key, 32)
    nrm = lambda k, shape, s=1.0: jax.random.normal(k, shape, jnp.float32) * s
    gain = lambda k, shape: 1.0 + 0.02 * jax.random.normal(k, shape, jnp.float32)
    return {
        'x_prompt': nrm(ks[0], (BATCH, SEQ, D_MODEL)),
        'x_sample': nrm(ks[1], (DEC_BATCH, DEC_SEQ, D_MODEL)),
        'c': nrm(ks[2], (DEC_BATCH, D_MODEL)),
        'cache_gqa_k': nrm(ks[3], (DEC_BATCH, DEPTH, PAST_LEN, GQA_KV_HEADS, HEAD_DIM)),
        'cache_gqa_v': nrm(ks[4], (DEC_BATCH, DEPTH, PAST_LEN, GQA_KV_HEADS, HEAD_DIM)),
        'state_gla': nrm(ks[5], (DEC_BATCH, DEPTH, 2, GLA_HEADS, GLA_DK, GLA_DV)),
        'cache_diff_k': nrm(ks[6], (DEC_BATCH, DEPTH, PAST_LEN, DIFF_HEADS, 2, HEAD_DIM)),
        'cache_diff_v': nrm(ks[7], (DEC_BATCH, DEPTH, PAST_LEN, DIFF_HEADS, DIFF_DV)),
        'c_ctx': nrm(ks[8], (D_MODEL,)),
        'w_mod': nrm(ks[9], (DEPTH, D_MODEL, 6 * D_MODEL), 0.5 * D_MODEL ** -0.5),
        'b_mod': nrm(ks[10], (DEPTH, 6 * D_MODEL), 0.01),
        'norm1': gain(ks[11], (DEPTH, D_MODEL)),
        'norm2': gain(ks[12], (DEPTH, D_MODEL)),
        'w_in': nrm(ks[13], (DEPTH, D_MODEL, N_IN), D_MODEL ** -0.5),
        'gqa_q_norm': gain(ks[14], (DEPTH, HEAD_DIM)),
        'gqa_k_norm': gain(ks[15], (DEPTH, HEAD_DIM)),
        'gla_alpha_up': nrm(ks[16], (DEPTH, 2, GLA_RANK, GLA_HEADS * GLA_DK), GLA_RANK ** -0.5),
        'gla_alpha_bias': nrm(ks[17], (DEPTH, 2, GLA_HEADS * GLA_DK), 0.1),
        'gla_out_norm': gain(ks[18], (DEPTH, GLA_DV)),
        'diff_q_norm': gain(ks[19], (DEPTH, HEAD_DIM)),
        'diff_k_norm': gain(ks[20], (DEPTH, HEAD_DIM)),
        'diff_lambda': nrm(ks[21], (DEPTH, 4, HEAD_DIM), 0.1),
        'diff_sub_norm': gain(ks[22], (DEPTH, DIFF_DV)),
        'w_branch': nrm(ks[23], (DEPTH, N_BRANCH, BRANCH_W, D_MODEL), BRANCH_W ** -0.5),
        'w_out': nrm(ks[24], (DEPTH, D_MODEL, D_MODEL), D_MODEL ** -0.5),
        'w_ffn_in': nrm(ks[25], (DEPTH, D_MODEL, 2 * FFN_HIDDEN), D_MODEL ** -0.5),
        'w_ffn_out': nrm(ks[26], (DEPTH, FFN_HIDDEN, D_MODEL), FFN_HIDDEN ** -0.5),
    }

def reference(x_prompt, x_sample, c, cache_gqa_k, cache_gqa_v, state_gla, cache_diff_k, cache_diff_v,
              c_ctx, w_mod, b_mod, norm1, norm2, w_in, gqa_q_norm, gqa_k_norm, gla_alpha_up, gla_alpha_bias,
              gla_out_norm, diff_q_norm, diff_k_norm, diff_lambda, diff_sub_norm, w_branch, w_out,
              w_ffn_in, w_ffn_out):
    p = {
        'w_mod': w_mod, 'b_mod': b_mod, 'norm1': norm1, 'norm2': norm2, 'w_in': w_in,
        'gqa_q_norm': gqa_q_norm, 'gqa_k_norm': gqa_k_norm, 'gla_alpha_up': gla_alpha_up,
        'gla_alpha_bias': gla_alpha_bias, 'gla_out_norm': gla_out_norm, 'diff_q_norm': diff_q_norm,
        'diff_k_norm': diff_k_norm, 'diff_lambda': diff_lambda, 'diff_sub_norm': diff_sub_norm,
        'w_branch': w_branch, 'w_out': w_out, 'w_ffn_in': w_ffn_in, 'w_ffn_out': w_ffn_out,
    }
    y_prompt = x_prompt
    cond_ctx = c_ctx[None, None, :]
    ctx_tensors = []
    for l in range(DEPTH):
        y_prompt, ctx_t = layer(y_prompt, cond_ctx, p, l, None, None)
        ctx_tensors.append(ctx_t)
    new_gqa_k = jnp.stack([t[0] for t in ctx_tensors], axis=1)
    new_gqa_v = jnp.stack([t[1] for t in ctx_tensors], axis=1)
    new_state_gla = jnp.stack([t[2] for t in ctx_tensors], axis=1)
    new_diff_k = jnp.stack([t[3] for t in ctx_tensors], axis=1)
    new_diff_v = jnp.stack([t[4] for t in ctx_tensors], axis=1)
    angles = axial_rope_angles(x_sample.shape[1])
    y_sample = x_sample
    cond_lat = c[:, None, :]
    for l in range(DEPTH):
        ctx = (cache_gqa_k[:, l], cache_gqa_v[:, l], state_gla[:, l], cache_diff_k[:, l], cache_diff_v[:, l])
        y_sample, _ = layer(y_sample, cond_lat, p, l, angles, ctx)
    return (y_prompt, y_sample, new_gqa_k, new_gqa_v, new_state_gla, new_diff_k, new_diff_v)


_drawn_inputs = setup_inputs


def setup_inputs(seed=0):
    import zlib

    import numpy as np

    out = dict(_drawn_inputs(seed))
    spreads = {}
    factors = {'cache_gqa_k': 8.0,
     'cache_gqa_v': 7.8,
     'state_gla': 8.0,
     'norm2': 6.828,
     'gqa_q_norm': 8.0,
     'gqa_k_norm': 7.666,
     'gla_out_norm': 22.955,
     'diff_q_norm': 8.0,
     'diff_k_norm': 2.916,
     'diff_lambda': 3.588,
     'diff_sub_norm': 30.863,
     'cache_diff_k': 8.0,
     'cache_diff_v': 8.0}
    for name, (base, spread) in spreads.items():
        noise = np.random.default_rng([zlib.crc32(name.encode()), seed]).standard_normal(out[name].shape)
        drawn = base * np.exp(spread * noise) if base else spread * noise
        out[name] = __import__('jax').numpy.asarray(drawn.astype(out[name].dtype))
    for name, factor in factors.items():
        out[name] = (out[name] * factor).astype(out[name].dtype)
    return out
```

```python
import math
from contextlib import ExitStack, contextmanager

import numpy as np

import concourse.bass as bass
from concourse import mybir

F32 = mybir.dt.float32
F32R = mybir.dt.float32r
I32 = mybir.dt.int32
ACT = mybir.ActivationFunctionType
ALU = mybir.AluOpType
AX = mybir.AxisListType
ds = bass.ds

P = 128
D = 1024
KT = D // P
DEPTH = 2
SEQ, DEC, PAST = 128, 512, 128
TT = (SEQ + DEC) // P
CTX = TT - 1
HALF = 320
TILE_AT = [0, 128, 384, 512, 256]
T = 2 * HALF
HD = 64
BW = 512
RANK = 16
TAU = 16.0
CH = 64
NCH = T // CH
FF = 2816
FT = FF // P
EPS = 1e-6
SLAB = 2048
W256 = 256
C_GQ, C_GK, C_GV, C_LQ, C_LK, C_LV, C_LR, C_LGO, C_DQ, C_DK, C_DV, C_MG = (
    0, 512, 640, 768, 1024, 1280, 1792, 1824, 2336, 2848, 3360, 3872)
K_ID, K_ONE, K_SEL, K_LAM = 0, 128, 256, 258
K_COLS = 264
G_MF, G_MB, G_CM, G_COLS = 0, 128, 256, 256 + T
RING = 10
ROW_BANK = [0, 1, 2, 3, 4, 5, 6, 7, 0, 1]
ROW_BACK = [2, 2, 10, 10, 10, 10, 10, 10, 8, 8]


class Signal:

    def __init__(self, sem):
        self.sem, self.base, self.local = sem, 0, 0

    def step(self, ins, by=1):
        ins.then_inc(self.sem, by)
        self.local += by
        return self.sem, self.base + self.local


@contextmanager
def loop(eng, start, stop, **per_round):
    began = {k: s.base + s.local for k, (s, _) in per_round.items()}
    with eng.Fori(start, stop) as i:
        for k, (s, n) in per_round.items():
            s.base, s.local = began[k] + (i - start) * n, 0
        yield i
        for k, (s, n) in per_round.items():
            assert s.local == n, (k, s.local, n)
    for k, (s, n) in per_round.items():
        s.base, s.local = began[k] + (stop - start) * n, 0


def tok(buf, tt):
    return buf[:, TILE_AT[tt]:TILE_AT[tt] + P]


def chunk_pos(idx):
    return TILE_AT[idx // 2] // CH + idx % 2


def segments(buf):
    step = buf.ap[-1][0]
    assert step == 1
    lat = bass.AP(buf.tensor, buf.offset, [list(buf.ap[0]), [384, 2], [1, 256]])
    return lat, buf[:, 256:384].rearrange("p (h c) -> p h c", h=2)


def psum_segments(ps, pair):
    base = ps[:, 2 * pair, :]
    return [bass.AP(base.tensor, base.offset + at, [list(base.ap[0]), [step, 2], [1, n]])
            for at, step, n in ((0, 576, 256), (256, 256, CH))]


class Stages:

    def __init__(self, nc, ctx):
        self.nc, self.ctx, self.sems = nc, ctx, {}
        at = self.at
        self.xT = at("xT", [P, KT, T], 0)
        self.hH = at("hH", [P, KT, T], 20480, F32R)
        self.hL = at("hL", [P, KT, T], 40960, F32R)
        self.raw = at("raw", [P, 2, SLAB], 61440)
        self.wH = at("wH", [P, 2, SLAB], 77824, F32R)
        self.wL = at("wL", [P, 2, SLAB], 94208, F32R)
        x0, x1 = 110592, 110592 + 61440
        small = [x1 + 30720]

        def place(name, shape):
            t = at(name, shape, small[0])
            small[0] += -(-4 * int(np.prod(shape[1:])) // 32) * 32
            return t

        self.cst = place("cst", [P, K_COLS])
        self.sc = place("sc", [P, KT, 2])
        self.mod = place("mod", [P, 48, 2])
        self.aff = place("aff", [P, 2, KT, 2])
        self.nw = place("nw", [P, 2, KT])
        self.nlam = place("nlam", [P, 4])
        self.lp = place("lp", [P, 4 * HD])
        self.gains = place("gains", [P, 4, HD])
        self.subn = place("subn", [P, P])
        self.lpw = place("lpw", [P, 2, HD])
        self.sml = place("sml", [P, 160])
        assert small[0] + 16512 <= 229344
        self.mrow = at("mrow", [3, 6 * D], x0)
        self.sq = at("sq", [P, 2, T], x0)
        self.std = at("std", [P, T], x0 + 5120)
        self.rstd = at("rstd", [P, T], x0 + 7680)
        self.xn = at("xn", [P, 2, T], x0 + 10240)
        self.hf = at("hf", [P, 2, T], x0 + 15360)
        self.xrow = at("xrow", [P, 2, D], x0)
        self.lv = at("lv", [P, TT, BW], x0)
        self.lg = at("lg", [P, TT, BW], x0 + 10240)
        self.lT = at("lT", [P, 5, T], x0 + 20480)
        g = x0 + 33280
        self.g_min, self.g_abs, self.g_sp, self.g_la, self.g_cum, self.g_eq, self.g_ek = [
            at(name, [P, T], g + 2560 * n)
            for n, name in enumerate(("g_min", "g_abs", "g_sp", "g_la", "g_cum", "g_eq", "g_ek"))]
        g = x1
        self.g_qd = at("g_qd", [P, T], x0 + 33280 + 17920)
        self.g_ki = at("g_ki", [P, T], x0 + 33280 + 20480)
        self.g_ke = at("g_ke", [P, T], x0 + 33280 + 23040)
        self.g_ker = at("g_ker", [P, TT, P], g)
        self.g_s = at("g_s", [P, NCH, P], g + 2560)
        self.g_sf = at("g_sf", [P, P], g + 7680)
        self.g_am = at("g_am", [P, 2, 2, 2, P], g + 8192)
        self.g_au = at("g_au", [32, 2, 256], g + 12288)
        self.g_cst = at("g_cst", [P, G_COLS], g + 14336)
        self.g_on = at("g_on", [P, P], g + 17920)
        self.g_ab = at("g_ab", [P, 2, 2], g + 18432)
        self.g_dec = at("g_dec", [P, NCH], g + 18464)
        self.g_st = at("g_st", [P, 80], g + 18528)
        self.g_sq = at("g_sq", [P, TT, BW], x0 + 33280)
        self.rq = at("rq", [P, 8, TT, P], x1)
        self.glr = at("glr", [P, TT, BW], x1 + 20480)
        self.kv = at("kv", [P, 11, TT + 1, P], x0)
        a = x0 + 33792
        self.r_sq = at("r_sq", [P, 2 * T], a)
        self.r_t = at("r_t", [P, 2 * T], a + 5120)
        self.r_c = at("r_c", [P, 4, TT, HD], a + 10240)
        self.r_s = at("r_s", [P, 4, TT, HD], a + 15360)
        self.r_tab = at("r_tab", [P, 2, TT, HD], a + 20480)
        self.r_st = at("r_st", [P, 4, 20], a + 23040)
        self.e = at("e", [P, 4, T], a)
        self.eT = at("eT", [P, 2, TT, P], a + 10240)
        self.a_st = at("a_st", [P, 32, 8], a + 15360)
        self.o_sq = at("o_sq", [P, 4, T], a + 16384)
        self.oH = at("oH", [P, 12, T], x0, F32R)
        self.oL = at("oL", [P, 12, T], x0 + 30720, F32R)
        self.mix = at("mix", [P, KT, T], x1)
        self.gate = at("gate", [P, 2, T], x1 + 20480)
        self.gy = at("gy", [P, 2, T], x1 + 25600)
        self.gH = at("gH", [P, 12, T], x0, F32R)
        self.gL = at("gL", [P, 12, T], x0 + 30720, F32R)
        self.act = at("act", [P, 2, T], x1)
        self.gf = at("gf", [P, 2, T], x1 + 5120)
        self.ps = ctx.enter_context(nc.psum_tensor("ps", [P, 8, 512], F32))

    def at(self, name, shape, offset, dt=F32):
        return self.nc.alloc_sbuf_tensor_at(name, shape, dt, offset=16512 + offset)

    def sem(self, name):
        if name not in self.sems:
            self.sems[name] = self.ctx.enter_context(self.nc.semaphore(name))
        return self.sems[name]

    @contextmanager
    def block(self):
        with self.nc.Block() as block:
            yield block
        nums = [s.num for s in self.sems.values()]
        self.nc.gpsimd.sem_clear(range(min(nums), max(nums) + 1))
        self.nc.all_engine_barrier()


def flat(ap):
    return ap.rearrange("p h c -> p (h c)")


def halves(ap):
    return ap.rearrange("p (h c) -> p h c", h=2)


def high_part(nc, m, act, slot, loaded, used=None):
    act.wait_ge(m.sem(f"slab_loaded{slot}"), loaded)
    if used is not None:
        act.wait_ge(*used)
    nc.scalar.activation(m.wH[:, slot, :], m.raw[:, slot, :], ACT.Copy).then_inc(m.sem("high_ready"), 1)


def low_part(nc, m, dve, s, slot):
    dve.wait_ge(m.sem("high_ready"), s + 1)
    nc.vector.tensor_tensor(m.wL[:, slot, :], m.raw[:, slot, :], m.wH[:, slot, :].bitcast(F32),
                            ALU.subtract).then_inc(m.sem("low_ready"), 1)


def transposed_tile(nc, m, slot, col, cols, nk, aH, aL, k0, pair):
    wh = m.wH[:, slot, 0:nk * cols].rearrange("p (k c) -> p k c", k=nk)
    wl = m.wL[:, slot, 0:nk * cols].rearrange("p (k c) -> p k c", k=nk)
    for k in range(nk):
        for q, (w, a) in enumerate(((wl, aH), (wh, aL), (wh, aH))):
            for n in range(2):
                last = nc.tensor.matmul(m.ps[:, 2 * pair + n, 0:HALF], w[:, k, col:col + P],
                                        a[:, k0 + k, n * HALF:(n + 1) * HALF],
                                        start=(k == 0 and q == 0), stop=(k == nk - 1 and q == 2))
    return last


def row_tile(nc, m, slot, tt, bank):
    wh = m.wH[:, slot, :].rearrange("p (k c) -> p k c", k=KT)
    wl = m.wL[:, slot, :].rearrange("p (k c) -> p k c", k=KT)
    for k in range(KT):
        for q, (a, w) in enumerate(((m.hL, wh), (m.hH, wl), (m.hH, wh))):
            last = nc.tensor.matmul(m.ps[:, bank, 0:W256], tok(a[:, k, :], tt), w[:, k, :],
                                    start=(k == 0 and q == 0), stop=(k == KT - 1 and q == 2))
    return last


def k_tiles(w, L, c0, n):
    return w[ds(L, 1), :, ds(c0, n)].rearrange("a (k p) c -> p (a k) c", p=P)


def first_stage(nc, m, d):
    with m.block() as block:
        @block.sync
        def _(sp):
            sp.dma_start(m.cst[:, :], d["const_all"]).then_inc(m.sem("constants"), 16)
            for tt in range(TT):
                if tt >= 2:
                    sp.wait_ge(m.sem("row_turned"), tt - 1)
                src = d["x_sample"][0, tt * P:(tt + 1) * P, :] if tt < CTX else d["x_prompt"][0, :, :]
                sp.dma_start(m.xrow[:, tt % 2, :], src).then_inc(m.sem(f"row{tt % 2}"), 16)

        @block.scalar
        def _(act):
            act.dma_start(m.sc[:, :, 0:1], d["c"].rearrange("a (k p) -> p k a", p=P),
                          allow_slow_non_contiguous=True).then_inc(m.sem("cond"), 16)
            act.dma_start(m.sc[:, :, 1:2], d["c_ctx"].rearrange("(a k p) -> p k a", p=P, a=1),
                          allow_slow_non_contiguous=True).then_inc(m.sem("cond"), 16)
            act.wait_ge(m.sem("cond"), 32)
            nc.scalar.activation(m.sc[:, :, :], m.sc[:, :, :], ACT.Silu).then_inc(m.sem("silu"), 1)

        @block.tensor
        def _(pe):
            pe.wait_ge(m.sem("constants"), 16)
            for tt in range(TT):
                pe.wait_ge(m.sem(f"row{tt % 2}"), 16 * (tt // 2 + 1))
                if tt >= 4:
                    pe.wait_ge(m.sem("copied"), tt - 3)
                for k in range(KT):
                    b = 2 * (tt % 4) + k // 4
                    last = nc.tensor.transpose(m.ps[:, b, (k % 4) * P:(k % 4 + 1) * P],
                                               m.xrow[:, tt % 2, k * P:(k + 1) * P], m.cst[:, K_ID:K_ID + P])
                last.then_inc(m.sem("row_turned"), 1)

        @block.vector
        def _(dve):
            for tt in range(TT):
                dve.wait_ge(m.sem("row_turned"), tt + 1)
                b = 2 * (tt % 4)
                src = m.ps[:, b:b + 2, :].rearrange("p b (k c) -> p (b k) c", k=4)
                nc.vector.tensor_copy(m.xT[:, :, TILE_AT[tt]:TILE_AT[tt] + P], src).then_inc(m.sem("copied"), 1)


def modulation(nc, m, d, L):
    slabs = 6 * D // W256
    with m.block() as block:
        @block.sync
        def _(sp):
            for s in range(2):
                sp.dma_start(m.raw[:, s, :].rearrange("p (k c) -> p k c", k=KT),
                             k_tiles(d["w_mod"], L, s * W256, W256)).then_inc(m.sem(f"slab_loaded{s}"), 16)
            with sp.Fori(1, slabs // 2) as i:
                for s in range(2):
                    sp.wait_ge(m.sem("slab_used"), 2 * i + s - 1)
                    sp.dma_start(m.raw[:, s, :].rearrange("p (k c) -> p k c", k=KT),
                                 k_tiles(d["w_mod"], L, i * (2 * W256) + s * W256, W256)
                                 ).then_inc(m.sem(f"slab_loaded{s}"), 16)

        @block.tensor
        def _(pe):
            with pe.Fori(0, slabs // 2) as i:
                for s in range(2):
                    raw = m.raw[:, s, :].rearrange("p (k c) -> p k c", k=KT)
                    pe.wait_ge(m.sem(f"slab_loaded{s}"), 16 * i + 16)
                    pe.wait_ge(m.sem("mod_copied"), 2 * i + s + 1)
                    for k in range(KT):
                        last = nc.tensor.matmul(m.ps[0:2, s, 0:W256], m.sc[:, k, :], raw[:, k, :],
                                                start=(k == 0), stop=(k == KT - 1))
                    last.then_inc(m.sem("slab_used"), 1)
            pe.wait_ge(m.sem("mod_copied"), slabs + 2)
            pe.wait_ge(m.sem("bias_row"), 16)
            for t in range(48):
                last = nc.tensor.matmul(m.ps[:, 2, 2 * t:2 * t + 2], m.mrow[0:3, t * P:(t + 1) * P],
                                        m.cst[0:3, K_SEL:K_SEL + 2], start=True, stop=True)
            last.then_inc(m.sem("mod_turned"), 1)

        @block.scalar
        def _(act):
            small = m.sem("small_params")
            act.dma_start(m.mrow[2:3, :], d["b_mod"][ds(L, 1), :]).then_inc(m.sem("bias_row"), 16)
            act.dma_start(m.nw[:, 0, :], d["norm1"][ds(L, 1), :].rearrange("a (k p) -> p (a k)", p=P),
                           allow_slow_non_contiguous=True).then_inc(small, 16)
            act.dma_start(m.nw[:, 1, :], d["norm2"][ds(L, 1), :].rearrange("a (k p) -> p (a k)", p=P),
                           allow_slow_non_contiguous=True).then_inc(small, 16)
            for n, name in enumerate(("gqa_q_norm", "diff_q_norm", "gqa_k_norm", "diff_k_norm")):
                act.dma_start(m.gains[:, n, :], d[name][ds(L, 1), :].rearrange("a c -> (a c)").
                               partition_broadcast(P)).then_inc(small, 16)
            act.dma_start(m.subn[:, :], d["diff_sub_norm"][ds(L, 1), :].rearrange("a c -> (a c)").
                           partition_broadcast(P)).then_inc(small, 16)
            act.dma_start(m.lp[:, :], d["diff_lambda"][ds(L, 1), :, :].rearrange("a b c -> (a b c)").
                           partition_broadcast(P)).then_inc(small, 16)
            act.dma_start(m.nlam[:, 0:2], d["const_lam"][ds(L, 1), :].rearrange("a c -> (a c)").
                           partition_broadcast(P)).then_inc(small, 16)
            act.sem_inc(m.sem("mod_copied"), 2)
            with act.Fori(0, slabs // 2) as i:
                for s in range(2):
                    act.wait_ge(m.sem("slab_used"), 2 * i + s + 1)
                    nc.scalar.activation(m.mrow[0:2, ds(i * (2 * W256) + s * W256, W256)], m.ps[0:2, s, 0:W256],
                                         ACT.Copy).then_inc(m.sem("mod_copied"), 1)
            act.wait_ge(m.sem("lam_sums"), 2)
            nc.scalar.activation(m.nlam[:, 2:4], m.nlam[:, 2:4], ACT.Exp).then_inc(m.sem("lam_exp"), 1)

        @block.vector
        def _(dve):
            order = Signal(m.sem("dve_order"))
            dve.wait_ge(m.sem("small_params"), 9 * 16)
            lp = m.lp[:, :].rearrange("p (a b c) -> p a b c", a=2, b=2)
            done = order.step(nc.vector.tensor_tensor(m.lpw[:, :, :], lp[:, :, 0, :], lp[:, :, 1, :], ALU.mult))
            dve.wait_ge(*done)
            nc.vector.tensor_reduce(m.nlam[:, 2:4], m.lpw[:, :, :], AX.X, ALU.add).then_inc(m.sem("lam_sums"), 2)
            dve.wait_ge(m.sem("lam_exp"), 1)
            done = order.step(nc.vector.tensor_tensor(m.nlam[:, 2:3], m.nlam[:, 3:4], m.nlam[:, 2:3], ALU.subtract))
            dve.wait_ge(*done)
            done = order.step(nc.vector.tensor_tensor(m.nlam[:, 0:1], m.nlam[:, 2:3], m.nlam[:, 0:1], ALU.add))
            order.step(nc.vector.tensor_scalar(m.subn[:, :], m.subn[:, :], m.nlam[:, 1:2], None, ALU.mult))
            dve.wait_ge(m.sem("mod_turned"), 1)
            done = order.step(nc.vector.tensor_copy(m.mod[:, :, :], m.ps[:, 2, 0:96].rearrange("p (t c) -> p t c", c=2)))
            dve.wait_ge(*done)
            for n, first in enumerate((8, 32)):
                done = order.step(nc.vector.tensor_scalar(m.aff[:, n, :, :], m.mod[:, first:first + KT, :], 1.0, None, ALU.add))
                dve.wait_ge(*done)
                order.step(nc.vector.tensor_tensor(m.aff[:, n, :, :], m.aff[:, n, :, :],
                                                   m.nw[:, n, :].unsqueeze(2).broadcast_to([P, KT, 2]), ALU.mult))


def norm(nc, m, which):
    shift = (0, 24)[which]
    with m.block() as block:
        @block.scalar
        def _(act):
            for k in range(KT):
                if k >= 2:
                    act.wait_ge(m.sem("summed"), k - 1)
                nc.scalar.activation(m.sq[:, k % 2, :], m.xT[:, k, :], ACT.Square).then_inc(m.sem("squares"), 1)
            act.wait_ge(m.sem("summed"), KT)
            nc.scalar.activation(halves(m.std[:, :]), m.ps[:, 0:2, 0:HALF], ACT.Sqrt,
                                 bias=m.cst[:, K_LAM + 4:K_LAM + 5]).then_inc(m.sem("std"), 1)
            for k in range(KT):
                act.wait_ge(m.sem("normed"), k + 1)
                if k >= 2:
                    act.wait_ge(m.sem("low"), k - 1)
                for c, (o, i) in enumerate(zip(segments(m.hf[:, k % 2, :]), segments(m.xn[:, k % 2, :]))):
                    ins = nc.scalar.activation(o, i, ACT.Identity, bias=m.mod[:, shift + k, c:c + 1],
                                               scale=m.aff[:, which, k, c:c + 1])
                ins.then_inc(m.sem("shifted"), 1)
                act.wait_ge(m.sem("shifted"), k + 1)
                nc.scalar.activation(m.hH[:, k, :], m.hf[:, k % 2, :], ACT.Copy).then_inc(m.sem("high"), 1)

        @block.tensor
        def _(pe):
            for k in range(KT):
                pe.wait_ge(m.sem("squares"), k + 1)
                for n in range(2):
                    last = nc.tensor.matmul(m.ps[:, n, 0:HALF], m.cst[:, K_ONE:K_ONE + P],
                                            m.sq[:, k % 2, n * HALF:(n + 1) * HALF], start=(k == 0), stop=(k == KT - 1))
                last.then_inc(m.sem("summed"), 1)

        @block.vector
        def _(dve):
            dve.wait_ge(m.sem("std"), 1)
            nc.vector.reciprocal(m.rstd[:, :], m.std[:, :]).then_inc(m.sem("rstd"), 1)
            dve.wait_ge(m.sem("rstd"), 1)
            for k in range(KT + 1):
                if k < KT:
                    if k >= 2:
                        dve.wait_ge(m.sem("shifted"), k - 1)
                    nc.vector.tensor_tensor(m.xn[:, k % 2, :], m.xT[:, k, :], m.rstd[:, :], ALU.mult
                                            ).then_inc(m.sem("normed"), 1)
                if k >= 1:
                    dve.wait_ge(m.sem("high"), k)
                    nc.vector.tensor_tensor(m.hL[:, k - 1, :], m.hf[:, (k - 1) % 2, :],
                                            m.hH[:, k - 1, :].bitcast(F32), ALU.subtract).then_inc(m.sem("low"), 1)


def project_gla(nc, m, d, L):
    cols = [C_LV, C_LV + 256, C_LGO, C_LGO + 256, C_LQ, C_LK, C_LR]
    rows, n = 4, len(cols)
    tiles = {4: (0, 1), 5: (0, 1), 6: (0,)}
    done_after = [5, 10, 15, 20, 22, 24, 25]
    with m.block() as block:
        @block.sync
        def _(sp):
            for s, c in enumerate(cols):
                if s >= 2:
                    sp.wait_ge(m.sem("low_ready"), s - 1)
                sp.dma_start(m.raw[:, s % 2, :].rearrange("p (k c) -> p k c", k=KT),
                             k_tiles(d["w_in"], L, c, W256)).then_inc(m.sem(f"slab_loaded{s % 2}"), 16)

        @block.scalar
        def _(act):
            def high(s):
                high_part(nc, m, act, s % 2, 16 * (s // 2 + 1), (m.sem("tile_done"), done_after[s - 2]) if s > 1 else None)

            high(0)
            for s in range(n):
                if s + 1 < n:
                    high(s + 1)
                if s < rows:
                    dst = m.lv if s < 2 else m.lg
                    for tt in range(TT):
                        act.wait_ge(m.sem("tile_done"), 5 * s + tt + 1)
                        nc.scalar.activation(dst[:, tt, (s % 2) * 256:(s % 2 + 1) * 256],
                                             m.ps[:, ROW_BANK[(5 * s + tt) % RING], 0:256], ACT.Copy
                                             ).then_inc(m.sem("tile_copied"), 1)
                else:
                    for col in tiles[s]:
                        t = 2 * (s - rows) + col
                        act.wait_ge(m.sem("tile_done"), 20 + t + 1)
                        nc.scalar.activation(halves(m.lT[:, t, :]), m.ps[:, 2 * (t % 4):2 * (t % 4) + 2, 0:HALF],
                                             ACT.Copy, scale=(HD ** -0.5 if t < 2 else 1.0)
                                             ).then_inc(m.sem("tile_copied"), 1)

        @block.vector
        def _(dve):
            for s in range(n):
                low_part(nc, m, dve, s, s % 2)

        @block.tensor
        def _(pe):
            for s in range(n):
                pe.wait_ge(m.sem("low_ready"), s + 1)
                if s < rows:
                    for tt in range(TT):
                        g = 5 * s + tt
                        back = ROW_BACK[g % RING]
                        if g >= back:
                            pe.wait_ge(m.sem("tile_copied"), g - back + 1)
                        row_tile(nc, m, s % 2, tt, ROW_BANK[g % RING]).then_inc(m.sem("tile_done"), 1)
                else:
                    for col in tiles[s]:
                        t = 2 * (s - rows) + col
                        pe.wait_ge(m.sem("tile_copied"), 20 if t < 4 else 20 + t - 3)
                        transposed_tile(nc, m, s % 2, col * P, W256, KT, m.hH, m.hL, 0, t % 4
                                        ).then_inc(m.sem("tile_done"), 1)


def gla(nc, m, d, L):
    units = [(hp, dr) for hp in range(2) for dr in range(2)]
    def ds_at(idx, rows=slice(0, P)):
        tt, half = idx // 2, idx % 2
        return m.ps[rows, (2, 0)[half] + tt // 4, (tt % 4) * P:(tt % 4 + 1) * P]

    with m.block() as block:
        @block.gpsimd
        def _(pool):
            pool.memset(m.g_au[:, :, :], 0.0).then_inc(m.sem("au_zero"), 1)
            pool.memset(m.g_am[:, :, :, :, :], 0.0).then_inc(m.sem("am_zero"), 1)

        @block.sync
        def _(sp):
            ld = m.sem("gla_params")
            sp.dma_start(m.g_cst[:, :], d["const_gla"]).then_inc(ld, 16)
            sp.wait_ge(m.sem("au_zero"), 1)
            for z in range(2):
                sp.dma_start(m.g_au[RANK * z:RANK * (z + 1), z, :],
                             d["gla_alpha_up"][ds(L, 1), z, :, :].rearrange("a r c -> (a r) c")).then_inc(ld, 16)
            sp.dma_start(m.g_on[:, :], d["gla_out_norm"][ds(L, 1), :].rearrange("a c -> (a c)").
                         partition_broadcast(P)).then_inc(ld, 16)
            for z in range(2):
                sp.dma_start(m.g_ab[:, z, :], d["gla_alpha_bias"][ds(L, 1), z, :].rearrange("a (h p) -> p (a h)", p=P),
                             allow_slow_non_contiguous=True).then_inc(ld, 16)
            for u, (hp, dr) in enumerate(units):
                if u:
                    sp.wait_ge(m.sem("o_done"), 5 * u)
                sp.dma_start(m.g_s[:, (0, 7)[dr], :],
                             d["state_gla"][0, ds(L, 1), dr, 2 * hp:2 * hp + 2, :, :].
                             rearrange("a h k e -> (a h k) e")).then_inc(m.sem("state_in"), 16)
                sp.wait_ge(m.sem("state_done"), u + 1)
                sp.dma_start(d["new_state_gla"][0, ds(L, 1), dr, 2 * hp:2 * hp + 2, :, :].
                             rearrange("a h k e -> (a h k) e"), m.g_sf[:, :]).then_inc(m.sem("state_out"), 16)
            sp.wait_ge(m.sem("state_out"), 16 * len(units))

        @block.scalar
        def _(act):
            order = Signal(m.sem("act_order"))
            done = order.step(nc.scalar.activation(m.lg[:, :, :], m.lg[:, :, :], ACT.Silu))
            act.wait_ge(m.sem("gla_params"), 6 * 16)
            for u, (hp, dr) in enumerate(units):
                last = slice(CH - 1, CH) if dr == 0 else slice(0, 1)
                act.wait_ge(m.sem("z_min"), u + 1)
                done = order.step(nc.scalar.activation(halves(m.g_abs[:, :]), m.ps[:, 0:2, 0:HALF], ACT.Abs,
                                                       bias=m.g_ab[:, dr, hp:hp + 1]))
                act.wait_ge(*done)
                done = order.step(nc.scalar.activation(m.g_abs[:, :], m.g_abs[:, :], ACT.Exp, scale=-1.0))
                act.wait_ge(*done)
                nc.scalar.activation(m.g_sp[:, :], m.g_abs[:, :], ACT.Ln, bias=1.0).then_inc(m.sem("softplus"), 1)
                act.wait_ge(m.sem("cum_done"), u + 1)
                if u:
                    act.wait_ge(m.sem("q_decayed"), u)
                    act.wait_ge(m.sem("k_end"), u)
                    act.wait_ge(m.sem("state_done"), u)
                nc.scalar.activation(m.g_eq[:, :], m.g_cum[:, :], ACT.Exp, scale=1.0 / TAU).then_inc(m.sem("exp_q"), 1)
                nc.scalar.activation(m.g_ek[:, :], m.g_cum[:, :], ACT.Exp, scale=-1.0 / TAU).then_inc(m.sem("exp_k"), 1)
                nc.scalar.activation(m.g_dec[:, :], m.g_cum[:, :].rearrange("p (c t) -> p c t", t=CH)[:, :, last].
                                     rearrange("p c t -> p (c t)"), ACT.Exp, scale=1.0 / TAU).then_inc(m.sem("decay"), 1)
                act.wait_ge(m.sem("to_end"), u + 1)
                nc.scalar.activation(m.g_min[:, :], m.g_la[:, :], ACT.Exp, scale=1.0 / TAU).then_inc(m.sem("exp_end"), 1)
                act.wait_ge(m.sem("ke_turned"), u + 1)
                if u:
                    act.wait_ge(m.sem("ds_done"), u)
                nc.scalar.activation(m.g_ker[:, 0:4, :].rearrange("p t c -> p (t c)"), m.ps[:, 0, :], ACT.Copy)
                nc.scalar.activation(m.g_ker[:, 4, :], m.ps[:, 1, 0:P], ACT.Copy).then_inc(m.sem("ke_rows"), 1)
            act.wait_ge(m.sem("o_summed"), 20)
            nc.scalar.activation(m.g_sq[:, :, :], m.glr[:, :, :], ACT.Square).then_inc(m.sem("o_squares"), 1)
            act.wait_ge(m.sem("o_ms"), 1)
            nc.scalar.activation(m.g_st[:, 20:40], m.g_st[:, 0:20], ACT.Sqrt, scale=1.0 / P,
                                 bias=m.cst[:, K_LAM + 4:K_LAM + 5]).then_inc(m.sem("o_std"), 1)

        @block.tensor
        def _(pe):
            pe.wait_ge(m.sem("gla_params"), 6 * 16)
            for u, (hp, dr) in enumerate(units):
                if u:
                    pe.wait_ge(m.sem("ke_rows"), u)
                for n in range(2):
                    last = nc.tensor.matmul(m.ps[:, n, 0:HALF], m.g_au[0:32, dr, hp * P:(hp + 1) * P],
                                            m.lT[0:32, 4, n * HALF:(n + 1) * HALF], start=True, stop=True)
                last.then_inc(m.sem("z_done"), 1)
                pe.wait_ge(m.sem("k_end"), u + 1)
                for tt in range(TT):
                    last = nc.tensor.transpose(m.ps[:, tt // 4, (tt % 4) * P:(tt % 4 + 1) * P],
                                               tok(m.g_ke[:, :], tt), m.cst[:, K_ID:K_ID + P])
                last.then_inc(m.sem("ke_turned"), 1)
                pe.wait_ge(m.sem("ke_rows"), u + 1)
                for idx in range(NCH):
                    tt, half = idx // 2, idx % 2
                    for hh in range(2):
                        last = nc.tensor.matmul(ds_at(idx, slice(64 * hh, 64 * hh + 64)),
                                                m.g_ker[64 * half:64 * half + 64, tt, 64 * hh:64 * hh + 64],
                                                m.lv[64 * half:64 * half + 64, tt, (2 * hp + hh) * P:(2 * hp + hh + 1) * P],
                                                start=True, stop=True)
                last.then_inc(m.sem("ds_done"), 1)

                def scores(tt):
                    a = 5 * u + tt
                    if a >= 1:
                        pe.wait_ge(m.sem("a_masked"), a)
                    for hh in range(2):
                        h = slice(64 * hh, 64 * hh + 64)
                        last = nc.tensor.matmul(m.ps[:, 6 + hh, 0:P], tok(m.g_ki[h, :], tt),
                                                tok(m.g_qd[h, :], tt), start=True, stop=True)
                    last.then_inc(m.sem("a_done"), 1)

                def outputs(tt):
                    a = 5 * u + tt
                    pe.wait_ge(m.sem("a_masked"), a + 1)
                    if a >= 1:
                        pe.wait_ge(m.sem("o_summed"), a)
                    for hh in range(2):
                        nc.tensor.matmul(m.ps[:, 4 + hh, 0:P], m.g_am[:, dr, a % 2, hh, :],
                                         m.lv[:, tt, (2 * hp + hh) * P:(2 * hp + hh + 1) * P],
                                         start=True, stop=False, skip_group_check=True)
                        for half in range(2):
                            q = chunk_pos(2 * tt + half) * CH
                            last = nc.tensor.matmul(m.ps[64 * half:64 * half + 64, 4 + hh, 0:P],
                                                    m.g_qd[64 * hh:64 * hh + 64, q:q + CH],
                                                    m.g_s[64 * hh:64 * hh + 64, 2 * tt + half, :],
                                                    start=False, stop=True, skip_group_check=True)
                    last.then_inc(m.sem("o_done"), 1)

                pe.wait_ge(m.sem("k_inv"), u + 1)
                scores(0)
                pe.wait_ge(m.sem("state_done"), u + 1)
                for tt in range(TT):
                    if tt + 1 < TT:
                        scores(tt + 1)
                    outputs(tt)

        @block.vector
        def _(dve):
            order = Signal(m.sem("dve_order"))
            dve.wait_ge(m.sem("gla_params"), 6 * 16)
            dve.wait_ge(m.sem("am_zero"), 1)
            for u, (hp, dr) in enumerate(units):
                flip = slice(None, None, -1) if dr else slice(None)
                last = slice(CH - 1, CH) if dr == 0 else slice(0, 1)
                dve.wait_ge(m.sem("z_done"), u + 1)
                nc.vector.tensor_scalar(halves(m.g_min[:, :]), m.ps[:, 0:2, 0:HALF], m.g_ab[:, dr, hp:hp + 1], 0.0,
                                        ALU.add, ALU.min).then_inc(m.sem("z_min"), 1)
                dve.wait_ge(m.sem("z_min"), u + 1)
                dve.wait_ge(m.sem("softplus"), u + 1)
                done = (m.sem("la_done"), u + 1)
                nc.vector.tensor_tensor(m.g_la[:, :], m.g_min[:, :], m.g_sp[:, :], ALU.subtract).then_inc(m.sem("la_done"), 1)
                dve.wait_ge(*done)
                nc.vector.tensor_tensor_scan(m.g_cum[:, flip], m.g_cst[:, G_CM:G_CM + T], m.g_la[:, flip], 0.0,
                                             ALU.mult, ALU.add).then_inc(m.sem("cum_done"), 1)
                dve.wait_ge(m.sem("cum_done"), u + 1)
                cum = m.g_cum[:, :].rearrange("p (c t) -> p c t", t=CH)
                nc.vector.tensor_tensor(m.g_la[:, :].rearrange("p (c t) -> p c t", t=CH),
                                        cum[:, :, last].broadcast_to([P, NCH, CH]), cum, ALU.subtract
                                        ).then_inc(m.sem("to_end"), 1)
                if u:
                    dve.wait_ge(m.sem("o_done"), 5 * u)
                dve.wait_ge(m.sem("exp_q"), u + 1)
                nc.vector.tensor_tensor(m.g_qd[:, :], m.lT[:, hp, :], m.g_eq[:, :], ALU.mult).then_inc(m.sem("q_decayed"), 1)
                dve.wait_ge(m.sem("exp_k"), u + 1)
                nc.vector.tensor_tensor(m.g_ki[:, :], m.lT[:, 2 + hp, :], m.g_ek[:, :], ALU.mult).then_inc(m.sem("k_inv"), 1)
                dve.wait_ge(m.sem("exp_end"), u + 1)
                nc.vector.tensor_tensor(m.g_ke[:, :], m.lT[:, 2 + hp, :], m.g_min[:, :], ALU.mult).then_inc(m.sem("k_end"), 1)
                dve.wait_ge(m.sem("decay"), u + 1)
                dve.wait_ge(m.sem("ds_done"), u + 1)
                dve.wait_ge(m.sem("state_in"), 16 * (u + 1))
                if u:
                    dve.wait_ge(m.sem("state_out"), 16 * u)
                done = order.step(nc.vector.memset(m.g_s[:, (8, 9)[dr], :], 0.0))
                run = list(range(0, 7)) + [8] if dr == 0 else list(range(7, 0, -1)) + [9]
                to = 1 if dr == 0 else -1
                for idx in run:
                    dve.wait_ge(*done)
                    done = order.step(nc.vector.scalar_tensor_tensor(
                        out=m.g_s[:, idx + to, :], in0=m.g_s[:, idx, :],
                        scalar=m.g_dec[:, chunk_pos(idx):chunk_pos(idx) + 1],
                        in1=ds_at(idx), op0=ALU.mult, op1=ALU.add))
                dve.wait_ge(*done)
                idx = 9 if dr == 0 else 8
                nc.vector.scalar_tensor_tensor(
                    out=m.g_sf[:, :], in0=m.g_s[:, idx, :], scalar=m.g_dec[:, chunk_pos(idx):chunk_pos(idx) + 1],
                    in1=ds_at(idx), op0=ALU.mult, op1=ALU.add
                ).then_inc(m.sem("state_done"), 1)

                def mask(tt):
                    a = 5 * u + tt
                    dve.wait_ge(m.sem("a_done"), a + 1)
                    if a >= 2:
                        dve.wait_ge(m.sem("o_done"), a - 1)
                    msk = m.g_cst[:, (G_MF, G_MB)[dr]:(G_MF, G_MB)[dr] + P].bitcast(I32)
                    nc.vector.copy_predicated(m.g_am[:, dr, a % 2, :, :], msk.unsqueeze(1).broadcast_to([P, 2, P]),
                                              m.ps[:, 6:8, 0:P]
                                              ).then_inc(m.sem("a_masked"), 1)

                mask(0)
                for tt in range(TT):
                    a = 5 * u + tt
                    if tt + 1 < TT:
                        mask(tt + 1)
                    dve.wait_ge(m.sem("o_done"), a + 1)
                    dst = m.glr[:, tt, hp * 256:(hp + 1) * 256].rearrange("p (h c) -> p h c", h=2)
                    src = m.ps[:, 4:6, 0:P]
                    if dr == 0:
                        nc.vector.tensor_copy(dst, src).then_inc(m.sem("o_summed"), 1)
                    else:
                        dve.wait_ge(m.sem("o_summed"), a - 4)
                        nc.vector.tensor_tensor(dst, dst, src, ALU.add).then_inc(m.sem("o_summed"), 1)
            dve.wait_ge(m.sem("o_squares"), 1)
            nc.vector.tensor_reduce(m.g_st[:, 0:20], m.g_sq[:, :, :].rearrange("p t (h c) -> p (t h) c", c=P), AX.X,
                                    ALU.add).then_inc(m.sem("o_ms"), 1)
            dve.wait_ge(m.sem("o_std"), 1)
            done = order.step(nc.vector.reciprocal(m.g_st[:, 40:60], m.g_st[:, 20:40]))
            dve.wait_ge(*done)
            o = m.glr[:, :, :].rearrange("p t (h c) -> p (t h) c", c=P)
            done = order.step(nc.vector.tensor_tensor(o, o, m.g_st[:, 40:60].unsqueeze(2).broadcast_to([P, 20, P]), ALU.mult))
            dve.wait_ge(*done)
            done = order.step(nc.vector.tensor_tensor(o, o, m.g_on[:, :].unsqueeze(1).broadcast_to([P, 20, P]), ALU.mult))
            dve.wait_ge(*done)
            dve.wait_ge(m.sem("act_order"), 1)
            order.step(nc.vector.tensor_tensor(m.glr[:, :, :], m.glr[:, :, :], m.lg[:, :, :], ALU.mult))


def project_attention(nc, m, d, L):
    slabs = [(C_GQ, 0), (C_GQ + 256, 0), (C_DQ, 1), (C_DQ + 256, 1), (C_GK, 2), (C_DK, 3), (C_DK + 256, 3),
             (C_DV, None), (C_DV + 256, None)]
    n = len(slabs)

    def place(s):
        if s < 4:
            return m.rq[:, 2 * s:2 * s + 2, :, :]
        b = {4: 8, 5: 0, 6: 2, 7: 4, 8: 6}[s]
        return m.kv[:, b:b + 2, 0:TT, :]

    normed = [s for s in range(n) if slabs[s][1] is not None]
    with m.block() as block:
        @block.sync
        def _(sp):
            for s, (c, _) in enumerate(slabs):
                if s >= 2:
                    sp.wait_ge(m.sem("low_ready"), s - 1)
                sp.dma_start(m.raw[:, s % 2, :].rearrange("p (k c) -> p k c", k=KT),
                             k_tiles(d["w_in"], L, c, W256)).then_inc(m.sem(f"slab_loaded{s % 2}"), 16)
            out = m.sem("kv_stored")
            sp.wait_ge(m.sem("normed"), 7)
            sp.dma_start(d["new_gqa_k"][0, ds(L, 1), :, :, :].rearrange("a t h c -> (a t) (h c)"),
                         m.kv[:, 8, CTX, :]).then_inc(out, 16)
            sp.dma_start(d["new_diff_k"][0, ds(L, 1), :, :, :, :].rearrange("a t h m c -> (a t) h (m c)"),
                         m.kv[:, 0:4, CTX, :]).then_inc(out, 16)
            sp.wait_ge(m.sem("tile_copied"), 5 * n)
            sp.dma_start(d["new_gqa_v"][0, ds(L, 1), :, :, :].rearrange("a t h c -> (a t) (h c)"),
                         m.kv[:, 9, CTX, :]).then_inc(out, 16)
            sp.dma_start(d["new_diff_v"][0, ds(L, 1), :, :, :].rearrange("a t h c -> (a t) h c"),
                         m.kv[:, 4:8, CTX, :]).then_inc(out, 16)
            sp.wait_ge(out, 64)
            sp.wait_ge(m.sem("caches"), 6 * 16)

        @block.gpsimd
        def _(pool):
            pool.wait_ge(m.sem("rope_tables"), 16)
            for kind in range(4):
                w = m.gains[:, kind, :].unsqueeze(1).broadcast_to([P, TT, HD])
                nc.gpsimd.tensor_tensor(m.r_c[:, kind, :, :], m.r_tab[:, 0, :, :], w, ALU.mult).then_inc(m.sem("tables"), 1)
                nc.gpsimd.tensor_tensor(m.r_s[:, kind, :, :], m.r_tab[:, 1, :, :], w, ALU.mult).then_inc(m.sem("tables"), 1)

        @block.scalar
        def _(act):
            act.dma_start(m.r_tab[:, :, :, :], d["const_rope"]).then_inc(m.sem("rope_tables"), 16)
            caches = m.sem("caches")
            act.dma_start(m.kv[:, 0:4, TT, :], d["cache_diff_k"][0, ds(L, 1), :, :, :, :].
                           rearrange("a t h m c -> (a t) h (m c)")).then_inc(caches, 16)
            act.dma_start(m.kv[:, 4:8, TT, :], d["cache_diff_v"][0, ds(L, 1), :, :, :].
                           rearrange("a t h c -> (a t) h c")).then_inc(caches, 16)
            gk = d["cache_gqa_k"][0, ds(L, 1), :, :, :].rearrange("a t h c -> (a t) h c")
            act.dma_start(m.kv[:, 8, TT, :].rearrange("p (h c) -> p h c", h=2), gk).then_inc(caches, 16)
            act.dma_start(m.kv[:, 9, TT, :].rearrange("p (h c) -> p h c", h=2),
                           d["cache_gqa_v"][0, ds(L, 1), :, :, :].rearrange("a t h c -> (a t) h c")).then_inc(caches, 16)
            for h in range(2):
                act.dma_start(m.kv[:, 10, TT, (1 - h) * HD:(2 - h) * HD], gk[:, h, :]).then_inc(caches, 16)
            def high(s):
                high_part(nc, m, act, s % 2, 16 * (s // 2 + 1), (m.sem("tile_done"), 5 * (s - 1)) if s > 1 else None)

            high(0)
            q = 0
            for s in range(n):
                if s + 1 < n:
                    high(s + 1)
                for tt in range(TT):
                    act.wait_ge(m.sem("tile_done"), 5 * s + tt + 1)
                    nc.scalar.activation(place(s)[:, :, tt, :],
                                         m.ps[:, ROW_BANK[(5 * s + tt) % RING], 0:256].rearrange("p (b c) -> p b c", b=2),
                                         ACT.Copy).then_inc(m.sem("tile_copied"), 1)
                if s in normed:
                    nb = 1 if s == 4 else 2
                    act.wait_ge(m.sem("tile_copied"), 5 * s + 5)
                    if q:
                        act.wait_ge(m.sem("mean_squares"), q)
                    nc.scalar.activation(m.r_sq[:, 0:nb * T].rearrange("p (b t) -> p b t", b=nb),
                                         place(s)[:, 0:nb, :, :].rearrange("p b t c -> p b (t c)"), ACT.Square
                                         ).then_inc(m.sem("squares"), 1)
                    act.wait_ge(m.sem("mean_squares"), q + 1)
                    if q:
                        act.wait_ge(m.sem("normed"), q)
                    nc.scalar.activation(m.r_st[:, 1, 0:10 * nb], m.r_st[:, 0, 0:10 * nb], ACT.Sqrt, scale=1.0 / HD,
                                         bias=m.cst[:, K_LAM + 4:K_LAM + 5]).then_inc(m.sem("head_std"), 1)
                    q += 1

        @block.vector
        def _(dve):
            order = Signal(m.sem("dve_order"))
            low_part(nc, m, dve, 0, 0)
            q = 0
            for s, (_, kind) in enumerate(slabs):
                if s + 1 < n:
                    low_part(nc, m, dve, s + 1, (s + 1) % 2)
                if kind is None:
                    continue
                nb = 1 if s == 4 else 2
                x = place(s)
                dve.wait_ge(m.sem("squares"), q + 1)
                nc.vector.tensor_reduce(m.r_st[:, 0, 0:10 * nb],
                                        m.r_sq[:, 0:nb * T].rearrange("p (g c) -> p g c", c=HD), AX.X, ALU.add
                                        ).then_inc(m.sem("mean_squares"), 1)
                dve.wait_ge(m.sem("head_std"), q + 1)
                done = order.step(nc.vector.reciprocal(m.r_st[:, 2, 0:10 * nb], m.r_st[:, 1, 0:10 * nb]))
                if q == 0:
                    dve.wait_ge(m.sem("tables"), 8)
                marks = []
                dve.wait_ge(*done)
                for b in range(nb):
                    xb = x[:, b, :, :].rearrange("p t (h c) -> p (t h) c", c=HD)
                    r = m.r_st[:, 2, 10 * b:10 * b + 10].unsqueeze(2).broadcast_to([P, 10, HD])
                    done = order.step(nc.vector.tensor_tensor(xb, xb, r, ALU.mult))
                dve.wait_ge(*done)
                for b in range(nb):
                    xb = x[:, b, :, :].rearrange("p t (h c) -> p t h c", c=HD)
                    tb = m.r_t[:, b * T:(b + 1) * T].rearrange("p (t h c) -> p t h c", h=2, c=HD)
                    sin = m.r_s[:, kind, :, :].unsqueeze(2).broadcast_to([P, TT, 2, HD])
                    done = order.step(nc.vector.tensor_tensor(tb, xb, sin, ALU.mult))
                dve.wait_ge(*done)
                for b in range(nb):
                    xb = x[:, b, :, :].rearrange("p t (h c) -> p t h c", c=HD)
                    cos = m.r_c[:, kind, :, :].unsqueeze(2).broadcast_to([P, TT, 2, HD])
                    done = order.step(nc.vector.tensor_tensor(xb, xb, cos, ALU.mult))
                dve.wait_ge(*done)
                for b in range(nb):
                    xb = x[:, b, :, :].rearrange("p t (g u f) -> p (t g) u f", u=2, f=16)
                    tb = m.r_t[:, b * T:(b + 1) * T].rearrange("p (g u f) -> p g u f", u=2, f=16)[:, :, ::-1, :]
                    ins = nc.vector.tensor_tensor(xb, xb, tb, ALU.add)
                    if s == 4 or b == 0:
                        done = order.step(ins)
                if s == 4:
                    dve.wait_ge(*done)
                    for h in range(2):
                        ins = nc.vector.tensor_copy(m.kv[:, 10, 0:TT, (1 - h) * HD:(2 - h) * HD],
                                                    m.kv[:, 8, 0:TT, h * HD:(h + 1) * HD])
                ins.then_inc(m.sem("normed"), 1)
                dve.wait_ge(m.sem("normed"), q + 1)
                q += 1

        @block.tensor
        def _(pe):
            for s in range(n):
                pe.wait_ge(m.sem("low_ready"), s + 1)
                for tt in range(TT):
                    g = 5 * s + tt
                    back = ROW_BACK[g % RING]
                    if g >= back:
                        pe.wait_ge(m.sem("tile_copied"), g - back + 1)
                    row_tile(nc, m, s % 2, tt, ROW_BANK[g % RING]).then_inc(m.sem("tile_done"), 1)


def attention(nc, m, d, L):
    turn = [(m.rq, b, TT) for b in range(8)] + [(m.kv, b, TT + 1) for b in (0, 1, 2, 3, 8, 10)]
    items = []
    for qt in range(TT):
        for h in range(8):
            kvh = h // 4
            items.append((qt, h // 2, h % 2, 8 if kvh == h % 2 else 10, 9, kvh * HD, (h % 2) * HD, None))
        for h in range(4):
            for mp in range(2):
                items.append((qt, 4 + h, mp, h, 4 + h, 0, 0, mp))
    units = []
    for i, it in enumerate(items):
        if it[7] != 0:
            units.append(i)

    def keys(qt):
        return [0, 1, 2, 3, TT] if qt < CTX else [CTX]

    with m.block() as block:
        @block.tensor
        def _(pe):
            for t, (buf, b, tiles) in enumerate(turn):
                if t >= 4:
                    pe.wait_ge(m.sem("turned_copied"), t - 3)
                for tt in range(tiles):
                    last = nc.tensor.transpose(m.ps[:, 2 * (t % 4) + tt // 4, (tt % 4) * P:(tt % 4 + 1) * P],
                                               buf[:, b, tt, :], m.cst[:, K_ID:K_ID + P])
                last.then_inc(m.sem("turned"), 1)
            pe.wait_ge(m.sem("turned_copied"), len(turn))

            def scores(i):
                qt, qb, half, kb, *_ = items[i]
                if i >= 2:
                    pe.wait_ge(m.sem("exp_done"), i - 1)
                h = slice(64 * half, 64 * half + 64)
                q = m.rq[h, qb, qt, :]
                if qt < CTX:
                    nc.tensor.matmul(m.ps[:, 2 * (i % 2), :], q, m.kv[h, kb, 0:4, :].rearrange("p t c -> p (t c)"),
                                     start=True, stop=True)
                    last = nc.tensor.matmul(m.ps[:, 2 * (i % 2) + 1, 0:P], q, m.kv[h, kb, TT, :], start=True, stop=True)
                else:
                    last = nc.tensor.matmul(m.ps[:, 2 * (i % 2), 0:P], q, m.kv[h, kb, CTX, :], start=True, stop=True)
                last.then_inc(m.sem("scores"), 1)

            def weigh(u):
                i = units[u]
                qt, _, _, _, vb, vc, _, mp = items[i]
                ks = keys(qt)
                slot = i % 4 if mp is None else (i - 1) % 4
                if mp is None:
                    pe.wait_ge(m.sem("exp_done"), i + 1)
                else:
                    pe.wait_ge(m.sem("mixed"), sum(items[j][7] == 1 for j in units[:u + 1]))
                if u >= 1:
                    pe.wait_ge(m.sem("p_copied"), u)
                for n in range(len(ks)):
                    last = nc.tensor.transpose(m.ps[:, 4 + n // 4, (n % 4) * P:(n % 4 + 1) * P],
                                               m.e[:, slot, n * P:(n + 1) * P], m.cst[:, K_ID:K_ID + P])
                last.then_inc(m.sem("p_turned"), 1)

            def values(u):
                i = units[u]
                qt, _, _, _, vb, vc, _, mp = items[i]
                ks = keys(qt)
                pe.wait_ge(m.sem("p_copied"), u + 1)
                if u >= 2:
                    pe.wait_ge(m.sem("o_copied"), u - 1)
                w = HD if mp is None else P
                for n, kt in enumerate(ks):
                    last = nc.tensor.matmul(m.ps[:, 6 + u % 2, 0:w], m.eT[:, u % 2, n, :], m.kv[:, vb, kt, vc:vc + w],
                                            start=(n == 0), stop=(n == len(ks) - 1))
                last.then_inc(m.sem("o_done"), 1)

            scores(0)
            u = 0
            for i in range(len(items)):
                if i + 1 < len(items):
                    scores(i + 1)
                if items[i][7] != 0:
                    weigh(u)
                    if u >= 1:
                        values(u - 1)
                    u += 1
            values(u - 1)

        @block.scalar
        def _(act):
            for t, (buf, b, tiles) in enumerate(turn):
                act.wait_ge(m.sem("turned"), t + 1)
                p0 = 2 * (t % 4)
                nc.scalar.activation(buf[:, b, 0:tiles, :].rearrange("p t c -> p (t c)"),
                                     m.ps[:, p0:p0 + 2, :].rearrange("p b c -> p (b c)")[:, 0:tiles * P], ACT.Copy,
                                     scale=(HD ** -0.5 if t < 8 else 1.0)).then_inc(m.sem("turned_copied"), 1)

            def exp(i):
                n = len(keys(items[i][0])) * P
                act.wait_ge(m.sem("maximum"), i + 1)
                old = [u for u, j in enumerate(units) if j <= i - 4 or (items[j][7] == 1 and j - 1 <= i - 4)]
                if old:
                    act.wait_ge(m.sem("p_turned"), old[-1] + 1)
                if i >= 32:
                    act.wait_ge(m.sem("maximum"), i + 1)
                nc.scalar.activation(m.e[:, i % 4, 0:n], m.ps[:, 2 * (i % 2):2 * (i % 2) + 2, :].
                                     rearrange("p b c -> p (b c)")[:, 0:n], ACT.Exp, bias=m.a_st[:, i % 32, 0:1],
                                     accum_out=m.a_st[:, i % 32, 1:2]).then_inc(m.sem("exp_done"), 1)

            def copy(u):
                i = units[u]
                n = len(keys(items[i][0]))
                act.wait_ge(m.sem("p_turned"), u + 1)
                if u >= 2:
                    act.wait_ge(m.sem("o_done"), u - 1)
                nc.scalar.activation(m.eT[:, u % 2, 0:n, :].rearrange("p t c -> p (t c)"),
                                     m.ps[:, 4:6, :].rearrange("p b c -> p (b c)")[:, 0:n * P], ACT.Copy
                                     ).then_inc(m.sem("p_copied"), 1)

            u = 0
            exp(0)
            for i in range(len(items)):
                if i + 1 < len(items):
                    exp(i + 1)
                if items[i][7] != 0:
                    copy(u)
                    u += 1
            act.wait_ge(m.sem("o_copied"), len(units))
            nc.scalar.activation(m.o_sq[:, :, :], m.rq[:, 4:8, :, :].rearrange("p b t c -> p b (t c)"), ACT.Square
                                 ).then_inc(m.sem("o_squares"), 1)
            act.wait_ge(m.sem("o_ms"), 1)
            nc.scalar.activation(m.sml[:, 20:40], m.sml[:, 0:20], ACT.Sqrt, scale=1.0 / P,
                                 bias=m.cst[:, K_LAM + 4:K_LAM + 5]).then_inc(m.sem("o_std"), 1)

        @block.vector
        def _(dve):
            order = Signal(m.sem("dve_order"))

            def maximum(i):
                n = len(keys(items[i][0])) * P
                dve.wait_ge(m.sem("scores"), i + 1)
                nc.vector.tensor_reduce(m.a_st[:, i % 32, 0:1], m.ps[:, 2 * (i % 2):2 * (i % 2) + 2, :].
                                        rearrange("p b c -> p (b c)")[:, 0:n], AX.X, ALU.max, negate=True
                                        ).then_inc(m.sem("maximum"), 1)

            def inverse(u):
                i = units[u]
                mp = items[i][7]
                n = len(keys(items[i][0])) * P
                a = m.a_st[:, i % 32, :]
                dve.wait_ge(m.sem("exp_done"), i + 1)
                done = order.step(nc.vector.reciprocal(a[:, 2:3], a[:, 1:2]))
                if mp == 1:
                    b = m.a_st[:, (i - 1) % 32, :]
                    dve.wait_ge(*done)
                    done = order.step(nc.vector.scalar_tensor_tensor(out=a[:, 3:4], in0=b[:, 1:2], scalar=m.nlam[:, 0:1],
                                                                     in1=a[:, 2:3], op0=ALU.mult, op1=ALU.mult))
                    dve.wait_ge(*done)
                    nc.vector.scalar_tensor_tensor(out=m.e[:, (i - 1) % 4, 0:n], in0=m.e[:, i % 4, 0:n],
                                                   scalar=a[:, 3:4], in1=m.e[:, (i - 1) % 4, 0:n],
                                                   op0=ALU.mult, op1=ALU.add).then_inc(m.sem("mixed"), 1)
                    done = order.step(nc.vector.reciprocal(a[:, 2:3], b[:, 1:2]))
                return done

            def out(u, done):
                i = units[u]
                qt, qb, half, _, _, _, oc, mp = items[i]
                dve.wait_ge(*done)
                dve.wait_ge(m.sem("o_done"), u + 1)
                if mp is None and half == 0:
                    dve.wait_ge(m.sem("scores"), i + 2)
                w = HD if mp is None else P
                nc.vector.tensor_scalar(m.rq[:, qb, qt, oc:oc + w], m.ps[:, 6 + u % 2, 0:w], m.a_st[:, i % 32, 2:3],
                                        None, ALU.mult).then_inc(m.sem("o_copied"), 1)

            maximum(0)
            u, marks = 0, []
            for i in range(len(items)):
                if i + 1 < len(items):
                    maximum(i + 1)
                if items[i][7] != 0:
                    marks.append(inverse(u))
                    if u >= 1:
                        out(u - 1, marks[u - 1])
                    u += 1
            out(u - 1, marks[u - 1])
            dve.wait_ge(m.sem("o_squares"), 1)
            nc.vector.tensor_reduce(m.sml[:, 0:20], m.o_sq[:, :, :].rearrange("p b (t c) -> p (b t) c", c=P), AX.X, ALU.add
                                    ).then_inc(m.sem("o_ms"), 1)
            dve.wait_ge(m.sem("o_std"), 1)
            done = order.step(nc.vector.reciprocal(m.sml[:, 40:60], m.sml[:, 20:40]))
            dve.wait_ge(*done)
            o = m.rq[:, 4:8, :, :].rearrange("p b t c -> p (b t) c")
            done = order.step(nc.vector.tensor_tensor(o, o, m.sml[:, 40:60].unsqueeze(2).broadcast_to([P, 20, P]), ALU.mult))
            dve.wait_ge(*done)
            order.step(nc.vector.tensor_tensor(o, o, m.subn[:, :].unsqueeze(1).broadcast_to([P, 20, P]), ALU.mult))


def merge(nc, m, d, L):
    rows = [m.rq[:, b, :, :] for b in range(4)] + \
           [m.glr[:, :, b * P:(b + 1) * P] for b in range(4)] + [m.rq[:, 4 + b, :, :] for b in range(4)]
    pairs = KT // 2

    def load(sp, L, dp, i, kind):
        if kind == 0:
            sp.dma_start(m.raw[:, 0, :].rearrange("p (k c) -> p k c", k=KT),
                         k_tiles(d["w_in"], L, C_MG + i * D + dp * W256, W256)).then_inc(m.sem("slab_loaded0"), 16)
        else:
            sp.dma_start(m.raw[:, 1, 0:1024].rearrange("p (k c) -> p k c", k=4),
                         d["w_branch"][ds(L, 1), i, :, ds(dp * W256, W256)].rearrange("a (k p) c -> p (a k) c", p=P)
                         ).then_inc(m.sem("slab_loaded1"), 16)

    with m.block() as block:
        @block.sync
        def _(sp):
            with sp.Fori(0, pairs) as dp:
                for i in range(3):
                    for kind in range(2):
                        sp.wait_ge(m.sem("low_ready"), 6 * dp + 2 * i + kind + 1)
                        load(sp, L, dp, i, kind)

        @block.scalar
        def _(act):
            act.sem_inc(m.sem("gates_ready"), 2)
            for t in range(12):
                act.wait_ge(m.sem("turned"), t + 1)
                nc.scalar.activation(halves(m.oH[:, t, :]), m.ps[:, 2 * (t % 4):2 * (t % 4) + 2, 0:HALF], ACT.Copy
                                     ).then_inc(m.sem("turned_high"), 1)

            def high(dp, s):
                slot = s % 2
                act.wait_ge(m.sem(f"slab_loaded{slot}"), dp * 48 + 16 * (s // 2 + 1))
                act.wait_ge(m.sem("tile_done"), dp * 12 + 2 * s + 2)
                n = SLAB if slot == 0 else 1024
                nc.scalar.activation(m.wH[:, slot, 0:n], m.raw[:, slot, 0:n], ACT.Copy).then_inc(m.sem("high_ready"), 1)

            def round_(dp, last):
                for i in range(3):
                    high(dp, 2 * i + 1)
                    for c in range(2):
                        act.wait_ge(m.sem("tile_done"), dp * 12 + 4 * i + c + 1 + 4)
                        act.wait_ge(m.sem("gated"), dp * 6 + 2 * i + c + 1)
                        nc.scalar.activation(halves(m.gate[:, c, :]), m.ps[:, 2 * c:2 * c + 2, 0:HALF], ACT.Sigmoid
                                             ).then_inc(m.sem("gates_ready"), 1)
                    if not (last and i == 2):
                        high(dp, 2 * i + 2)

            high(0, 0)
            with act.Fori(0, pairs - 1) as dp:
                round_(dp, False)
            round_(pairs - 1, True)
            for k in range(KT):
                act.wait_ge(m.sem("mixed"), 6 * (k // 2 + 1))
                if k == 0:
                    act.wait_ge(m.sem("tile_done"), 48 + 4)
                nc.scalar.activation(m.hH[:, k, :], m.mix[:, k, :], ACT.Copy).then_inc(m.sem("mix_high"), 1)

        @block.vector
        def _(dve):
            order = Signal(m.sem("dve_order"))
            dve.sem_inc(m.sem("low_ready"), 2)
            dve.sem_inc(m.sem("gated"), 2)
            for t in range(12):
                dve.wait_ge(m.sem("turned_high"), t + 1)
                nc.vector.tensor_tensor(halves(m.oL[:, t, :]), m.ps[:, 2 * (t % 4):2 * (t % 4) + 2, 0:HALF],
                                        halves(m.oH[:, t, :]).bitcast(F32), ALU.subtract).then_inc(m.sem("turned_low"), 1)
            dve.wait_ge(m.sem("turned_low"), 12)
            done = order.step(nc.vector.memset(m.mix[:, :, :], 0.0))
            dve.wait_ge(*done)

            def low(dp, s):
                slot = s % 2
                n = SLAB if slot == 0 else 1024
                dve.wait_ge(m.sem("high_ready"), dp * 6 + s + 1)
                nc.vector.tensor_tensor(m.wL[:, slot, 0:n], m.raw[:, slot, 0:n], m.wH[:, slot, 0:n].bitcast(F32),
                                        ALU.subtract).then_inc(m.sem("low_ready"), 1)

            def round_(dp, last):
                for i in range(3):
                    low(dp, 2 * i + 1)
                    for c in range(2):
                        dve.wait_ge(m.sem("tile_done"), dp * 12 + 4 * i + 2 + c + 1 + 4)
                        dve.wait_ge(m.sem("gates_ready"), dp * 6 + 2 * i + c + 1 + 2)
                        nc.vector.tensor_tensor(halves(m.gy[:, c, :]), halves(m.gate[:, c, :]),
                                                m.ps[:, 4 + 2 * c:6 + 2 * c, 0:HALF], ALU.mult).then_inc(m.sem("gated"), 1)
                        dve.wait_ge(m.sem("gated"), dp * 6 + 2 * i + c + 1 + 2)
                        mix = m.mix[:, ds(dp * 2 + c, 1), :].rearrange("p a t -> p (a t)")
                        nc.vector.tensor_tensor(mix, mix, m.gy[:, c, :], ALU.add).then_inc(m.sem("mixed"), 1)
                        dve.wait_ge(m.sem("mixed"), dp * 6 + 2 * i + c + 1)
                    if not (last and i == 2):
                        low(dp, 2 * i + 2)

            low(0, 0)
            with dve.Fori(0, pairs - 1) as dp:
                round_(dp, False)
            round_(pairs - 1, True)
            for k in range(KT):
                dve.wait_ge(m.sem("mix_high"), k + 1)
                order.step(nc.vector.tensor_tensor(m.hL[:, k, :], m.mix[:, k, :], m.hH[:, k, :].bitcast(F32),
                                                   ALU.subtract))

        @block.tensor
        def _(pe):
            pe.sem_inc(m.sem("tile_done"), 4)
            for t in range(12):
                if t >= 4:
                    pe.wait_ge(m.sem("turned_low"), t - 3)
                b = 2 * (t % 4)
                for tt in range(CTX):
                    c = (tt % 2) * P + CH * (tt // 2)
                    nc.tensor.transpose(m.ps[:, b + tt // 2, c:c + P], rows[t][:, tt, :], m.cst[:, K_ID:K_ID + P])
                for h in range(2):
                    r = slice(CH * h, CH * h + CH)
                    c = 256 * (1 - h)
                    last = nc.tensor.transpose(m.ps[:, b + h, c:c + CH], rows[t][r, CTX, :],
                                               m.cst[r, K_ID + CH * h:K_ID + CH * h + CH])
                last.then_inc(m.sem("turned"), 1)
            pe.wait_ge(m.sem("turned_low"), 12)
            with pe.Fori(0, pairs) as dp:
                for i in range(3):
                    pe.wait_ge(m.sem("low_ready"), dp * 6 + 2 * i + 3)
                    for c in range(2):
                        pe.wait_ge(m.sem("gates_ready"), dp * 6 + 2 * i + c + 1)
                        transposed_tile(nc, m, 0, c * P, W256, KT, m.hH, m.hL, 0, c).then_inc(m.sem("tile_done"), 1)
                    pe.wait_ge(m.sem("low_ready"), dp * 6 + 2 * i + 4)
                    for c in range(2):
                        pe.wait_ge(m.sem("gated"), dp * 6 + 2 * i + c + 1)
                        transposed_tile(nc, m, 1, c * P, W256, 4, m.oH, m.oL, 4 * i, 2 + c).then_inc(m.sem("tile_done"), 1)


def add_gated(nc, m, k, gate_col, pair, signal):
    x = m.xT[:, ds(k, 1), :].rearrange("p a t -> p (a t)")
    src = psum_segments(m.ps, pair)
    for c, seg in enumerate(segments(x)):
        g = m.mod[:, ds(k + gate_col, 1), c:c + 1].rearrange("p a b -> p (a b)")
        ins = nc.vector.scalar_tensor_tensor(out=seg, in0=src[c], scalar=g, in1=seg, op0=ALU.mult, op1=ALU.add)
    ins.then_inc(signal, 1)


def project_out(nc, m, d, L, w, gate_col, k0, nk, cols, aH, aL):
    per = cols // P
    slabs = D // cols
    rounds = slabs // 2
    n = nk * cols

    def load(sp, s, slot):
        src = w[ds(L, 1), k0 * P:(k0 + nk) * P, ds(s * cols, cols)].rearrange("a (k p) c -> p (a k) c", p=P)
        sp.dma_start(m.raw[:, slot, 0:n].rearrange("p (k c) -> p k c", k=nk), src
                     ).then_inc(m.sem(f"slab_loaded{slot}"), 16)

    with m.block() as block:
        @block.sync
        def _(sp):
            with sp.Fori(0, rounds) as r:
                for slot in range(2):
                    sp.wait_ge(m.sem("low_ready"), 2 * r + slot + 1)
                    load(sp, 2 * r + slot, slot)

        @block.scalar
        def _(act):
            with act.Fori(0, rounds) as r:
                for slot in range(2):
                    act.wait_ge(m.sem(f"slab_loaded{slot}"), r * 16 + 16)
                    act.wait_ge(m.sem("tile_done"), r * (2 * per) + slot * per + per)
                    nc.scalar.activation(m.wH[:, slot, 0:n], m.raw[:, slot, 0:n], ACT.Copy
                                         ).then_inc(m.sem("high_ready"), 1)

        @block.vector
        def _(dve):
            dve.sem_inc(m.sem("low_ready"), 2)
            dve.sem_inc(m.sem("added"), 4)

            def low(s, slot):
                dve.wait_ge(m.sem("high_ready"), s + 1)
                nc.vector.tensor_tensor(m.wL[:, slot, 0:n], m.raw[:, slot, 0:n], m.wH[:, slot, 0:n].bitcast(F32),
                                        ALU.subtract).then_inc(m.sem("low_ready"), 1)

            def add(s, slot):
                for c in range(per):
                    dve.wait_ge(m.sem("tile_done"), s * per + c + 1 + 2 * per)
                    add_gated(nc, m, s * per + c, gate_col, (slot * per + c) % 4, m.sem("added"))

            low(0, 0)
            with dve.Fori(0, rounds - 1) as r:
                for slot in range(2):
                    low(2 * r + slot + 1, 1 - slot)
                    add(2 * r + slot, slot)
            low(2 * rounds - 1, 1)
            add(2 * rounds - 2, 0)
            add(2 * rounds - 1, 1)

        @block.tensor
        def _(pe):
            pe.sem_inc(m.sem("tile_done"), 2 * per)
            with pe.Fori(0, rounds) as r:
                for slot in range(2):
                    pe.wait_ge(m.sem("low_ready"), 2 * r + slot + 3)
                    for c in range(per):
                        pe.wait_ge(m.sem("added"), r * (2 * per) + slot * per + c + 1 + 4 - 2 * per)
                        transposed_tile(nc, m, slot, c * P, cols, nk, aH, aL, 0, slot * per + c
                                        ).then_inc(m.sem("tile_done"), 1)


def ffn_in(nc, m, d, L, f0, nf):
    rounds = nf // 2

    def load(sp, f, slot):
        raw = m.raw[:, slot, :].rearrange("p (k c) -> p k c", k=KT)
        for part in range(2):
            sp.dma_start(raw[:, :, part * P:(part + 1) * P], k_tiles(d["w_ffn_in"], L, f * P + f0 * P + part * FF, P)
                         ).then_inc(m.sem(f"slab_loaded{slot}"), 16)

    with m.block() as block:
        @block.sync
        def _(sp):
            with sp.Fori(0, rounds) as r:
                for slot in range(2):
                    sp.wait_ge(m.sem("low_ready"), 2 * r + slot + 1)
                    load(sp, 2 * r + slot, slot)

        @block.scalar
        def _(act):
            def high(s, slot):
                act.wait_ge(m.sem(f"slab_loaded{slot}"), s * 16 - slot * 16 + 32)
                act.wait_ge(m.sem("tile_done"), 2 * s + 2)
                nc.scalar.activation(m.wH[:, slot, :], m.raw[:, slot, :], ACT.Copy).then_inc(m.sem("high_ready"), 1)

            def silu(s, slot):
                act.wait_ge(m.sem("tile_done"), 2 * s + 5)
                act.wait_ge(m.sem("multiplied"), s + 1)
                nc.scalar.activation(halves(m.act[:, slot, :]), m.ps[:, 4 * slot:4 * slot + 2, 0:HALF], ACT.Silu
                                     ).then_inc(m.sem("silu"), 1)

            def split(s, slot):
                act.wait_ge(m.sem("multiplied"), s + 3)
                nc.scalar.activation(m.gH[:, ds(s, 1), :].rearrange("p a t -> p (a t)"), m.gf[:, slot, :], ACT.Copy
                                     ).then_inc(m.sem("g_high"), 1)

            def both(s, slot, more=True):
                if more:
                    high(s + 1, 1 - slot)
                silu(s, slot)
                split(s, slot)

            high(0, 0)
            with act.Fori(0, rounds - 1) as r:
                for slot in range(2):
                    both(2 * r + slot, slot)
            both(nf - 2, 0)
            both(nf - 1, 1, False)

        @block.vector
        def _(dve):
            dve.sem_inc(m.sem("low_ready"), 2)
            dve.sem_inc(m.sem("multiplied"), 2)

            def low(s, slot):
                dve.wait_ge(m.sem("high_ready"), s + 1)
                nc.vector.tensor_tensor(m.wL[:, slot, :], m.raw[:, slot, :], m.wH[:, slot, :].bitcast(F32), ALU.subtract
                                        ).then_inc(m.sem("low_ready"), 1)

            def g(s, slot):
                dve.wait_ge(m.sem("silu"), s + 1)
                dve.wait_ge(m.sem("tile_done"), 2 * s + 6)
                nc.vector.tensor_tensor(halves(m.gf[:, slot, :]), halves(m.act[:, slot, :]),
                                        m.ps[:, 4 * slot + 2:4 * slot + 4, 0:HALF], ALU.mult).then_inc(m.sem("multiplied"), 1)
                dve.wait_ge(m.sem("g_high"), s + 1)
                hi = m.gH[:, ds(s, 1), :].rearrange("p a t -> p (a t)").bitcast(F32)
                nc.vector.tensor_tensor(m.gL[:, ds(s, 1), :].rearrange("p a t -> p (a t)"), m.gf[:, slot, :], hi,
                                        ALU.subtract).then_inc(m.sem("g_low"), 1)

            low(0, 0)
            with dve.Fori(0, rounds - 1) as r:
                for slot in range(2):
                    low(2 * r + slot + 1, 1 - slot)
                    g(2 * r + slot, slot)
            low(nf - 1, 1)
            g(nf - 2, 0)
            g(nf - 1, 1)

        @block.tensor
        def _(pe):
            pe.sem_inc(m.sem("tile_done"), 4)
            with pe.Fori(0, rounds) as r:
                for slot in range(2):
                    pe.wait_ge(m.sem("low_ready"), 2 * r + slot + 3)
                    pe.wait_ge(m.sem("multiplied"), 2 * r + slot + 1)
                    for c in range(2):
                        transposed_tile(nc, m, slot, c * P, W256, KT, m.hH, m.hL, 0, 2 * slot + c
                                        ).then_inc(m.sem("tile_done"), 1)


def last_stage(nc, m, d):
    with m.block() as block:
        @block.tensor
        def _(pe):
            for tt in range(TT):
                if tt >= 4:
                    pe.wait_ge(m.sem("copied"), tt - 3)
                for k in range(KT):
                    b = 2 * (tt % 4) + k // 4
                    last = nc.tensor.transpose(m.ps[:, b, (k % 4) * P:(k % 4 + 1) * P], tok(m.xT[:, k, :], tt),
                                               m.cst[:, K_ID:K_ID + P])
                last.then_inc(m.sem("turned"), 1)

        @block.vector
        def _(dve):
            for tt in range(TT):
                dve.wait_ge(m.sem("turned"), tt + 1)
                if tt >= 2:
                    dve.wait_ge(m.sem(f"stored{tt % 2}"), 16 * (tt // 2))
                b = 2 * (tt % 4)
                nc.vector.tensor_copy(m.xrow[:, tt % 2, :], m.ps[:, b:b + 2, :].rearrange("p b c -> p (b c)")
                                      ).then_inc(m.sem("copied"), 1)

        @block.sync
        def _(sp):
            for tt in range(TT):
                sp.wait_ge(m.sem("copied"), tt + 1)
                dst = d["y_sample"][0, tt * P:(tt + 1) * P, :] if tt < CTX else d["y_prompt"][0, :, :]
                sp.dma_start(dst, m.xrow[:, tt % 2, :]).then_inc(m.sem(f"stored{tt % 2}"), 16)
            sp.wait_ge(m.sem("stored0"), 16 * 3)
            sp.wait_ge(m.sem("stored1"), 16 * 2)


def program(nc, d):
    with ExitStack() as ctx:
        m = Stages(nc, ctx)
        first_stage(nc, m, d)
        with nc.Fori(0, DEPTH) as L:
            modulation(nc, m, d, L)
            norm(nc, m, 0)
            project_gla(nc, m, d, L)
            gla(nc, m, d, L)
            project_attention(nc, m, d, L)
            attention(nc, m, d, L)
            merge(nc, m, d, L)
            project_out(nc, m, d, L, d["w_out"], 16, 0, KT, W256, m.hH, m.hL)
            norm(nc, m, 1)
            for f0, nf in ((0, 12), (12, 10)):
                ffn_in(nc, m, d, L, f0, nf)
                project_out(nc, m, d, L, d["w_ffn_out"], 40, f0, nf, P, m.gH, m.gL)
        last_stage(nc, m, d)


def constants():
    all_ = np.zeros((P, K_COLS), np.float32)
    all_[:, K_ID:K_ID + P] = np.eye(P)
    all_[:, K_ONE:K_ONE + P] = 1.0 / D
    all_[0:3, K_SEL:K_SEL + 2] = [[1, 0], [0, 1], [1, 1]]
    all_[:, K_LAM + 4] = EPS
    lam = np.array([[-(0.8 - 0.6 * math.exp(-0.3 * l)), 1.0 - (0.8 - 0.6 * math.exp(-0.3 * l))]
                    for l in range(DEPTH)], np.float32)
    g = np.zeros((P, G_COLS), np.float32)
    j, i = np.meshgrid(np.arange(P), np.arange(P), indexing="ij")
    same = j // CH == i // CH
    g[:, G_MF:G_MF + P] = same & (j <= i)
    g[:, G_MB:G_MB + P] = same & (j >= i)
    g[:, G_CM:G_CM + T] = (np.arange(T) % CH != 0)
    t = np.arange(DEC)
    f = np.float32(10000.0) ** (-np.arange(16, dtype=np.float32) / np.float32(16))
    rope = np.zeros((P, 2, TT, HD), np.float32)
    rope[:, 0] = 1.0
    for half, pos in enumerate((t // 64, t % 64)):
        ang = (pos.astype(np.float32)[:, None] * f).reshape(4, P, 16).transpose(1, 0, 2)
        c = half * 32
        rope[:, 0, 0:4, c:c + 16] = rope[:, 0, 0:4, c + 16:c + 32] = np.cos(ang)
        rope[:, 1, 0:4, c:c + 16] = np.sin(ang)
        rope[:, 1, 0:4, c + 16:c + 32] = -np.sin(ang)
    return {"const_all": all_, "const_lam": lam, "const_gla": g, "const_rope": rope}


OUTS = [("y_prompt", (1, SEQ, D)), ("y_sample", (1, DEC, D)), ("new_gqa_k", (1, DEPTH, SEQ, 2, HD)),
        ("new_gqa_v", (1, DEPTH, SEQ, 2, HD)), ("new_state_gla", (1, DEPTH, 2, 4, HD, P)),
        ("new_diff_k", (1, DEPTH, SEQ, 4, 2, HD)), ("new_diff_v", (1, DEPTH, SEQ, 4, P))]


def kernel(**inputs):
    import concourse.bacc as bacc
    from concourse.bass_utils import run_bass_kernel_spmd

    nc = bacc.Bacc("TRN2", target_bir_lowering=False, num_devices=1)
    arrays, d = {}, {}
    for name, a in {**inputs, **constants()}.items():
        a = np.ascontiguousarray(a)
        arrays[f"in_{name}"] = a
        d[name] = nc.dram_tensor(f"in_{name}", a.shape, F32, kind="ExternalInput").ap()
    for name, shape in OUTS:
        d[name] = nc.dram_tensor(f"out_{name}", shape, F32, kind="ExternalOutput").ap()
    program(nc, d)
    r = run_bass_kernel_spmd(nc, [arrays], core_ids=[0])
    return tuple(r.results[0][f"out_{name}"] for name, _ in OUTS)
```

```python
import math
from contextlib import ExitStack, contextmanager

import numpy as np

import concourse.bass as bass
from concourse import mybir

F32 = mybir.dt.float32
F32R = mybir.dt.float32r
I32 = mybir.dt.int32
ACT = mybir.ActivationFunctionType
ALU = mybir.AluOpType
AX = mybir.AxisListType
ds = bass.ds

P = 128
D = 1024
KT = D // P
DEPTH = 2
SEQ, DEC, PAST = 128, 512, 128
TT = (SEQ + DEC) // P
CTX = TT - 1
HALF = 320
TILE_AT = [0, 128, 384, 512, 256]
T = 2 * HALF
HD = 64
BW = 512
RANK = 16
TAU = 16.0
CH = 64
NCH = T // CH
FF = 2816
FT = FF // P
EPS = 1e-6
SLAB = 2048
W256 = 256
C_GQ, C_GK, C_GV, C_LQ, C_LK, C_LV, C_LR, C_LGO, C_DQ, C_DK, C_DV, C_MG = (
    0, 512, 640, 768, 1024, 1280, 1792, 1824, 2336, 2848, 3360, 3872)
K_ID, K_ONE, K_LAM = 0, 128, 258
K_COLS = 264
G_MF, G_MB, G_CM, G_COLS = 0, 128, 256, 256 + T
RING = 10
ROW_BANK = [0, 1, 2, 3, 4, 5, 6, 7, 0, 1]
ROW_BACK = [2, 2, 10, 10, 10, 10, 10, 10, 8, 8]


class Signal:

    def __init__(self, sem):
        self.sem, self.base, self.local = sem, 0, 0

    def step(self, ins, by=1):
        ins.then_inc(self.sem, by)
        self.local += by
        return self.sem, self.base + self.local


@contextmanager
def loop(eng, start, stop, **per_round):
    began = {k: s.base + s.local for k, (s, _) in per_round.items()}
    with eng.Fori(start, stop) as i:
        for k, (s, n) in per_round.items():
            s.base, s.local = began[k] + (i - start) * n, 0
        yield i
        for k, (s, n) in per_round.items():
            assert s.local == n, (k, s.local, n)
    for k, (s, n) in per_round.items():
        s.base, s.local = began[k] + (stop - start) * n, 0


def tok(buf, tt):
    return buf[:, TILE_AT[tt]:TILE_AT[tt] + P]


def chunk_pos(idx):
    return TILE_AT[idx // 2] // CH + idx % 2


def segments(buf):
    step = buf.ap[-1][0]
    assert step == 1
    lat = bass.AP(buf.tensor, buf.offset, [list(buf.ap[0]), [384, 2], [1, 256]])
    return lat, buf[:, 256:384].rearrange("p (h c) -> p h c", h=2)


def psum_segments(ps, pair):
    base = ps[:, 2 * pair, :]
    return [bass.AP(base.tensor, base.offset + at, [list(base.ap[0]), [step, 2], [1, n]])
            for at, step, n in ((0, 576, 256), (256, 256, CH))]


class Stages:

    def __init__(self, nc, ctx):
        self.nc, self.ctx, self.sems = nc, ctx, {}
        at = self.at
        self.xT = at("xT", [P, KT, T], 0)
        self.hH = at("hH", [P, KT, T], 20480, F32R)
        self.hL = at("hL", [P, KT, T], 40960, F32R)
        self.raw = at("raw", [P, 2, SLAB], 61440)
        self.wH = at("wH", [P, 2, SLAB], 77824, F32R)
        self.wL = at("wL", [P, 2, SLAB], 94208, F32R)
        x0, x1 = 110592, 110592 + 61440
        small = [x1 + 30720]

        def place(name, shape):
            t = at(name, shape, small[0])
            small[0] += -(-4 * int(np.prod(shape[1:])) // 32) * 32
            return t

        self.cst = place("cst", [P, K_COLS])
        self.sc = place("sc", [P, KT, 2])
        self.mod = place("mod", [P, 48, 2])
        self.aff = place("aff", [P, 2, KT, 2])
        self.nw = place("nw", [P, 2, KT])
        self.nlam = place("nlam", [P, 4])
        self.lp = place("lp", [P, 4 * HD])
        self.gains = place("gains", [P, 4, HD])
        self.subn = place("subn", [P, P])
        self.lpw = place("lpw", [P, 2, HD])
        self.mb = place("mb", [P, 48])
        self.sml = place("sml", [P, 160])
        self.modw = [at(f"modw{j}", [P, KT, W256], 61440 + (0, 8192, 32768, 40960)[j]) for j in range(4)]
        self.mrow = at("mrow", [2, 4, 512], 77824)
        self.mbr = at("mbr", [48, P], x0 + 20480)
        self.sq = at("sq", [P, 2, T], x0)
        self.std = at("std", [P, T], x0 + 5120)
        self.rstd = at("rstd", [P, T], x0 + 7680)
        self.xn = at("xn", [P, 2, T], x0 + 10240)
        self.hf = at("hf", [P, 2, T], x0 + 15360)
        self.xrow = at("xrow", [P, 2, D], x0)
        self.lv = at("lv", [P, TT, BW], x0)
        self.lg = at("lg", [P, TT, BW], x0 + 10240)
        self.lT = at("lT", [P, 5, T], x0 + 20480)
        g = x0 + 33280
        self.g_min, self.g_abs, self.g_sp, self.g_la, self.g_cum, self.g_eq, self.g_ek = [
            at(name, [P, T], g + 2560 * n)
            for n, name in enumerate(("g_min", "g_abs", "g_sp", "g_la", "g_cum", "g_eq", "g_ek"))]
        g = x1
        self.g_qd = at("g_qd", [P, T], x0 + 33280 + 17920)
        self.g_ki = at("g_ki", [P, T], x0 + 33280 + 20480)
        self.g_ke = at("g_ke", [P, T], x0 + 33280 + 23040)
        self.g_ker = at("g_ker", [P, TT, P], g)
        self.g_s = at("g_s", [P, NCH, P], g + 2560)
        self.g_sf = at("g_sf", [P, P], g + 7680)
        self.g_am = at("g_am", [P, 2, 2, 2, P], g + 8192)
        self.g_au = at("g_au", [32, 2, 256], g + 12288)
        self.g_cst = at("g_cst", [P, G_COLS], g + 14336)
        self.g_on = at("g_on", [P, P], g + 17920)
        self.g_ab = at("g_ab", [P, 2, 2], g + 18432)
        self.g_dec = at("g_dec", [P, NCH], g + 18464)
        self.g_st = at("g_st", [P, 80], g + 18528)
        self.g_sq = place("g_sq", [P, 2, P])
        self.rq = at("rq", [P, 8, TT, P], x1)
        self.glr = at("glr", [P, TT, BW], x1 + 20480)
        self.kv = at("kv", [P, 11, TT + 1, P], x0)
        a = x0 + 33792
        self.r_sq = at("r_sq", [P, 2 * T], a)
        self.r_t = at("r_t", [P, 2 * T], a + 5120)
        self.r_c = at("r_c", [P, 4, TT, HD], a + 10240)
        self.r_s = at("r_s", [P, 4, TT, HD], a + 15360)
        self.r_tab = at("r_tab", [P, 2, TT, HD], a + 20480)
        self.r_st = at("r_st", [P, 4, 20], a + 23040)
        self.e = at("e", [P, 4, T], a)
        self.eT = at("eT", [P, 2, TT, P], a + 10240)
        self.a_st = at("a_st", [P, 32, 8], a + 15360)
        self.o_sq = at("o_sq", [P, 2, P], a + 16384)
        self.oH = at("oH", [P, 12, T], x0, F32R)
        self.oL = at("oL", [P, 12, T], x0 + 30720, F32R)
        self.mix = at("mix", [P, KT, T], x1)
        self.gate = at("gate", [P, 2, T], x1 + 20480)
        self.gy = at("gy", [P, 2, T], x1 + 25600)
        self.gH = at("gH", [P, 12, T], x0, F32R)
        self.gL = at("gL", [P, 12, T], x0 + 30720, F32R)
        self.act = at("act", [P, 2, T], x1)
        self.gf = at("gf", [P, 2, T], x1 + 5120)
        assert small[0] + 16512 <= 229344
        self.ps = ctx.enter_context(nc.psum_tensor("ps", [P, 8, 512], F32))

    def at(self, name, shape, offset, dt=F32):
        return self.nc.alloc_sbuf_tensor_at(name, shape, dt, offset=16512 + offset)

    def sem(self, name):
        if name not in self.sems:
            self.sems[name] = self.ctx.enter_context(self.nc.semaphore(name))
        return self.sems[name]

    @contextmanager
    def block(self):
        with self.nc.Block() as block:
            yield block
        nums = [s.num for s in self.sems.values()]
        self.nc.gpsimd.sem_clear(range(min(nums), max(nums) + 1))
        self.nc.all_engine_barrier()


def flat(ap):
    return ap.rearrange("p h c -> p (h c)")


def halves(ap):
    return ap.rearrange("p (h c) -> p h c", h=2)


def high_part(nc, m, act, slot, loaded, used=None):
    act.wait_ge(m.sem(f"slab_loaded{slot}"), loaded)
    if used is not None:
        act.wait_ge(*used)
    nc.scalar.activation(m.wH[:, slot, :], m.raw[:, slot, :], ACT.Copy).then_inc(m.sem("high_ready"), 1)


def low_part(nc, m, dve, s, slot):
    dve.wait_ge(m.sem("high_ready"), s + 1)
    nc.vector.tensor_tensor(m.wL[:, slot, :], m.raw[:, slot, :], m.wH[:, slot, :].bitcast(F32),
                            ALU.subtract).then_inc(m.sem("low_ready"), 1)


def transposed_tile(nc, m, slot, col, cols, nk, aH, aL, k0, pair):
    wh = m.wH[:, slot, 0:nk * cols].rearrange("p (k c) -> p k c", k=nk)
    wl = m.wL[:, slot, 0:nk * cols].rearrange("p (k c) -> p k c", k=nk)
    for k in range(nk):
        for q, (w, a) in enumerate(((wl, aH), (wh, aL), (wh, aH))):
            for n in range(2):
                last = nc.tensor.matmul(m.ps[:, 2 * pair + n, 0:HALF], w[:, k, col:col + P],
                                        a[:, k0 + k, n * HALF:(n + 1) * HALF],
                                        start=(k == 0 and q == 0), stop=(k == nk - 1 and q == 2))
    return last


def row_tile(nc, m, slot, tt, bank):
    wh = m.wH[:, slot, :].rearrange("p (k c) -> p k c", k=KT)
    wl = m.wL[:, slot, :].rearrange("p (k c) -> p k c", k=KT)
    for k in range(KT):
        for q, (a, w) in enumerate(((m.hL, wh), (m.hH, wl), (m.hH, wh))):
            last = nc.tensor.matmul(m.ps[:, bank, 0:W256], tok(a[:, k, :], tt), w[:, k, :],
                                    start=(k == 0 and q == 0), stop=(k == KT - 1 and q == 2))
    return last


def k_tiles(w, L, c0, n):
    return w[ds(L, 1), :, ds(c0, n)].rearrange("a (k p) c -> p (a k) c", p=P)


def first_stage(nc, m, d):
    with m.block() as block:
        @block.sync
        def _(sp):
            sp.dma_start(m.cst[:, :], d["const_all"]).then_inc(m.sem("constants"), 16)
            for tt in range(TT):
                if tt >= 2:
                    sp.wait_ge(m.sem("row_turned"), tt - 1)
                src = d["x_sample"][0, tt * P:(tt + 1) * P, :] if tt < CTX else d["x_prompt"][0, :, :]
                sp.dma_start(m.xrow[:, tt % 2, :], src).then_inc(m.sem(f"row{tt % 2}"), 16)

        @block.scalar
        def _(act):
            act.dma_start(m.sc[:, :, 0:1], d["c"].rearrange("a (k p) -> p k a", p=P),
                          allow_slow_non_contiguous=True).then_inc(m.sem("cond"), 16)
            act.dma_start(m.sc[:, :, 1:2], d["c_ctx"].rearrange("(a k p) -> p k a", p=P, a=1),
                          allow_slow_non_contiguous=True).then_inc(m.sem("cond"), 16)
            act.wait_ge(m.sem("cond"), 32)
            nc.scalar.activation(m.sc[:, :, :], m.sc[:, :, :], ACT.Silu).then_inc(m.sem("silu"), 1)

        @block.tensor
        def _(pe):
            pe.wait_ge(m.sem("constants"), 16)
            for tt in range(TT):
                pe.wait_ge(m.sem(f"row{tt % 2}"), 16 * (tt // 2 + 1))
                if tt >= 4:
                    pe.wait_ge(m.sem("copied"), tt - 3)
                for k in range(KT):
                    b = 2 * (tt % 4) + k // 4
                    last = nc.tensor.transpose(m.ps[:, b, (k % 4) * P:(k % 4 + 1) * P],
                                               m.xrow[:, tt % 2, k * P:(k + 1) * P], m.cst[:, K_ID:K_ID + P])
                last.then_inc(m.sem("row_turned"), 1)

        @block.vector
        def _(dve):
            for tt in range(TT):
                dve.wait_ge(m.sem("row_turned"), tt + 1)
                b = 2 * (tt % 4)
                src = m.ps[:, b:b + 2, :].rearrange("p b (k c) -> p (b k) c", k=4)
                nc.vector.tensor_copy(m.xT[:, :, TILE_AT[tt]:TILE_AT[tt] + P], src).then_inc(m.sem("copied"), 1)


def load_mod(sp, m, d, L, s):
    sp.dma_start(m.modw[s % 4][:, :, :], k_tiles(d["w_mod"], L, s * W256, W256)).then_inc(m.sem(f"mod_loaded{s % 4}"), 16)


def mod_slab(nc, pe, m, s, loaded, bank):
    pe.wait_ge(m.sem(f"mod_loaded{s % 4}"), 16 * loaded)
    for k in range(KT):
        last = nc.tensor.matmul(m.ps[0:2, bank, (s % 2) * W256:(s % 2 + 1) * W256], m.sc[:, k, :],
                                m.modw[s % 4][:, k, :], start=(k == 0), stop=(k == KT - 1))
    return last


def mod_rows(nc, m, b, bank):
    return nc.scalar.activation(m.mrow[:, b:b + 2, :], m.ps[0:2, bank:bank + 2, :], ACT.Copy)


def turn_mod(nc, m, n, bank):
    for t in range(n):
        last = nc.tensor.transpose(m.ps[:, bank, 2 * t:2 * t + 2], m.mrow[:, t // 4, (t % 4) * P:(t % 4 + 1) * P],
                                   m.cst[0:2, K_ID:K_ID + 2])
    return last


def add_mod_bias(nc, m, bank, t, n):
    return nc.vector.tensor_tensor(m.mod[:, t:t + n, :], m.ps[:, bank, 0:2 * n].rearrange("p (t c) -> p t c", c=2),
                                   m.mb[:, t:t + n].unsqueeze(2).broadcast_to([P, n, 2]), ALU.add)


def affine(nc, m, dve, order, n):
    first = (8, 32)[n]
    done = order.step(nc.vector.tensor_scalar(m.aff[:, n, :, :], m.mod[:, first:first + KT, :], 1.0, None, ALU.add))
    dve.wait_ge(*done)
    return nc.vector.tensor_tensor(m.aff[:, n, :, :], m.aff[:, n, :, :],
                                   m.nw[:, n, :].unsqueeze(2).broadcast_to([P, KT, 2]), ALU.mult)


def norm(nc, m, d, L, which):
    shift = (0, 24)[which]
    first = which == 0
    with m.block() as block:
        if first:
            @block.sync
            def _(sp):
                for s in range(8):
                    if s >= 4:
                        sp.wait_ge(m.sem("slab_used"), s - 3)
                    load_mod(sp, m, d, L, s)

        @block.scalar
        def _(act):
            if first:
                small = m.sem("small_params")
                act.dma_start(m.mbr[:, :], d["b_mod"][ds(L, 1), :].rearrange("a (t c) -> (a t) c", c=P)
                              ).then_inc(m.sem("bias_rows"), 16)
                act.dma_start(m.lp[:, :], d["diff_lambda"][ds(L, 1), :, :].rearrange("a b c -> (a b c)").
                              partition_broadcast(P)).then_inc(small, 16)
                act.dma_start(m.nlam[:, 0:2], d["const_lam"][ds(L, 1), :].rearrange("a c -> (a c)").
                              partition_broadcast(P)).then_inc(small, 16)
                for n, name in enumerate(("gqa_q_norm", "diff_q_norm", "gqa_k_norm", "diff_k_norm")):
                    act.dma_start(m.gains[:, n, :], d[name][ds(L, 1), :].rearrange("a c -> (a c)").
                                  partition_broadcast(P)).then_inc(small, 16)
                act.dma_start(m.subn[:, :], d["diff_sub_norm"][ds(L, 1), :].rearrange("a c -> (a c)").
                              partition_broadcast(P)).then_inc(small, 16)
                for n, name in enumerate(("norm1", "norm2")):
                    act.dma_start(m.nw[:, n, :], d[name][ds(L, 1), :].rearrange("a (k p) -> p (a k)", p=P),
                                  allow_slow_non_contiguous=True).then_inc(small, 16)
            for k in range(KT):
                if k >= 2:
                    act.wait_ge(m.sem("summed"), k - 1)
                nc.scalar.activation(m.sq[:, k % 2, :], m.xT[:, k, :], ACT.Square).then_inc(m.sem("squares"), 1)
                if first and k == 1:
                    act.wait_ge(m.sem("lam_sums"), 2)
                    nc.scalar.activation(m.nlam[:, 2:4], m.nlam[:, 2:4], ACT.Exp).then_inc(m.sem("lam_exp"), 1)
                if first and k == 5:
                    act.wait_ge(m.sem("slab_used"), 4)
                    mod_rows(nc, m, 0, 3).then_inc(m.sem("mod_rows"), 1)
            if first:
                act.wait_ge(m.sem("slab_used"), 8)
                mod_rows(nc, m, 2, 5).then_inc(m.sem("mod_rows"), 1)
            act.wait_ge(m.sem("summed"), KT)
            nc.scalar.activation(halves(m.std[:, :]), m.ps[:, 0:2, 0:HALF], ACT.Sqrt,
                                 bias=m.cst[:, K_LAM + 4:K_LAM + 5]).then_inc(m.sem("std"), 1)
            if first:
                act.wait_ge(m.sem("mod_ready"), 1)
            for k in range(KT):
                act.wait_ge(m.sem("normed"), k + 1)
                if k >= 2:
                    act.wait_ge(m.sem("low"), k - 1)
                for c, (o, i) in enumerate(zip(segments(m.hf[:, k % 2, :]), segments(m.xn[:, k % 2, :]))):
                    ins = nc.scalar.activation(o, i, ACT.Identity, bias=m.mod[:, shift + k, c:c + 1],
                                               scale=m.aff[:, which, k, c:c + 1])
                ins.then_inc(m.sem("shifted"), 1)
                act.wait_ge(m.sem("shifted"), k + 1)
                nc.scalar.activation(m.hH[:, k, :], m.hf[:, k % 2, :], ACT.Copy).then_inc(m.sem("high"), 1)

        @block.tensor
        def _(pe):
            if first:
                pe.wait_ge(m.sem("bias_rows"), 16)
                nc.tensor.transpose(m.ps[:, 2, 0:48], m.mbr[:, :], m.cst[0:48, K_ID:K_ID + 48]
                                    ).then_inc(m.sem("bias_turned"), 1)
            for k in range(KT):
                if first:
                    mod_slab(nc, pe, m, k, k // 4 + 1, 3 + k // 2).then_inc(m.sem("slab_used"), 1)
                pe.wait_ge(m.sem("squares"), k + 1)
                for n in range(2):
                    last = nc.tensor.matmul(m.ps[:, n, 0:HALF], m.cst[:, K_ONE:K_ONE + P],
                                            m.sq[:, k % 2, n * HALF:(n + 1) * HALF], start=(k == 0), stop=(k == KT - 1))
                last.then_inc(m.sem("summed"), 1)
            if first:
                pe.wait_ge(m.sem("mod_rows"), 2)
                turn_mod(nc, m, 16, 7).then_inc(m.sem("mod_turned"), 1)

        @block.vector
        def _(dve):
            if first:
                order = Signal(m.sem("dve_order"))
                dve.wait_ge(m.sem("small_params"), 9 * 16)
                lp = m.lp[:, :].rearrange("p (a b c) -> p a b c", a=2, b=2)
                done = order.step(nc.vector.tensor_tensor(m.lpw[:, :, :], lp[:, :, 0, :], lp[:, :, 1, :], ALU.mult))
                dve.wait_ge(*done)
                nc.vector.tensor_reduce(m.nlam[:, 2:4], m.lpw[:, :, :], AX.X, ALU.add).then_inc(m.sem("lam_sums"), 2)
                dve.wait_ge(m.sem("lam_exp"), 1)
                done = order.step(nc.vector.tensor_tensor(m.nlam[:, 2:3], m.nlam[:, 3:4], m.nlam[:, 2:3], ALU.subtract))
                dve.wait_ge(*done)
                order.step(nc.vector.tensor_tensor(m.nlam[:, 0:1], m.nlam[:, 2:3], m.nlam[:, 0:1], ALU.add))
                order.step(nc.vector.tensor_scalar(m.subn[:, :], m.subn[:, :], m.nlam[:, 1:2], None, ALU.mult))
                dve.wait_ge(m.sem("bias_turned"), 1)
                done = order.step(nc.vector.tensor_copy(m.mb[:, :], m.ps[:, 2, 0:48]))
                dve.wait_ge(*done)
                dve.wait_ge(m.sem("mod_turned"), 1)
                done = order.step(add_mod_bias(nc, m, 7, 0, 16))
                dve.wait_ge(*done)
                affine(nc, m, dve, order, 0).then_inc(m.sem("mod_ready"), 1)
            dve.wait_ge(m.sem("std"), 1)
            nc.vector.reciprocal(m.rstd[:, :], m.std[:, :]).then_inc(m.sem("rstd"), 1)
            dve.wait_ge(m.sem("rstd"), 1)
            for k in range(KT + 1):
                if k < KT:
                    if k >= 2:
                        dve.wait_ge(m.sem("shifted"), k - 1)
                    nc.vector.tensor_tensor(m.xn[:, k % 2, :], m.xT[:, k, :], m.rstd[:, :], ALU.mult
                                            ).then_inc(m.sem("normed"), 1)
                if k >= 1:
                    dve.wait_ge(m.sem("high"), k)
                    nc.vector.tensor_tensor(m.hL[:, k - 1, :], m.hf[:, (k - 1) % 2, :],
                                            m.hH[:, k - 1, :].bitcast(F32), ALU.subtract).then_inc(m.sem("low"), 1)


def project_gla(nc, m, d, L):
    cols = [C_LV, C_LV + 256, C_LGO, C_LGO + 256, C_LQ, C_LK, C_LR]
    rows, n = 4, len(cols)
    tiles = {4: (0, 1), 5: (0, 1), 6: (0,)}
    done_after = [5, 10, 15, 20, 22, 24, 25]
    with m.block() as block:
        @block.sync
        def _(sp):
            for s, c in enumerate(cols):
                if s >= 2:
                    sp.wait_ge(m.sem("low_ready"), s - 1)
                sp.dma_start(m.raw[:, s % 2, :].rearrange("p (k c) -> p k c", k=KT),
                             k_tiles(d["w_in"], L, c, W256)).then_inc(m.sem(f"slab_loaded{s % 2}"), 16)

        @block.scalar
        def _(act):
            def high(s):
                high_part(nc, m, act, s % 2, 16 * (s // 2 + 1), (m.sem("tile_done"), done_after[s - 2]) if s > 1 else None)

            high(0)
            for s in range(n):
                if s + 1 < n:
                    high(s + 1)
                if s < rows:
                    dst = m.lv if s < 2 else m.lg
                    for tt in range(TT):
                        act.wait_ge(m.sem("tile_done"), 5 * s + tt + 1)
                        nc.scalar.activation(dst[:, tt, (s % 2) * 256:(s % 2 + 1) * 256],
                                             m.ps[:, ROW_BANK[(5 * s + tt) % RING], 0:256], ACT.Copy
                                             ).then_inc(m.sem("tile_copied"), 1)
                else:
                    for col in tiles[s]:
                        t = 2 * (s - rows) + col
                        act.wait_ge(m.sem("tile_done"), 20 + t + 1)
                        nc.scalar.activation(halves(m.lT[:, t, :]), m.ps[:, 2 * (t % 4):2 * (t % 4) + 2, 0:HALF],
                                             ACT.Copy, scale=(HD ** -0.5 if t < 2 else 1.0)
                                             ).then_inc(m.sem("tile_copied"), 1)

        @block.vector
        def _(dve):
            for s in range(n):
                low_part(nc, m, dve, s, s % 2)

        @block.tensor
        def _(pe):
            for s in range(n):
                pe.wait_ge(m.sem("low_ready"), s + 1)
                if s < rows:
                    for tt in range(TT):
                        g = 5 * s + tt
                        back = ROW_BACK[g % RING]
                        if g >= back:
                            pe.wait_ge(m.sem("tile_copied"), g - back + 1)
                        row_tile(nc, m, s % 2, tt, ROW_BANK[g % RING]).then_inc(m.sem("tile_done"), 1)
                else:
                    for col in tiles[s]:
                        t = 2 * (s - rows) + col
                        pe.wait_ge(m.sem("tile_copied"), 20 if t < 4 else 20 + t - 3)
                        transposed_tile(nc, m, s % 2, col * P, W256, KT, m.hH, m.hL, 0, t % 4
                                        ).then_inc(m.sem("tile_done"), 1)


def gla(nc, m, d, L):
    units = [(hp, dr) for hp in range(2) for dr in range(2)]
    def ds_at(idx, rows=slice(0, P)):
        tt, half = idx // 2, idx % 2
        return m.ps[rows, (2, 0)[half] + tt // 4, (tt % 4) * P:(tt % 4 + 1) * P]

    with m.block() as block:
        @block.gpsimd
        def _(pool):
            pool.memset(m.g_au[:, :, :], 0.0).then_inc(m.sem("au_zero"), 1)
            pool.memset(m.g_am[:, :, :, :, :], 0.0).then_inc(m.sem("am_zero"), 1)

        @block.sync
        def _(sp):
            ld = m.sem("gla_params")
            sp.dma_start(m.g_cst[:, :], d["const_gla"]).then_inc(ld, 16)
            sp.wait_ge(m.sem("au_zero"), 1)
            for z in range(2):
                sp.dma_start(m.g_au[RANK * z:RANK * (z + 1), z, :],
                             d["gla_alpha_up"][ds(L, 1), z, :, :].rearrange("a r c -> (a r) c")).then_inc(ld, 16)
            sp.dma_start(m.g_on[:, :], d["gla_out_norm"][ds(L, 1), :].rearrange("a c -> (a c)").
                         partition_broadcast(P)).then_inc(ld, 16)
            for z in range(2):
                sp.dma_start(m.g_ab[:, z, :], d["gla_alpha_bias"][ds(L, 1), z, :].rearrange("a (h p) -> p (a h)", p=P),
                             allow_slow_non_contiguous=True).then_inc(ld, 16)
            for u, (hp, dr) in enumerate(units):
                for j in range(4):
                    if u:
                        sp.wait_ge(m.sem("slab_used"), 4 * u - 3 + j)
                    load_mod(sp, m, d, L, 8 + 4 * u + j)
                if u:
                    sp.wait_ge(m.sem("o_done"), 5 * u)
                sp.dma_start(m.g_s[:, (0, 7)[dr], :],
                             d["state_gla"][0, ds(L, 1), dr, 2 * hp:2 * hp + 2, :, :].
                             rearrange("a h k e -> (a h k) e")).then_inc(m.sem("state_in"), 16)
                sp.wait_ge(m.sem("state_done"), u + 1)
                sp.dma_start(d["new_state_gla"][0, ds(L, 1), dr, 2 * hp:2 * hp + 2, :, :].
                             rearrange("a h k e -> (a h k) e"), m.g_sf[:, :]).then_inc(m.sem("state_out"), 16)
            sp.wait_ge(m.sem("state_out"), 16 * len(units))

        @block.scalar
        def _(act):
            order = Signal(m.sem("act_order"))
            done = order.step(nc.scalar.activation(m.lg[:, :, :], m.lg[:, :, :], ACT.Silu))
            act.wait_ge(m.sem("gla_params"), 6 * 16)
            for u, (hp, dr) in enumerate(units):
                last = slice(CH - 1, CH) if dr == 0 else slice(0, 1)
                act.wait_ge(m.sem("z_min"), u + 1)
                done = order.step(nc.scalar.activation(halves(m.g_abs[:, :]), m.ps[:, 0:2, 0:HALF], ACT.Abs,
                                                       bias=m.g_ab[:, dr, hp:hp + 1]))
                act.wait_ge(*done)
                done = order.step(nc.scalar.activation(m.g_abs[:, :], m.g_abs[:, :], ACT.Exp, scale=-1.0))
                act.wait_ge(*done)
                nc.scalar.activation(m.g_sp[:, :], m.g_abs[:, :], ACT.Ln, bias=1.0).then_inc(m.sem("softplus"), 1)
                act.wait_ge(m.sem("cum_done"), u + 1)
                if u:
                    act.wait_ge(m.sem("q_decayed"), u)
                    act.wait_ge(m.sem("k_end"), u)
                    act.wait_ge(m.sem("state_done"), u)
                nc.scalar.activation(m.g_eq[:, :], m.g_cum[:, :], ACT.Exp, scale=1.0 / TAU).then_inc(m.sem("exp_q"), 1)
                nc.scalar.activation(m.g_ek[:, :], m.g_cum[:, :], ACT.Exp, scale=-1.0 / TAU).then_inc(m.sem("exp_k"), 1)
                nc.scalar.activation(m.g_dec[:, :], m.g_cum[:, :].rearrange("p (c t) -> p c t", t=CH)[:, :, last].
                                     rearrange("p c t -> p (c t)"), ACT.Exp, scale=1.0 / TAU).then_inc(m.sem("decay"), 1)
                act.wait_ge(m.sem("to_end"), u + 1)
                nc.scalar.activation(m.g_min[:, :], m.g_la[:, :], ACT.Exp, scale=1.0 / TAU).then_inc(m.sem("exp_end"), 1)
                act.wait_ge(m.sem("ke_turned"), u + 1)
                if u:
                    act.wait_ge(m.sem("ds_done"), u)
                nc.scalar.activation(m.g_ker[:, 0:4, :].rearrange("p t c -> p (t c)"), m.ps[:, 0, :], ACT.Copy)
                nc.scalar.activation(m.g_ker[:, 4, :], m.ps[:, 1, 0:P], ACT.Copy).then_inc(m.sem("ke_rows"), 1)
                act.wait_ge(m.sem("slab_used"), 4 * u + 4)
                mod_rows(nc, m, 0, 4).then_inc(m.sem("mod_rows"), 1)
                if dr == 1:
                    for tt in range(TT):
                        act.wait_ge(m.sem("o_summed"), 5 * u + tt + 1)
                        for hh in range(2):
                            g = 10 * hp + 2 * tt + hh
                            done = order.step(nc.scalar.activation(
                                m.g_sq[:, hh, :], m.glr[:, tt, (2 * hp + hh) * P:(2 * hp + hh + 1) * P], ACT.Square,
                                accum_out=m.g_st[:, g:g + 1]))
                        act.wait_ge(*done)
                    half = slice(10 * hp, 10 * hp + 10)
                    nc.scalar.activation(m.g_st[:, 20:40][:, half], m.g_st[:, half], ACT.Sqrt, scale=1.0 / P,
                                         bias=m.cst[:, K_LAM + 4:K_LAM + 5]).then_inc(m.sem("o_std"), 1)

        @block.tensor
        def _(pe):
            pe.wait_ge(m.sem("gla_params"), 6 * 16)
            for u, (hp, dr) in enumerate(units):
                if u:
                    pe.wait_ge(m.sem("ke_rows"), u)
                for n in range(2):
                    last = nc.tensor.matmul(m.ps[:, n, 0:HALF], m.g_au[0:32, dr, hp * P:(hp + 1) * P],
                                            m.lT[0:32, 4, n * HALF:(n + 1) * HALF], start=True, stop=True)
                last.then_inc(m.sem("z_done"), 1)
                if u:
                    pe.wait_ge(m.sem("o_summed"), 5 * u)
                for j in range(3):
                    mod_slab(nc, pe, m, j, u + 1, 4 + j // 2).then_inc(m.sem("slab_used"), 1)
                pe.wait_ge(m.sem("k_end"), u + 1)
                for tt in range(TT):
                    last = nc.tensor.transpose(m.ps[:, tt // 4, (tt % 4) * P:(tt % 4 + 1) * P],
                                               tok(m.g_ke[:, :], tt), m.cst[:, K_ID:K_ID + P])
                last.then_inc(m.sem("ke_turned"), 1)
                pe.wait_ge(m.sem("ke_rows"), u + 1)
                if u:
                    pe.wait_ge(m.sem("mod_copied"), u)
                for idx in range(NCH):
                    tt, half = idx // 2, idx % 2
                    for hh in range(2):
                        last = nc.tensor.matmul(ds_at(idx, slice(64 * hh, 64 * hh + 64)),
                                                m.g_ker[64 * half:64 * half + 64, tt, 64 * hh:64 * hh + 64],
                                                m.lv[64 * half:64 * half + 64, tt, (2 * hp + hh) * P:(2 * hp + hh + 1) * P],
                                                start=True, stop=True)
                last.then_inc(m.sem("ds_done"), 1)

                def scores(tt):
                    a = 5 * u + tt
                    if a >= 1:
                        pe.wait_ge(m.sem("a_masked"), a)
                    for hh in range(2):
                        h = slice(64 * hh, 64 * hh + 64)
                        last = nc.tensor.matmul(m.ps[:, 6 + hh, 0:P], tok(m.g_ki[h, :], tt),
                                                tok(m.g_qd[h, :], tt), start=True, stop=True)
                    last.then_inc(m.sem("a_done"), 1)

                def outputs(tt):
                    a = 5 * u + tt
                    pe.wait_ge(m.sem("a_masked"), a + 1)
                    if a >= 1:
                        pe.wait_ge(m.sem("o_summed"), a)
                    for hh in range(2):
                        nc.tensor.matmul(m.ps[:, 4 + hh, 0:P], m.g_am[:, dr, a % 2, hh, :],
                                         m.lv[:, tt, (2 * hp + hh) * P:(2 * hp + hh + 1) * P],
                                         start=True, stop=False, skip_group_check=True)
                        for half in range(2):
                            q = chunk_pos(2 * tt + half) * CH
                            last = nc.tensor.matmul(m.ps[64 * half:64 * half + 64, 4 + hh, 0:P],
                                                    m.g_qd[64 * hh:64 * hh + 64, q:q + CH],
                                                    m.g_s[64 * hh:64 * hh + 64, 2 * tt + half, :],
                                                    start=False, stop=True, skip_group_check=True)
                    last.then_inc(m.sem("o_done"), 1)

                pe.wait_ge(m.sem("k_inv"), u + 1)
                scores(0)
                mod_slab(nc, pe, m, 3, u + 1, 5).then_inc(m.sem("slab_used"), 1)
                pe.wait_ge(m.sem("state_done"), u + 1)
                pe.wait_ge(m.sem("mod_rows"), u + 1)
                turn_mod(nc, m, 8, 2).then_inc(m.sem("mod_turned"), 1)
                for tt in range(TT):
                    if tt + 1 < TT:
                        scores(tt + 1)
                    outputs(tt)

        @block.vector
        def _(dve):
            order = Signal(m.sem("dve_order"))
            dve.wait_ge(m.sem("gla_params"), 6 * 16)
            dve.wait_ge(m.sem("am_zero"), 1)

            def inverse(hp):
                return order.step(nc.vector.reciprocal(m.g_st[:, 40 + 10 * hp:50 + 10 * hp],
                                                       m.g_st[:, 20 + 10 * hp:30 + 10 * hp]))

            def gate(hp, tt):
                for hh in range(2):
                    c = slice((2 * hp + hh) * P, (2 * hp + hh + 1) * P)
                    g = 40 + 10 * hp + 2 * tt + hh
                    order.step(nc.vector.scalar_tensor_tensor(out=m.glr[:, tt, c], in0=m.glr[:, tt, c],
                                                              scalar=m.g_st[:, g:g + 1], in1=m.lg[:, tt, c],
                                                              op0=ALU.mult, op1=ALU.mult))

            for u, (hp, dr) in enumerate(units):
                flip = slice(None, None, -1) if dr else slice(None)
                last = slice(CH - 1, CH) if dr == 0 else slice(0, 1)
                dve.wait_ge(m.sem("z_done"), u + 1)
                nc.vector.tensor_scalar(halves(m.g_min[:, :]), m.ps[:, 0:2, 0:HALF], m.g_ab[:, dr, hp:hp + 1], 0.0,
                                        ALU.add, ALU.min).then_inc(m.sem("z_min"), 1)
                if u == 0:
                    dve.wait_ge(m.sem("act_order"), 1)
                    lg = m.lg[:, :, :].rearrange("p t (h c) -> p (t h) c", c=P)
                    gated = order.step(nc.vector.tensor_tensor(lg, lg, m.g_on[:, :].unsqueeze(1).broadcast_to([P, 20, P]),
                                                               ALU.mult))
                    dve.wait_ge(*gated)
                dve.wait_ge(m.sem("z_min"), u + 1)
                dve.wait_ge(m.sem("softplus"), u + 1)
                done = (m.sem("la_done"), u + 1)
                nc.vector.tensor_tensor(m.g_la[:, :], m.g_min[:, :], m.g_sp[:, :], ALU.subtract).then_inc(m.sem("la_done"), 1)
                dve.wait_ge(*done)
                nc.vector.tensor_tensor_scan(m.g_cum[:, flip], m.g_cst[:, G_CM:G_CM + T], m.g_la[:, flip], 0.0,
                                             ALU.mult, ALU.add).then_inc(m.sem("cum_done"), 1)
                dve.wait_ge(m.sem("cum_done"), u + 1)
                cum = m.g_cum[:, :].rearrange("p (c t) -> p c t", t=CH)
                nc.vector.tensor_tensor(m.g_la[:, :].rearrange("p (c t) -> p c t", t=CH),
                                        cum[:, :, last].broadcast_to([P, NCH, CH]), cum, ALU.subtract
                                        ).then_inc(m.sem("to_end"), 1)
                if u:
                    dve.wait_ge(m.sem("o_done"), 5 * u)
                dve.wait_ge(m.sem("exp_q"), u + 1)
                nc.vector.tensor_tensor(m.g_qd[:, :], m.lT[:, hp, :], m.g_eq[:, :], ALU.mult).then_inc(m.sem("q_decayed"), 1)
                dve.wait_ge(m.sem("exp_k"), u + 1)
                nc.vector.tensor_tensor(m.g_ki[:, :], m.lT[:, 2 + hp, :], m.g_ek[:, :], ALU.mult).then_inc(m.sem("k_inv"), 1)
                dve.wait_ge(m.sem("exp_end"), u + 1)
                nc.vector.tensor_tensor(m.g_ke[:, :], m.lT[:, 2 + hp, :], m.g_min[:, :], ALU.mult).then_inc(m.sem("k_end"), 1)
                dve.wait_ge(m.sem("decay"), u + 1)
                dve.wait_ge(m.sem("ds_done"), u + 1)
                dve.wait_ge(m.sem("state_in"), 16 * (u + 1))
                if u:
                    dve.wait_ge(m.sem("state_out"), 16 * u)
                done = order.step(nc.vector.memset(m.g_s[:, (8, 9)[dr], :], 0.0))
                run = list(range(0, 7)) + [8] if dr == 0 else list(range(7, 0, -1)) + [9]
                to = 1 if dr == 0 else -1
                for idx in run:
                    dve.wait_ge(*done)
                    done = order.step(nc.vector.scalar_tensor_tensor(
                        out=m.g_s[:, idx + to, :], in0=m.g_s[:, idx, :],
                        scalar=m.g_dec[:, chunk_pos(idx):chunk_pos(idx) + 1],
                        in1=ds_at(idx), op0=ALU.mult, op1=ALU.add))
                dve.wait_ge(*done)
                idx = 9 if dr == 0 else 8
                nc.vector.scalar_tensor_tensor(
                    out=m.g_sf[:, :], in0=m.g_s[:, idx, :], scalar=m.g_dec[:, chunk_pos(idx):chunk_pos(idx) + 1],
                    in1=ds_at(idx), op0=ALU.mult, op1=ALU.add
                ).then_inc(m.sem("state_done"), 1)

                def mask(tt):
                    a = 5 * u + tt
                    dve.wait_ge(m.sem("a_done"), a + 1)
                    if a >= 2:
                        dve.wait_ge(m.sem("o_done"), a - 1)
                    msk = m.g_cst[:, (G_MF, G_MB)[dr]:(G_MF, G_MB)[dr] + P].bitcast(I32)
                    nc.vector.copy_predicated(m.g_am[:, dr, a % 2, :, :], msk.unsqueeze(1).broadcast_to([P, 2, P]),
                                              m.ps[:, 6:8, 0:P]
                                              ).then_inc(m.sem("a_masked"), 1)

                mask(0)
                dve.wait_ge(m.sem("mod_turned"), u + 1)
                add_mod_bias(nc, m, 2, 16 + 8 * u, 8).then_inc(m.sem("mod_copied"), 1)
                if u == 2:
                    dve.wait_ge(m.sem("o_std"), 1)
                    done = inverse(0)
                    dve.wait_ge(*done)
                for tt in range(TT):
                    a = 5 * u + tt
                    if tt + 1 < TT:
                        mask(tt + 1)
                    if u == 2:
                        gate(0, tt)
                    dve.wait_ge(m.sem("o_done"), a + 1)
                    dst = m.glr[:, tt, hp * 256:(hp + 1) * 256].rearrange("p (h c) -> p h c", h=2)
                    src = m.ps[:, 4:6, 0:P]
                    if dr == 0:
                        nc.vector.tensor_copy(dst, src).then_inc(m.sem("o_summed"), 1)
                    else:
                        dve.wait_ge(m.sem("o_summed"), a - 4)
                        nc.vector.tensor_tensor(dst, dst, src, ALU.add).then_inc(m.sem("o_summed"), 1)
            dve.wait_ge(m.sem("mod_copied"), 4)
            order.step(affine(nc, m, dve, order, 1))
            dve.wait_ge(m.sem("o_std"), 2)
            done = inverse(1)
            dve.wait_ge(*done)
            for tt in range(TT):
                gate(1, tt)


def project_attention(nc, m, d, L):
    slabs = [(C_GQ, 0), (C_GQ + 256, 0), (C_DQ, 1), (C_DQ + 256, 1), (C_GK, 2), (C_DK, 3), (C_DK + 256, 3),
             (C_DV, None), (C_DV + 256, None)]
    n = len(slabs)

    def place(s):
        if s < 4:
            return m.rq[:, 2 * s:2 * s + 2, :, :]
        b = {4: 8, 5: 0, 6: 2, 7: 4, 8: 6}[s]
        return m.kv[:, b:b + 2, 0:TT, :]

    normed = [s for s in range(n) if slabs[s][1] is not None]
    turns = {s: [] for s in range(n)}
    for s in normed:
        if s < 4:
            turns[s + 2] += [(2 * c, m.rq, 2 * s + c, TT, 0) for c in range(2)]
        elif s == 4:
            turns[s + 2] += [(0, m.kv, 8, TT + 1, 1), (2, m.kv, 10, TT + 1, 1)]
        else:
            turns[s + 2] += [(2 * c, m.kv, 2 * (s - 5) + c, TT + 1, s - 3) for c in range(2)]
    with m.block() as block:
        @block.sync
        def _(sp):
            out = m.sem("kv_stored")
            for s, (c, _) in enumerate(slabs):
                if s >= 2:
                    sp.wait_ge(m.sem("low_ready"), s - 1)
                sp.dma_start(m.raw[:, s % 2, :].rearrange("p (k c) -> p k c", k=KT),
                             k_tiles(d["w_in"], L, c, W256)).then_inc(m.sem(f"slab_loaded{s % 2}"), 16)
                if s == 7:
                    sp.wait_ge(m.sem("normed"), 5)
                    sp.dma_start(d["new_gqa_k"][0, ds(L, 1), :, :, :].rearrange("a t h c -> (a t) (h c)"),
                                 m.kv[:, 8, CTX, :]).then_inc(m.sem("k_stored0"), 16)
            for h in range(2):
                sp.wait_ge(m.sem("normed"), 6 + h)
                sp.dma_start(d["new_diff_k"][0, ds(L, 1), :, 2 * h:2 * h + 2, :, :].rearrange("a t h m c -> (a t) h (m c)"),
                             m.kv[:, 2 * h:2 * h + 2, CTX, :]).then_inc(m.sem(f"k_stored{h + 1}"), 16)
            sp.wait_ge(m.sem("tile_copied"), 5 * n)
            sp.dma_start(d["new_gqa_v"][0, ds(L, 1), :, :, :].rearrange("a t h c -> (a t) (h c)"),
                         m.kv[:, 9, CTX, :]).then_inc(out, 16)
            sp.dma_start(d["new_diff_v"][0, ds(L, 1), :, :, :].rearrange("a t h c -> (a t) h c"),
                         m.kv[:, 4:8, CTX, :]).then_inc(out, 16)
            sp.wait_ge(out, 32)
            sp.wait_ge(m.sem("caches"), 6 * 16)

        @block.gpsimd
        def _(pool):
            pool.wait_ge(m.sem("rope_tables"), 16)
            for kind in range(4):
                w = m.gains[:, kind, :].unsqueeze(1).broadcast_to([P, TT, HD])
                nc.gpsimd.tensor_tensor(m.r_c[:, kind, :, :], m.r_tab[:, 0, :, :], w, ALU.mult).then_inc(m.sem("tables"), 1)
                nc.gpsimd.tensor_tensor(m.r_s[:, kind, :, :], m.r_tab[:, 1, :, :], w, ALU.mult).then_inc(m.sem("tables"), 1)

        @block.scalar
        def _(act):
            act.dma_start(m.r_tab[:, :, :, :], d["const_rope"]).then_inc(m.sem("rope_tables"), 16)
            caches = m.sem("caches")
            act.dma_start(m.kv[:, 0:4, TT, :], d["cache_diff_k"][0, ds(L, 1), :, :, :, :].
                           rearrange("a t h m c -> (a t) h (m c)")).then_inc(caches, 16)
            act.dma_start(m.kv[:, 4:8, TT, :], d["cache_diff_v"][0, ds(L, 1), :, :, :].
                           rearrange("a t h c -> (a t) h c")).then_inc(caches, 16)
            gk = d["cache_gqa_k"][0, ds(L, 1), :, :, :].rearrange("a t h c -> (a t) h c")
            act.dma_start(m.kv[:, 8, TT, :].rearrange("p (h c) -> p h c", h=2), gk).then_inc(caches, 16)
            act.dma_start(m.kv[:, 9, TT, :].rearrange("p (h c) -> p h c", h=2),
                           d["cache_gqa_v"][0, ds(L, 1), :, :, :].rearrange("a t h c -> (a t) h c")).then_inc(caches, 16)
            for h in range(2):
                act.dma_start(m.kv[:, 10, TT, (1 - h) * HD:(2 - h) * HD], gk[:, h, :]).then_inc(caches, 16)
            def high(s):
                high_part(nc, m, act, s % 2, 16 * (s // 2 + 1), (m.sem("tile_done"), 5 * (s - 1)) if s > 1 else None)

            high(0)
            q = turn = 0
            for s in range(n):
                if s + 1 < n:
                    high(s + 1)
                for tt in range(TT):
                    act.wait_ge(m.sem("tile_done"), 5 * s + tt + 1)
                    nc.scalar.activation(place(s)[:, :, tt, :],
                                         m.ps[:, (5 * s + tt) % 6, 0:256].rearrange("p (b c) -> p b c", b=2),
                                         ACT.Copy).then_inc(m.sem("tile_copied"), 1)
                    for after, buf, b, tiles, stored in turns[s]:
                        if after == tt:
                            act.wait_ge(m.sem("turned"), turn + 1)
                            if stored:
                                act.wait_ge(m.sem(f"k_stored{stored - 1}"), 16)
                            nc.scalar.activation(buf[:, b, 0:tiles, :].rearrange("p t c -> p (t c)"),
                                                 m.ps[:, 6:8, :].rearrange("p b c -> p (b c)")[:, 0:tiles * P], ACT.Copy,
                                                 scale=(HD ** -0.5 if turn < 8 else 1.0)
                                                 ).then_inc(m.sem("turned_copied"), 1)
                            turn += 1
                if s in normed:
                    nb = 1 if s == 4 else 2
                    act.wait_ge(m.sem("tile_copied"), 5 * s + 5)
                    if q:
                        act.wait_ge(m.sem("mean_squares"), q)
                    nc.scalar.activation(m.r_sq[:, 0:nb * T].rearrange("p (b t) -> p b t", b=nb),
                                         place(s)[:, 0:nb, :, :].rearrange("p b t c -> p b (t c)"), ACT.Square
                                         ).then_inc(m.sem("squares"), 1)
                    act.wait_ge(m.sem("mean_squares"), q + 1)
                    if q:
                        act.wait_ge(m.sem("normed"), q)
                    nc.scalar.activation(m.r_st[:, 1, 0:10 * nb], m.r_st[:, 0, 0:10 * nb], ACT.Sqrt, scale=1.0 / HD,
                                         bias=m.cst[:, K_LAM + 4:K_LAM + 5]).then_inc(m.sem("head_std"), 1)
                    q += 1

        @block.vector
        def _(dve):
            order = Signal(m.sem("dve_order"))
            low_part(nc, m, dve, 0, 0)
            q = 0
            for s, (_, kind) in enumerate(slabs):
                if s + 1 < n:
                    low_part(nc, m, dve, s + 1, (s + 1) % 2)
                if kind is None:
                    continue
                nb = 1 if s == 4 else 2
                x = place(s)
                dve.wait_ge(m.sem("squares"), q + 1)
                nc.vector.tensor_reduce(m.r_st[:, 0, 0:10 * nb],
                                        m.r_sq[:, 0:nb * T].rearrange("p (g c) -> p g c", c=HD), AX.X, ALU.add
                                        ).then_inc(m.sem("mean_squares"), 1)
                dve.wait_ge(m.sem("head_std"), q + 1)
                done = order.step(nc.vector.reciprocal(m.r_st[:, 2, 0:10 * nb], m.r_st[:, 1, 0:10 * nb]))
                if q == 0:
                    dve.wait_ge(m.sem("tables"), 8)
                marks = []
                dve.wait_ge(*done)
                for b in range(nb):
                    xb = x[:, b, :, :].rearrange("p t (h c) -> p (t h) c", c=HD)
                    r = m.r_st[:, 2, 10 * b:10 * b + 10].unsqueeze(2).broadcast_to([P, 10, HD])
                    done = order.step(nc.vector.tensor_tensor(xb, xb, r, ALU.mult))
                dve.wait_ge(*done)
                for b in range(nb):
                    xb = x[:, b, :, :].rearrange("p t (h c) -> p t h c", c=HD)
                    tb = m.r_t[:, b * T:(b + 1) * T].rearrange("p (t h c) -> p t h c", h=2, c=HD)
                    sin = m.r_s[:, kind, :, :].unsqueeze(2).broadcast_to([P, TT, 2, HD])
                    done = order.step(nc.vector.tensor_tensor(tb, xb, sin, ALU.mult))
                dve.wait_ge(*done)
                for b in range(nb):
                    xb = x[:, b, :, :].rearrange("p t (h c) -> p t h c", c=HD)
                    cos = m.r_c[:, kind, :, :].unsqueeze(2).broadcast_to([P, TT, 2, HD])
                    done = order.step(nc.vector.tensor_tensor(xb, xb, cos, ALU.mult))
                dve.wait_ge(*done)
                for b in range(nb):
                    xb = x[:, b, :, :].rearrange("p t (g u f) -> p (t g) u f", u=2, f=16)
                    tb = m.r_t[:, b * T:(b + 1) * T].rearrange("p (g u f) -> p g u f", u=2, f=16)[:, :, ::-1, :]
                    ins = nc.vector.tensor_tensor(xb, xb, tb, ALU.add)
                    if s == 4 or b == 0:
                        done = order.step(ins)
                if s == 4:
                    dve.wait_ge(*done)
                    for h in range(2):
                        ins = nc.vector.tensor_copy(m.kv[:, 10, 0:TT, (1 - h) * HD:(2 - h) * HD],
                                                    m.kv[:, 8, 0:TT, h * HD:(h + 1) * HD])
                ins.then_inc(m.sem("normed"), 1)
                dve.wait_ge(m.sem("normed"), q + 1)
                q += 1

        @block.tensor
        def _(pe):
            turn = 0
            for s in range(n):
                pe.wait_ge(m.sem("low_ready"), s + 1)
                for tt in range(TT):
                    g = 5 * s + tt
                    if g >= 6:
                        pe.wait_ge(m.sem("tile_copied"), g - 5)
                    row_tile(nc, m, s % 2, tt, g % 6).then_inc(m.sem("tile_done"), 1)
                    for after, buf, b, tiles, _ in turns[s]:
                        if after == tt:
                            pe.wait_ge(m.sem("normed"), s - 1)
                            if tiles > TT:
                                pe.wait_ge(m.sem("caches"), 6 * 16)
                            if turn:
                                pe.wait_ge(m.sem("turned_copied"), turn)
                            for t in range(tiles):
                                last = nc.tensor.transpose(m.ps[:, 6 + t // 4, (t % 4) * P:(t % 4 + 1) * P],
                                                           buf[:, b, t, :], m.cst[:, K_ID:K_ID + P])
                            last.then_inc(m.sem("turned"), 1)
                            turn += 1


def attention(nc, m, d, L):
    def of_tile(qt):
        gqa = [(qt, h // 2, h % 2, 8 if h // 4 == h % 2 else 10, 9, h // 4 * HD, (h % 2) * HD, None) for h in range(8)]
        diff = [(qt, 4 + h, mp, h, 4 + h, 0, 0, mp) for h in range(4) for mp in range(2)]
        both = gqa + diff
        return [both[j:j + 2] for j in range(0, 16, 2)]

    items = []
    short = of_tile(CTX)
    for qt in range(CTX):
        for j, two in enumerate(of_tile(qt)):
            items += two
            if j % 4 == 1:
                items += short.pop(0)
    units = []
    for i, it in enumerate(items):
        if it[7] != 0:
            units.append(i)

    unit_of = {i: u for u, i in enumerate(units)}

    def keys(qt):
        return [0, 1, 2, 3, TT] if qt < CTX else [CTX]

    def pair(i, n):
        return m.ps[:, 2 * (i % 3):2 * (i % 3) + 2, :].rearrange("p b c -> p (b c)")[:, 0:n * P]

    with m.block() as block:
        @block.tensor
        def _(pe):
            def scores(i):
                qt, qb, half, kb, *_ = items[i]
                j = i - 3
                if j in unit_of:
                    pe.wait_ge(m.sem("p_copied"), unit_of[j] + 1)
                elif j >= 0:
                    pe.wait_ge(m.sem("exp_done"), j + 1)
                h = slice(64 * half, 64 * half + 64)
                q = m.rq[h, qb, qt, :]
                b = 2 * (i % 3)
                if qt < CTX:
                    nc.tensor.matmul(m.ps[:, b, :], q, m.kv[h, kb, 0:4, :].rearrange("p t c -> p (t c)"),
                                     start=True, stop=True)
                    last = nc.tensor.matmul(m.ps[:, b + 1, 0:P], q, m.kv[h, kb, TT, :], start=True, stop=True)
                else:
                    last = nc.tensor.matmul(m.ps[:, b, 0:P], q, m.kv[h, kb, CTX, :], start=True, stop=True)
                last.then_inc(m.sem("scores"), 1)

            def weigh(u):
                i = units[u]
                mp = items[i][7]
                slot = i % 4 if mp is None else (i - 1) % 4
                pe.wait_ge(m.sem("exp_done"), i + 1)
                if mp == 1:
                    pe.wait_ge(m.sem("mixed"), sum(items[j][7] == 1 for j in units[:u + 1]))
                for n in range(len(keys(items[i][0]))):
                    last = nc.tensor.transpose(m.ps[:, 2 * (i % 3) + n // 4, (n % 4) * P:(n % 4 + 1) * P],
                                               m.e[:, slot, n * P:(n + 1) * P], m.cst[:, K_ID:K_ID + P])
                last.then_inc(m.sem("p_turned"), 1)

            def values(u):
                qt, _, _, _, vb, vc, _, mp = items[units[u]]
                ks = keys(qt)
                pe.wait_ge(m.sem("p_copied"), u + 1)
                if u >= 2:
                    pe.wait_ge(m.sem("o_copied"), u - 1)
                w = HD if mp is None else P
                for n, kt in enumerate(ks):
                    last = nc.tensor.matmul(m.ps[:, 6 + u % 2, 0:w], m.eT[:, u % 2, n, :], m.kv[:, vb, kt, vc:vc + w],
                                            start=(n == 0), stop=(n == len(ks) - 1))
                last.then_inc(m.sem("o_done"), 1)

            scores(0)
            scores(1)
            for i in range(len(items)):
                if i + 2 < len(items):
                    scores(i + 2)
                if i in unit_of:
                    weigh(unit_of[i])
                    if unit_of[i] >= 1:
                        values(unit_of[i] - 1)
            values(len(units) - 1)

        @block.scalar
        def _(act):
            def exp(i):
                act.wait_ge(m.sem("maximum"), i + 1)
                n = len(keys(items[i][0]))
                old = [u for u, j in enumerate(units) if j <= i - 4 or (items[j][7] == 1 and j - 1 <= i - 4)]
                if old:
                    act.wait_ge(m.sem("p_turned"), old[-1] + 1)
                nc.scalar.activation(m.e[:, i % 4, 0:n * P], pair(i, n), ACT.Exp, bias=m.a_st[:, i % 32, 0:1],
                                     accum_out=m.a_st[:, i % 32, 1:2]).then_inc(m.sem("exp_done"), 1)

            def copy(u):
                i = units[u]
                n = len(keys(items[i][0]))
                act.wait_ge(m.sem("p_turned"), u + 1)
                if u >= 2:
                    act.wait_ge(m.sem("o_done"), u - 1)
                nc.scalar.activation(m.eT[:, u % 2, 0:n, :].rearrange("p t c -> p (t c)"), pair(i, n), ACT.Copy
                                     ).then_inc(m.sem("p_copied"), 1)

            def square(u):
                qt, qb, *_, mp = items[units[u]]
                if mp == 1:
                    act.wait_ge(m.sem("o_copied"), u + 1)
                    g = (qb - 4) * TT + qt
                    k = sum(items[j][7] == 1 for j in units[:u])
                    if k >= 2:
                        act.wait_ge(m.sem("o_squared"), k - 1)
                    nc.scalar.activation(m.o_sq[:, k % 2, :], m.rq[:, qb, qt, :], ACT.Square, accum_out=m.sml[:, g:g + 1]
                                         ).then_inc(m.sem("o_squared"), 1)

            exp(0)
            for i in range(len(items)):
                if i + 1 < len(items):
                    exp(i + 1)
                if i in unit_of:
                    copy(unit_of[i])
                    if unit_of[i] >= 2:
                        square(unit_of[i] - 2)
            square(len(units) - 2)
            square(len(units) - 1)

        @block.vector
        def _(dve):
            order = Signal(m.sem("dve_order"))

            def maximum(i):
                dve.wait_ge(m.sem("scores"), i + 1)
                nc.vector.tensor_reduce(m.a_st[:, i % 32, 0:1], pair(i, len(keys(items[i][0]))), AX.X, ALU.max,
                                        negate=True).then_inc(m.sem("maximum"), 1)

            def inverse(u):
                i = units[u]
                n = len(keys(items[i][0])) * P
                a = m.a_st[:, i % 32, :]
                dve.wait_ge(m.sem("exp_done"), i + 1)
                done = order.step(nc.vector.reciprocal(a[:, 2:3], a[:, 1:2]))
                if items[i][7] == 1:
                    b = m.a_st[:, (i - 1) % 32, :]
                    dve.wait_ge(*done)
                    done = order.step(nc.vector.scalar_tensor_tensor(out=a[:, 3:4], in0=b[:, 1:2], scalar=m.nlam[:, 0:1],
                                                                     in1=a[:, 2:3], op0=ALU.mult, op1=ALU.mult))
                    dve.wait_ge(*done)
                    nc.vector.scalar_tensor_tensor(out=m.e[:, (i - 1) % 4, 0:n], in0=m.e[:, i % 4, 0:n],
                                                   scalar=a[:, 3:4], in1=m.e[:, (i - 1) % 4, 0:n],
                                                   op0=ALU.mult, op1=ALU.add).then_inc(m.sem("mixed"), 1)
                    done = order.step(nc.vector.reciprocal(a[:, 2:3], b[:, 1:2]))
                return done

            def out(u, done):
                i = units[u]
                qt, qb, half, _, _, _, oc, mp = items[i]
                dve.wait_ge(*done)
                dve.wait_ge(m.sem("o_done"), u + 1)
                if mp is None and half == 0:
                    dve.wait_ge(m.sem("scores"), i + 2)
                w = HD if mp is None else P
                nc.vector.tensor_scalar(m.rq[:, qb, qt, oc:oc + w], m.ps[:, 6 + u % 2, 0:w], m.a_st[:, i % 32, 2:3],
                                        None, ALU.mult).then_inc(m.sem("o_copied"), 1)

            maximum(0)
            maximum(1)
            marks = []
            for i in range(len(items)):
                if i in unit_of:
                    u = unit_of[i]
                    marks.append(inverse(u))
                if i + 2 < len(items):
                    maximum(i + 2)
                if i in unit_of and unit_of[i] >= 1:
                    out(unit_of[i] - 1, marks[unit_of[i] - 1])
            out(len(units) - 1, marks[-1])


def merge(nc, m, d, L):
    rows = [m.rq[:, b, :, :] for b in range(4)] + \
           [m.glr[:, :, b * P:(b + 1) * P] for b in range(4)] + [m.rq[:, 4 + b, :, :] for b in range(4)]
    pairs = KT // 2

    def load(sp, L, dp, i, kind):
        if kind == 0:
            sp.dma_start(m.raw[:, 0, :].rearrange("p (k c) -> p k c", k=KT),
                         k_tiles(d["w_in"], L, C_MG + i * D + dp * W256, W256)).then_inc(m.sem("slab_loaded0"), 16)
        else:
            sp.dma_start(m.raw[:, 1, 0:1024].rearrange("p (k c) -> p k c", k=4),
                         d["w_branch"][ds(L, 1), i, :, ds(dp * W256, W256)].rearrange("a (k p) c -> p (a k) c", p=P)
                         ).then_inc(m.sem("slab_loaded1"), 16)

    with m.block() as block:
        @block.sync
        def _(sp):
            with sp.Fori(0, pairs) as dp:
                for i in range(3):
                    for kind in range(2):
                        sp.wait_ge(m.sem("low_ready"), 6 * dp + 2 * i + kind + 1)
                        load(sp, L, dp, i, kind)

        @block.scalar
        def _(act):
            act.sem_inc(m.sem("gates_ready"), 2)
            nc.scalar.activation(m.sml[:, 20:40], m.sml[:, 0:20], ACT.Sqrt, scale=1.0 / P,
                                 bias=m.cst[:, K_LAM + 4:K_LAM + 5]).then_inc(m.sem("o_std"), 1)
            for t in range(12):
                act.wait_ge(m.sem("turned"), t + 1)
                nc.scalar.activation(halves(m.oH[:, t, :]), m.ps[:, 2 * (t % 4):2 * (t % 4) + 2, 0:HALF], ACT.Copy
                                     ).then_inc(m.sem("turned_high"), 1)

            def high(dp, s):
                slot = s % 2
                act.wait_ge(m.sem(f"slab_loaded{slot}"), dp * 48 + 16 * (s // 2 + 1))
                act.wait_ge(m.sem("tile_done"), dp * 12 + 2 * s + 2)
                n = SLAB if slot == 0 else 1024
                nc.scalar.activation(m.wH[:, slot, 0:n], m.raw[:, slot, 0:n], ACT.Copy).then_inc(m.sem("high_ready"), 1)

            def round_(dp, last):
                for i in range(3):
                    high(dp, 2 * i + 1)
                    for c in range(2):
                        act.wait_ge(m.sem("tile_done"), dp * 12 + 4 * i + c + 1 + 4)
                        act.wait_ge(m.sem("gated"), dp * 6 + 2 * i + c + 1)
                        nc.scalar.activation(halves(m.gate[:, c, :]), m.ps[:, 2 * c:2 * c + 2, 0:HALF], ACT.Sigmoid
                                             ).then_inc(m.sem("gates_ready"), 1)
                    if not (last and i == 2):
                        high(dp, 2 * i + 2)

            high(0, 0)
            with act.Fori(0, pairs - 1) as dp:
                round_(dp, False)
            round_(pairs - 1, True)
            for k in range(KT):
                act.wait_ge(m.sem("mixed"), 6 * (k // 2 + 1))
                if k == 0:
                    act.wait_ge(m.sem("tile_done"), 48 + 4)
                nc.scalar.activation(m.hH[:, k, :], m.mix[:, k, :], ACT.Copy).then_inc(m.sem("mix_high"), 1)

        @block.vector
        def _(dve):
            order = Signal(m.sem("dve_order"))
            dve.sem_inc(m.sem("low_ready"), 2)
            dve.sem_inc(m.sem("gated"), 2)
            dve.wait_ge(m.sem("o_std"), 1)
            done = order.step(nc.vector.reciprocal(m.sml[:, 40:60], m.sml[:, 20:40]))
            dve.wait_ge(*done)
            o = m.rq[:, 4:8, :, :].rearrange("p b t c -> p (b t) c")
            done = order.step(nc.vector.tensor_tensor(o, o, m.sml[:, 40:60].unsqueeze(2).broadcast_to([P, 20, P]), ALU.mult))
            dve.wait_ge(*done)
            nc.vector.tensor_tensor(o, o, m.subn[:, :].unsqueeze(1).broadcast_to([P, 20, P]), ALU.mult
                                    ).then_inc(m.sem("o_normed"), 1)
            for t in range(12):
                dve.wait_ge(m.sem("turned_high"), t + 1)
                nc.vector.tensor_tensor(halves(m.oL[:, t, :]), m.ps[:, 2 * (t % 4):2 * (t % 4) + 2, 0:HALF],
                                        halves(m.oH[:, t, :]).bitcast(F32), ALU.subtract).then_inc(m.sem("turned_low"), 1)
            dve.wait_ge(m.sem("turned_low"), 12)
            done = order.step(nc.vector.memset(m.mix[:, :, :], 0.0))
            dve.wait_ge(*done)

            def low(dp, s):
                slot = s % 2
                n = SLAB if slot == 0 else 1024
                dve.wait_ge(m.sem("high_ready"), dp * 6 + s + 1)
                nc.vector.tensor_tensor(m.wL[:, slot, 0:n], m.raw[:, slot, 0:n], m.wH[:, slot, 0:n].bitcast(F32),
                                        ALU.subtract).then_inc(m.sem("low_ready"), 1)

            def round_(dp, last):
                for i in range(3):
                    low(dp, 2 * i + 1)
                    if not (last and i == 2):
                        low(dp, 2 * i + 2)
                    for c in range(2):
                        dve.wait_ge(m.sem("tile_done"), dp * 12 + 4 * i + 2 + c + 1 + 4)
                        dve.wait_ge(m.sem("gates_ready"), dp * 6 + 2 * i + c + 1 + 2)
                        nc.vector.tensor_tensor(halves(m.gy[:, c, :]), halves(m.gate[:, c, :]),
                                                m.ps[:, 4 + 2 * c:6 + 2 * c, 0:HALF], ALU.mult).then_inc(m.sem("gated"), 1)
                        dve.wait_ge(m.sem("gated"), dp * 6 + 2 * i + c + 1 + 2)
                        mix = m.mix[:, ds(dp * 2 + c, 1), :].rearrange("p a t -> p (a t)")
                        nc.vector.tensor_tensor(mix, mix, m.gy[:, c, :], ALU.add).then_inc(m.sem("mixed"), 1)
                        dve.wait_ge(m.sem("mixed"), dp * 6 + 2 * i + c + 1)

            low(0, 0)
            with dve.Fori(0, pairs - 1) as dp:
                round_(dp, False)
            round_(pairs - 1, True)
            for k in range(KT):
                dve.wait_ge(m.sem("mix_high"), k + 1)
                order.step(nc.vector.tensor_tensor(m.hL[:, k, :], m.mix[:, k, :], m.hH[:, k, :].bitcast(F32),
                                                   ALU.subtract))

        @block.tensor
        def _(pe):
            pe.sem_inc(m.sem("tile_done"), 4)
            for t in range(12):
                if t >= 4:
                    pe.wait_ge(m.sem("turned_low"), t - 3)
                if t == 8:
                    pe.wait_ge(m.sem("o_normed"), 1)
                b = 2 * (t % 4)
                for tt in range(CTX):
                    c = (tt % 2) * P + CH * (tt // 2)
                    nc.tensor.transpose(m.ps[:, b + tt // 2, c:c + P], rows[t][:, tt, :], m.cst[:, K_ID:K_ID + P])
                for h in range(2):
                    r = slice(CH * h, CH * h + CH)
                    c = 256 * (1 - h)
                    last = nc.tensor.transpose(m.ps[:, b + h, c:c + CH], rows[t][r, CTX, :],
                                               m.cst[r, K_ID + CH * h:K_ID + CH * h + CH])
                last.then_inc(m.sem("turned"), 1)
            pe.wait_ge(m.sem("turned_low"), 12)
            with pe.Fori(0, pairs) as dp:
                for i in range(3):
                    pe.wait_ge(m.sem("low_ready"), dp * 6 + 2 * i + 3)
                    for c in range(2):
                        pe.wait_ge(m.sem("gates_ready"), dp * 6 + 2 * i + c + 1)
                        transposed_tile(nc, m, 0, c * P, W256, KT, m.hH, m.hL, 0, c).then_inc(m.sem("tile_done"), 1)
                    pe.wait_ge(m.sem("low_ready"), dp * 6 + 2 * i + 4)
                    for c in range(2):
                        pe.wait_ge(m.sem("gated"), dp * 6 + 2 * i + c + 1)
                        transposed_tile(nc, m, 1, c * P, W256, 4, m.oH, m.oL, 4 * i, 2 + c).then_inc(m.sem("tile_done"), 1)


def add_gated(nc, m, k, gate_col, pair, signal):
    x = m.xT[:, ds(k, 1), :].rearrange("p a t -> p (a t)")
    src = psum_segments(m.ps, pair)
    for c, seg in enumerate(segments(x)):
        g = m.mod[:, ds(k + gate_col, 1), c:c + 1].rearrange("p a b -> p (a b)")
        ins = nc.vector.scalar_tensor_tensor(out=seg, in0=src[c], scalar=g, in1=seg, op0=ALU.mult, op1=ALU.add)
    ins.then_inc(signal, 1)


def project_out(nc, m, d, L, w, gate_col, k0, nk, cols, aH, aL):
    per = cols // P
    slabs = D // cols
    rounds = slabs // 2
    n = nk * cols

    def load(sp, s, slot):
        src = w[ds(L, 1), k0 * P:(k0 + nk) * P, ds(s * cols, cols)].rearrange("a (k p) c -> p (a k) c", p=P)
        sp.dma_start(m.raw[:, slot, 0:n].rearrange("p (k c) -> p k c", k=nk), src
                     ).then_inc(m.sem(f"slab_loaded{slot}"), 16)

    with m.block() as block:
        @block.sync
        def _(sp):
            with sp.Fori(0, rounds) as r:
                for slot in range(2):
                    sp.wait_ge(m.sem("low_ready"), 2 * r + slot + 1)
                    load(sp, 2 * r + slot, slot)

        @block.scalar
        def _(act):
            with act.Fori(0, rounds) as r:
                for slot in range(2):
                    act.wait_ge(m.sem(f"slab_loaded{slot}"), r * 16 + 16)
                    act.wait_ge(m.sem("tile_done"), r * (2 * per) + slot * per + per)
                    nc.scalar.activation(m.wH[:, slot, 0:n], m.raw[:, slot, 0:n], ACT.Copy
                                         ).then_inc(m.sem("high_ready"), 1)

        @block.vector
        def _(dve):
            dve.sem_inc(m.sem("low_ready"), 2)
            dve.sem_inc(m.sem("added"), 4)

            def low(s, slot):
                dve.wait_ge(m.sem("high_ready"), s + 1)
                nc.vector.tensor_tensor(m.wL[:, slot, 0:n], m.raw[:, slot, 0:n], m.wH[:, slot, 0:n].bitcast(F32),
                                        ALU.subtract).then_inc(m.sem("low_ready"), 1)

            def add(s, slot):
                for c in range(per):
                    dve.wait_ge(m.sem("tile_done"), s * per + c + 1 + 2 * per)
                    add_gated(nc, m, s * per + c, gate_col, (slot * per + c) % 4, m.sem("added"))

            low(0, 0)
            with dve.Fori(0, rounds - 1) as r:
                for slot in range(2):
                    low(2 * r + slot + 1, 1 - slot)
                    add(2 * r + slot, slot)
            low(2 * rounds - 1, 1)
            add(2 * rounds - 2, 0)
            add(2 * rounds - 1, 1)

        @block.tensor
        def _(pe):
            pe.sem_inc(m.sem("tile_done"), 2 * per)
            with pe.Fori(0, rounds) as r:
                for slot in range(2):
                    pe.wait_ge(m.sem("low_ready"), 2 * r + slot + 3)
                    for c in range(per):
                        pe.wait_ge(m.sem("added"), r * (2 * per) + slot * per + c + 1 + 4 - 2 * per)
                        transposed_tile(nc, m, slot, c * P, cols, nk, aH, aL, 0, slot * per + c
                                        ).then_inc(m.sem("tile_done"), 1)


def ffn_in(nc, m, d, L, f0, nf):
    rounds = nf // 2

    def load(sp, f, slot):
        raw = m.raw[:, slot, :].rearrange("p (k c) -> p k c", k=KT)
        for part in range(2):
            sp.dma_start(raw[:, :, part * P:(part + 1) * P], k_tiles(d["w_ffn_in"], L, f * P + f0 * P + part * FF, P)
                         ).then_inc(m.sem(f"slab_loaded{slot}"), 16)

    with m.block() as block:
        @block.sync
        def _(sp):
            with sp.Fori(0, rounds) as r:
                for slot in range(2):
                    sp.wait_ge(m.sem("low_ready"), 2 * r + slot + 1)
                    load(sp, 2 * r + slot, slot)

        @block.scalar
        def _(act):
            def high(s, slot):
                act.wait_ge(m.sem(f"slab_loaded{slot}"), s * 16 - slot * 16 + 32)
                act.wait_ge(m.sem("tile_done"), 2 * s + 2)
                nc.scalar.activation(m.wH[:, slot, :], m.raw[:, slot, :], ACT.Copy).then_inc(m.sem("high_ready"), 1)

            def silu(s, slot):
                act.wait_ge(m.sem("tile_done"), 2 * s + 5)
                act.wait_ge(m.sem("multiplied"), s + 1)
                nc.scalar.activation(halves(m.act[:, slot, :]), m.ps[:, 4 * slot:4 * slot + 2, 0:HALF], ACT.Silu
                                     ).then_inc(m.sem("silu"), 1)

            def split(s, slot):
                act.wait_ge(m.sem("multiplied"), s + 3)
                nc.scalar.activation(m.gH[:, ds(s, 1), :].rearrange("p a t -> p (a t)"), m.gf[:, slot, :], ACT.Copy
                                     ).then_inc(m.sem("g_high"), 1)

            def both(s, slot, more=True):
                if more:
                    high(s + 1, 1 - slot)
                silu(s, slot)
                split(s, slot)

            high(0, 0)
            with act.Fori(0, rounds - 1) as r:
                for slot in range(2):
                    both(2 * r + slot, slot)
            both(nf - 2, 0)
            both(nf - 1, 1, False)

        @block.vector
        def _(dve):
            dve.sem_inc(m.sem("low_ready"), 2)
            dve.sem_inc(m.sem("multiplied"), 2)

            def low(s, slot):
                dve.wait_ge(m.sem("high_ready"), s + 1)
                nc.vector.tensor_tensor(m.wL[:, slot, :], m.raw[:, slot, :], m.wH[:, slot, :].bitcast(F32), ALU.subtract
                                        ).then_inc(m.sem("low_ready"), 1)

            def g(s, slot):
                dve.wait_ge(m.sem("silu"), s + 1)
                dve.wait_ge(m.sem("tile_done"), 2 * s + 6)
                nc.vector.tensor_tensor(halves(m.gf[:, slot, :]), halves(m.act[:, slot, :]),
                                        m.ps[:, 4 * slot + 2:4 * slot + 4, 0:HALF], ALU.mult).then_inc(m.sem("multiplied"), 1)
                dve.wait_ge(m.sem("g_high"), s + 1)
                hi = m.gH[:, ds(s, 1), :].rearrange("p a t -> p (a t)").bitcast(F32)
                nc.vector.tensor_tensor(m.gL[:, ds(s, 1), :].rearrange("p a t -> p (a t)"), m.gf[:, slot, :], hi,
                                        ALU.subtract).then_inc(m.sem("g_low"), 1)

            low(0, 0)
            with dve.Fori(0, rounds - 1) as r:
                for slot in range(2):
                    low(2 * r + slot + 1, 1 - slot)
                    g(2 * r + slot, slot)
            low(nf - 1, 1)
            g(nf - 2, 0)
            g(nf - 1, 1)

        @block.tensor
        def _(pe):
            pe.sem_inc(m.sem("tile_done"), 4)
            with pe.Fori(0, rounds) as r:
                for slot in range(2):
                    pe.wait_ge(m.sem("low_ready"), 2 * r + slot + 3)
                    pe.wait_ge(m.sem("multiplied"), 2 * r + slot + 1)
                    for c in range(2):
                        transposed_tile(nc, m, slot, c * P, W256, KT, m.hH, m.hL, 0, 2 * slot + c
                                        ).then_inc(m.sem("tile_done"), 1)


def last_stage(nc, m, d):
    with m.block() as block:
        @block.tensor
        def _(pe):
            for tt in range(TT):
                if tt >= 4:
                    pe.wait_ge(m.sem("copied"), tt - 3)
                for k in range(KT):
                    b = 2 * (tt % 4) + k // 4
                    last = nc.tensor.transpose(m.ps[:, b, (k % 4) * P:(k % 4 + 1) * P], tok(m.xT[:, k, :], tt),
                                               m.cst[:, K_ID:K_ID + P])
                last.then_inc(m.sem("turned"), 1)

        @block.vector
        def _(dve):
            for tt in range(TT):
                dve.wait_ge(m.sem("turned"), tt + 1)
                if tt >= 2:
                    dve.wait_ge(m.sem(f"stored{tt % 2}"), 16 * (tt // 2))
                b = 2 * (tt % 4)
                nc.vector.tensor_copy(m.xrow[:, tt % 2, :], m.ps[:, b:b + 2, :].rearrange("p b c -> p (b c)")
                                      ).then_inc(m.sem("copied"), 1)

        @block.sync
        def _(sp):
            for tt in range(TT):
                sp.wait_ge(m.sem("copied"), tt + 1)
                dst = d["y_sample"][0, tt * P:(tt + 1) * P, :] if tt < CTX else d["y_prompt"][0, :, :]
                sp.dma_start(dst, m.xrow[:, tt % 2, :]).then_inc(m.sem(f"stored{tt % 2}"), 16)
            sp.wait_ge(m.sem("stored0"), 16 * 3)
            sp.wait_ge(m.sem("stored1"), 16 * 2)


def program(nc, d):
    with ExitStack() as ctx:
        m = Stages(nc, ctx)
        first_stage(nc, m, d)
        with nc.Fori(0, DEPTH) as L:
            norm(nc, m, d, L, 0)
            project_gla(nc, m, d, L)
            gla(nc, m, d, L)
            project_attention(nc, m, d, L)
            attention(nc, m, d, L)
            merge(nc, m, d, L)
            project_out(nc, m, d, L, d["w_out"], 16, 0, KT, W256, m.hH, m.hL)
            norm(nc, m, d, L, 1)
            for f0, nf in ((0, 12), (12, 10)):
                ffn_in(nc, m, d, L, f0, nf)
                project_out(nc, m, d, L, d["w_ffn_out"], 40, f0, nf, P, m.gH, m.gL)
        last_stage(nc, m, d)


def constants():
    all_ = np.zeros((P, K_COLS), np.float32)
    all_[:, K_ID:K_ID + P] = np.eye(P)
    all_[:, K_ONE:K_ONE + P] = 1.0 / D
    all_[:, K_LAM + 4] = EPS
    lam = np.array([[-(0.8 - 0.6 * math.exp(-0.3 * l)), 1.0 - (0.8 - 0.6 * math.exp(-0.3 * l))]
                    for l in range(DEPTH)], np.float32)
    g = np.zeros((P, G_COLS), np.float32)
    j, i = np.meshgrid(np.arange(P), np.arange(P), indexing="ij")
    same = j // CH == i // CH
    g[:, G_MF:G_MF + P] = same & (j <= i)
    g[:, G_MB:G_MB + P] = same & (j >= i)
    g[:, G_CM:G_CM + T] = (np.arange(T) % CH != 0)
    t = np.arange(DEC)
    f = np.float32(10000.0) ** (-np.arange(16, dtype=np.float32) / np.float32(16))
    rope = np.zeros((P, 2, TT, HD), np.float32)
    rope[:, 0] = 1.0
    for half, pos in enumerate((t // 64, t % 64)):
        ang = (pos.astype(np.float32)[:, None] * f).reshape(4, P, 16).transpose(1, 0, 2)
        c = half * 32
        rope[:, 0, 0:4, c:c + 16] = rope[:, 0, 0:4, c + 16:c + 32] = np.cos(ang)
        rope[:, 1, 0:4, c:c + 16] = np.sin(ang)
        rope[:, 1, 0:4, c + 16:c + 32] = -np.sin(ang)
    return {"const_all": all_, "const_lam": lam, "const_gla": g, "const_rope": rope}


OUTS = [("y_prompt", (1, SEQ, D)), ("y_sample", (1, DEC, D)), ("new_gqa_k", (1, DEPTH, SEQ, 2, HD)),
        ("new_gqa_v", (1, DEPTH, SEQ, 2, HD)), ("new_state_gla", (1, DEPTH, 2, 4, HD, P)),
        ("new_diff_k", (1, DEPTH, SEQ, 4, 2, HD)), ("new_diff_v", (1, DEPTH, SEQ, 4, P))]


def kernel(**inputs):
    import concourse.bacc as bacc
    from concourse.bass_utils import run_bass_kernel_spmd

    nc = bacc.Bacc("TRN2", target_bir_lowering=False, num_devices=1)
    arrays, d = {}, {}
    for name, a in {**inputs, **constants()}.items():
        a = np.ascontiguousarray(a)
        arrays[f"in_{name}"] = a
        d[name] = nc.dram_tensor(f"in_{name}", a.shape, F32, kind="ExternalInput").ap()
    for name, shape in OUTS:
        d[name] = nc.dram_tensor(f"out_{name}", shape, F32, kind="ExternalOutput").ap()
    program(nc, d)
    r = run_bass_kernel_spmd(nc, [arrays], core_ids=[0])
    return tuple(r.results[0][f"out_{name}"] for name, _ in OUTS)
```

```python
import math
from contextlib import ExitStack, contextmanager

import numpy as np

import concourse.bass as bass
from concourse import mybir

F32 = mybir.dt.float32
F32R = mybir.dt.float32r
I32 = mybir.dt.int32
ACT = mybir.ActivationFunctionType
ALU = mybir.AluOpType
AX = mybir.AxisListType
ds = bass.ds

P = 128
D = 1024
KT = D // P
DEPTH = 2
SEQ, DEC, PAST = 128, 512, 128
TT = (SEQ + DEC) // P
CTX = TT - 1
HALF = 320
TILE_AT = [0, 128, 384, 512, 256]
T = 2 * HALF
HD = 64
BW = 512
RANK = 16
TAU = 16.0
CH = 64
NCH = T // CH
FF = 2816
FT = FF // P
EPS = 1e-6
SLAB = 2048
W256 = 256
C_GQ, C_GK, C_GV, C_LQ, C_LK, C_LV, C_LR, C_LGO, C_DQ, C_DK, C_DV, C_MG = (
    0, 512, 640, 768, 1024, 1280, 1792, 1824, 2336, 2848, 3360, 3872)
K_ID, K_ONE, K_LAM = 0, 128, 258
K_COLS = 264
G_MF, G_MB, G_CM, G_COLS = 0, 128, 256, 256 + T
RING = 10
ROW_BANK = [0, 1, 2, 3, 4, 5, 6, 7, 0, 1]
ROW_BACK = [2, 2, 10, 10, 10, 10, 10, 10, 8, 8]


class Signal:

    def __init__(self, sem):
        self.sem, self.base, self.local = sem, 0, 0

    def step(self, ins, by=1):
        ins.then_inc(self.sem, by)
        self.local += by
        return self.sem, self.base + self.local


@contextmanager
def loop(eng, start, stop, **per_round):
    began = {k: s.base + s.local for k, (s, _) in per_round.items()}
    with eng.Fori(start, stop) as i:
        for k, (s, n) in per_round.items():
            s.base, s.local = began[k] + (i - start) * n, 0
        yield i
        for k, (s, n) in per_round.items():
            assert s.local == n, (k, s.local, n)
    for k, (s, n) in per_round.items():
        s.base, s.local = began[k] + (stop - start) * n, 0


def tok(buf, tt):
    return buf[:, TILE_AT[tt]:TILE_AT[tt] + P]


def chunk_pos(idx):
    return TILE_AT[idx // 2] // CH + idx % 2


def segments(buf):
    step = buf.ap[-1][0]
    assert step == 1
    lat = bass.AP(buf.tensor, buf.offset, [list(buf.ap[0]), [384, 2], [1, 256]])
    return lat, buf[:, 256:384].rearrange("p (h c) -> p h c", h=2)


def psum_segments(ps, pair):
    base = ps[:, 2 * pair, :]
    return [bass.AP(base.tensor, base.offset + at, [list(base.ap[0]), [step, 2], [1, n]])
            for at, step, n in ((0, 576, 256), (256, 256, CH))]


class Stages:

    def __init__(self, nc, ctx):
        self.nc, self.ctx, self.sems = nc, ctx, {}
        at = self.at
        self.xT = at("xT", [P, KT, T], 0)
        self.hH = at("hH", [P, KT, T], 20480, F32R)
        self.hL = at("hL", [P, KT, T], 40960, F32R)
        self.raw = at("raw", [P, 2, SLAB], 61440)
        self.wH = at("wH", [P, 2, SLAB], 77824, F32R)
        self.wL = at("wL", [P, 2, SLAB], 94208, F32R)
        x0, x1 = 110592, 110592 + 61440
        small = [x1 + 30720]

        def place(name, shape):
            t = at(name, shape, small[0])
            small[0] += -(-4 * int(np.prod(shape[1:])) // 32) * 32
            return t

        self.cst = place("cst", [P, K_COLS])
        self.sc = place("sc", [P, KT, 2])
        self.mod = place("mod", [P, 48, 2])
        self.aff = place("aff", [P, 2, KT, 2])
        self.nw = place("nw", [P, 2, KT])
        self.nlam = place("nlam", [P, 4])
        self.lp = place("lp", [P, 4 * HD])
        self.gains = place("gains", [P, 4, HD])
        self.subn = place("subn", [P, P])
        self.lpw = place("lpw", [P, 2, HD])
        self.mb = place("mb", [P, 48])
        self.sml = place("sml", [P, 160])
        self.modw = [at(f"modw{j}", [P, KT, W256], 61440 + (0, 8192, 32768, 40960)[j]) for j in range(4)]
        self.mrow = at("mrow", [2, 4, 512], 77824 + 8192)
        self.mbr = at("mbr", [48, P], x0 + 30720)
        self.sq = at("sq", [P, 2, T], x0)
        self.std = at("std", [P, T], x0 + 5120)
        self.rstd = at("rstd", [P, T], x0 + 7680)
        self.xn = at("xn", [P, 4, T], x0 + 10240)
        self.hf = at("hf", [P, 4, T], x0 + 20480)
        self.xrow = at("xrow", [P, 2, D], x0)
        self.lv = at("lv", [P, TT, BW], x0)
        self.lg = at("lg", [P, TT, BW], x0 + 10240)
        self.lT = at("lT", [P, 5, T], x0 + 20480)
        g = x0 + 33280
        self.g_min, self.g_abs, self.g_sp, self.g_la, self.g_cum, self.g_eq, self.g_ek = [
            at(name, [P, T], g + 2560 * n)
            for n, name in enumerate(("g_min", "g_abs", "g_sp", "g_la", "g_cum", "g_eq", "g_ek"))]
        g = x1
        self.g_qd = at("g_qd", [P, T], x0 + 33280 + 17920)
        self.g_ki = at("g_ki", [P, T], x0 + 33280 + 20480)
        self.g_ke = at("g_ke", [P, T], x0 + 33280 + 23040)
        self.g_ker = at("g_ker", [P, TT, P], g)
        self.g_s = at("g_s", [P, NCH, P], g + 2560)
        self.g_sf = at("g_sf", [P, P], g + 7680)
        self.g_am = at("g_am", [P, 2, 2, 2, P], g + 8192)
        self.g_au = at("g_au", [32, 2, 256], g + 12288)
        self.g_cst = at("g_cst", [P, G_COLS], g + 14336)
        self.g_on = at("g_on", [P, P], g + 17920)
        self.g_ab = at("g_ab", [P, 2, 2], g + 18432)
        self.g_dec = at("g_dec", [P, NCH], g + 18464)
        self.g_st = at("g_st", [P, 80], g + 18528)
        self.g_sq = place("g_sq", [P, 2, P])
        self.rq = at("rq", [P, 8, TT, P], x1)
        self.glr = at("glr", [P, TT, BW], x1 + 20480)
        self.kv = at("kv", [P, 11, TT + 1, P], x0)
        a = x0 + 33792
        self.r_sq = at("r_sq", [P, 2 * T], a)
        self.r_t = at("r_t", [P, 2 * T], a + 5120)
        self.r_c = at("r_c", [P, 4, TT, HD], a + 10240)
        self.r_s = at("r_s", [P, 4, TT, HD], a + 15360)
        self.r_tab = at("r_tab", [P, 2, TT, HD], a + 20480)
        self.r_st = at("r_st", [P, 4, 20], a + 23040)
        self.e = at("e", [P, 4, T], a)
        self.eT = at("eT", [P, 2, TT, P], a + 10240)
        self.a_st = at("a_st", [P, 32, 8], a + 15360)
        self.o_sq = at("o_sq", [P, 2, 2, P], a + 16384)
        self.a_q = at("a_q", [P, 4, 16], a + 18432)
        self.oH = at("oH", [P, 12, T], x0, F32R)
        self.oL = at("oL", [P, 12, T], x0 + 30720, F32R)
        self.mix = at("mix", [P, KT, T], x1)
        self.gate = at("gate", [P, 2, T], x1 + 20480)
        self.gy = at("gy", [P, 2, T], x1 + 25600)
        self.gH = at("gH", [P, 12, T], x0, F32R)
        self.gL = at("gL", [P, 12, T], x0 + 30720, F32R)
        self.act = at("act", [P, 2, T], x1)
        self.gf = at("gf", [P, 2, T], x1 + 5120)
        assert small[0] + 16512 <= 229344
        self.ps = ctx.enter_context(nc.psum_tensor("ps", [P, 8, 512], F32))

    def at(self, name, shape, offset, dt=F32):
        return self.nc.alloc_sbuf_tensor_at(name, shape, dt, offset=16512 + offset)

    def sem(self, name):
        if name not in self.sems:
            self.sems[name] = self.ctx.enter_context(self.nc.semaphore(name))
        return self.sems[name]

    @contextmanager
    def block(self):
        with self.nc.Block() as block:
            yield block
        nums = [s.num for s in self.sems.values()]
        self.nc.gpsimd.sem_clear(range(min(nums), max(nums) + 1))
        self.nc.all_engine_barrier()


def flat(ap):
    return ap.rearrange("p h c -> p (h c)")


def halves(ap):
    return ap.rearrange("p (h c) -> p h c", h=2)


def high_part(nc, m, act, slot, loaded, used=None):
    act.wait_ge(m.sem(f"slab_loaded{slot}"), loaded)
    if used is not None:
        act.wait_ge(*used)
    nc.scalar.activation(m.wH[:, slot, :], m.raw[:, slot, :], ACT.Copy).then_inc(m.sem("high_ready"), 1)


def low_part(nc, m, dve, s, slot):
    dve.wait_ge(m.sem("high_ready"), s + 1)
    nc.vector.tensor_tensor(m.wL[:, slot, :], m.raw[:, slot, :], m.wH[:, slot, :].bitcast(F32),
                            ALU.subtract).then_inc(m.sem("low_ready"), 1)


def next_load(sp, m, nxt, j, *free):
    if free:
        sp.wait_ge(m.sem(free[0]), free[1])
    nxt[1](sp, j, m.sem(f"next_loaded{j}"))


def next_loaded(sp, m, nxt):
    sp.wait_ge(m.sem("next_loaded0"), nxt[2])
    sp.wait_ge(m.sem("next_loaded1"), nxt[2])


def next_high(nc, m, act, nxt, *used):
    act.wait_ge(m.sem("next_loaded0"), nxt[2])
    if used:
        act.wait_ge(m.sem(used[0]), used[1])
    nc.scalar.activation(m.wH[:, 0, 0:nxt[0]], m.raw[:, 0, 0:nxt[0]], ACT.Copy).then_inc(m.sem("next_high"), 1)


def next_low(engine, m, eng, nxt):
    eng.wait_ge(m.sem("next_high"), 1)
    engine.tensor_tensor(m.wL[:, 0, 0:nxt[0]], m.raw[:, 0, 0:nxt[0]], m.wH[:, 0, 0:nxt[0]].bitcast(F32),
                            ALU.subtract).then_inc(m.sem("next_low"), 1)


def took_loads(sp, m, by=16):
    for slot in range(2):
        sp.sem_inc(m.sem(f"slab_loaded{slot}"), by)


def load_w_in(sp, m, d, L, c, slot, sem):
    sp.dma_start(m.raw[:, slot, :].rearrange("p (k c) -> p k c", k=KT), k_tiles(d["w_in"], L, c, W256)).then_inc(sem, 16)


def load_out(sp, m, w, L, s, k0, nk, cols, slot, sem):
    src = w[ds(L, 1), k0 * P:(k0 + nk) * P, ds(s * cols, cols)].rearrange("a (k p) c -> p (a k) c", p=P)
    sp.dma_start(m.raw[:, slot, 0:nk * cols].rearrange("p (k c) -> p k c", k=nk), src).then_inc(sem, 16)


def load_merge(sp, m, d, L, dp, i, kind, sem):
    if kind == 0:
        load_w_in(sp, m, d, L, C_MG + i * D + dp * W256, 0, sem)
    else:
        sp.dma_start(m.raw[:, 1, 0:1024].rearrange("p (k c) -> p k c", k=4),
                     d["w_branch"][ds(L, 1), i, :, ds(dp * W256, W256)].rearrange("a (k p) c -> p (a k) c", p=P)
                     ).then_inc(sem, 16)


def load_ffn(sp, m, d, L, f0, f, slot, sem):
    raw = m.raw[:, slot, :].rearrange("p (k c) -> p k c", k=KT)
    for part in range(2):
        sp.dma_start(raw[:, :, part * P:(part + 1) * P], k_tiles(d["w_ffn_in"], L, f * P + f0 * P + part * FF, P)
                     ).then_inc(sem, 16)


def transposed_tile(nc, m, slot, col, cols, nk, aH, aL, k0, pair, ks=None):
    wh = m.wH[:, slot, 0:nk * cols].rearrange("p (k c) -> p k c", k=nk)
    wl = m.wL[:, slot, 0:nk * cols].rearrange("p (k c) -> p k c", k=nk)
    for k in ks or range(nk):
        for q, (w, a) in enumerate(((wl, aH), (wh, aL), (wh, aH))):
            for n in range(2):
                last = nc.tensor.matmul(m.ps[:, 2 * pair + n, 0:HALF], w[:, k, col:col + P],
                                        a[:, k0 + k, n * HALF:(n + 1) * HALF],
                                        start=(k == 0 and q == 0), stop=(k == nk - 1 and q == 2))
    return last


def row_tile(nc, m, slot, tt, bank):
    wh = m.wH[:, slot, :].rearrange("p (k c) -> p k c", k=KT)
    wl = m.wL[:, slot, :].rearrange("p (k c) -> p k c", k=KT)
    for k in range(KT):
        for q, (a, w) in enumerate(((m.hL, wh), (m.hH, wl), (m.hH, wh))):
            last = nc.tensor.matmul(m.ps[:, bank, 0:W256], tok(a[:, k, :], tt), w[:, k, :],
                                    start=(k == 0 and q == 0), stop=(k == KT - 1 and q == 2))
    return last


def k_tiles(w, L, c0, n):
    return w[ds(L, 1), :, ds(c0, n)].rearrange("a (k p) c -> p (a k) c", p=P)


def first_stage(nc, m, d):
    with m.block() as block:
        @block.sync
        def _(sp):
            sp.dma_start(m.cst[:, :], d["const_all"]).then_inc(m.sem("constants"), 16)
            for tt in range(TT):
                if tt >= 2:
                    sp.wait_ge(m.sem("row_turned"), tt - 1)
                src = d["x_sample"][0, tt * P:(tt + 1) * P, :] if tt < CTX else d["x_prompt"][0, :, :]
                sp.dma_start(m.xrow[:, tt % 2, :], src).then_inc(m.sem(f"row{tt % 2}"), 16)

        @block.scalar
        def _(act):
            act.dma_start(m.sc[:, :, 0:1], d["c"].rearrange("a (k p) -> p k a", p=P),
                          allow_slow_non_contiguous=True).then_inc(m.sem("cond"), 16)
            act.dma_start(m.sc[:, :, 1:2], d["c_ctx"].rearrange("(a k p) -> p k a", p=P, a=1),
                          allow_slow_non_contiguous=True).then_inc(m.sem("cond"), 16)
            act.wait_ge(m.sem("cond"), 32)
            nc.scalar.activation(m.sc[:, :, :], m.sc[:, :, :], ACT.Silu).then_inc(m.sem("silu"), 1)

        @block.tensor
        def _(pe):
            pe.wait_ge(m.sem("constants"), 16)
            for tt in range(TT):
                pe.wait_ge(m.sem(f"row{tt % 2}"), 16 * (tt // 2 + 1))
                if tt >= 4:
                    pe.wait_ge(m.sem("copied"), tt - 3)
                for k in range(KT):
                    b = 2 * (tt % 4) + k // 4
                    last = nc.tensor.transpose(m.ps[:, b, (k % 4) * P:(k % 4 + 1) * P],
                                               m.xrow[:, tt % 2, k * P:(k + 1) * P], m.cst[:, K_ID:K_ID + P])
                last.then_inc(m.sem("row_turned"), 1)

        @block.vector
        def _(dve):
            for tt in range(TT):
                dve.wait_ge(m.sem("row_turned"), tt + 1)
                b = 2 * (tt % 4)
                src = m.ps[:, b:b + 2, :].rearrange("p b (k c) -> p (b k) c", k=4)
                nc.vector.tensor_copy(m.xT[:, :, TILE_AT[tt]:TILE_AT[tt] + P], src).then_inc(m.sem("copied"), 1)


def load_mod(sp, m, d, L, s):
    sp.dma_start(m.modw[s % 4][:, :, :], k_tiles(d["w_mod"], L, s * W256, W256)).then_inc(m.sem(f"mod_loaded{s % 4}"), 16)


def mod_slab(nc, pe, m, s, loaded, bank):
    pe.wait_ge(m.sem(f"mod_loaded{s % 4}"), 16 * loaded)
    for k in range(KT):
        last = nc.tensor.matmul(m.ps[0:2, bank, (s % 2) * W256:(s % 2 + 1) * W256], m.sc[:, k, :],
                                m.modw[s % 4][:, k, :], start=(k == 0), stop=(k == KT - 1))
    return last


def mod_rows(nc, m, b, bank):
    return nc.scalar.activation(m.mrow[:, b:b + 2, :], m.ps[0:2, bank:bank + 2, :], ACT.Copy)


def turn_mod(nc, m, n, bank):
    for t in range(n):
        last = nc.tensor.transpose(m.ps[:, bank, 2 * t:2 * t + 2], m.mrow[:, t // 4, (t % 4) * P:(t % 4 + 1) * P],
                                   m.cst[0:2, K_ID:K_ID + 2])
    return last


def add_mod_bias(nc, m, bank, t, n):
    return nc.vector.tensor_tensor(m.mod[:, t:t + n, :], m.ps[:, bank, 0:2 * n].rearrange("p (t c) -> p t c", c=2),
                                   m.mb[:, t:t + n].unsqueeze(2).broadcast_to([P, n, 2]), ALU.add)


def affine(nc, m, dve, order, n):
    first = (8, 32)[n]
    done = order.step(nc.vector.tensor_scalar(m.aff[:, n, :, :], m.mod[:, first:first + KT, :], 1.0, None, ALU.add))
    dve.wait_ge(*done)
    return nc.vector.tensor_tensor(m.aff[:, n, :, :], m.aff[:, n, :, :],
                                   m.nw[:, n, :].unsqueeze(2).broadcast_to([P, KT, 2]), ALU.mult)


def norm(nc, m, d, L, which, nxt):
    shift = (0, 24)[which]
    first = which == 0
    with m.block() as block:
        @block.sync
        def _(sp):
            if first:
                for s in range(8):
                    if s >= 4:
                        sp.wait_ge(m.sem("slab_used"), s - 3)
                    load_mod(sp, m, d, L, s)
            for j in range(2):
                next_load(sp, m, nxt, j, *(("slab_used", 5 + j) if first else ()))
            next_loaded(sp, m, nxt)

        @block.gpsimd
        def _(pool):
            next_low(nc.gpsimd, m, pool, nxt)

        @block.scalar
        def _(act):
            if first:
                small = m.sem("small_params")
                act.dma_start(m.mbr[:, :], d["b_mod"][ds(L, 1), :].rearrange("a (t c) -> (a t) c", c=P)
                              ).then_inc(m.sem("bias_rows"), 16)
                act.dma_start(m.lp[:, :], d["diff_lambda"][ds(L, 1), :, :].rearrange("a b c -> (a b c)").
                              partition_broadcast(P)).then_inc(small, 16)
                act.dma_start(m.nlam[:, 0:2], d["const_lam"][ds(L, 1), :].rearrange("a c -> (a c)").
                              partition_broadcast(P)).then_inc(small, 16)
                for n, name in enumerate(("gqa_q_norm", "diff_q_norm", "gqa_k_norm", "diff_k_norm")):
                    act.dma_start(m.gains[:, n, :], d[name][ds(L, 1), :].rearrange("a c -> (a c)").
                                  partition_broadcast(P)).then_inc(small, 16)
                act.dma_start(m.subn[:, :], d["diff_sub_norm"][ds(L, 1), :].rearrange("a c -> (a c)").
                              partition_broadcast(P)).then_inc(small, 16)
                for n, name in enumerate(("norm1", "norm2")):
                    act.dma_start(m.nw[:, n, :], d[name][ds(L, 1), :].rearrange("a (k p) -> p (a k)", p=P),
                                  allow_slow_non_contiguous=True).then_inc(small, 16)
            for k in range(KT):
                if k >= 2:
                    act.wait_ge(m.sem("summed"), k - 1)
                nc.scalar.activation(m.sq[:, k % 2, :], m.xT[:, k, :], ACT.Square).then_inc(m.sem("squares"), 1)
                if first and k == 1:
                    act.wait_ge(m.sem("lam_sums"), 2)
                    nc.scalar.activation(m.nlam[:, 2:4], m.nlam[:, 2:4], ACT.Exp).then_inc(m.sem("lam_exp"), 1)
                if first and k == 5:
                    act.wait_ge(m.sem("slab_used"), 4)
                    mod_rows(nc, m, 0, 3).then_inc(m.sem("mod_rows"), 1)
            if first:
                act.wait_ge(m.sem("slab_used"), 8)
                mod_rows(nc, m, 2, 5).then_inc(m.sem("mod_rows"), 1)
            act.wait_ge(m.sem("summed"), KT)
            nc.scalar.activation(halves(m.std[:, :]), m.ps[:, 0:2, 0:HALF], ACT.Sqrt,
                                 bias=m.cst[:, K_LAM + 4:K_LAM + 5]).then_inc(m.sem("std"), 1)
            if first:
                act.wait_ge(m.sem("mod_ready"), 1)
            next_high(nc, m, act, nxt)
            for k in range(KT + 1):
                if k < KT:
                    act.wait_ge(m.sem("normed"), k + 1)
                    if k >= 4:
                        act.wait_ge(m.sem("low"), k - 3)
                    for c, (o, i) in enumerate(zip(segments(m.hf[:, k % 4, :]), segments(m.xn[:, k % 4, :]))):
                        ins = nc.scalar.activation(o, i, ACT.Identity, bias=m.mod[:, shift + k, c:c + 1],
                                                   scale=m.aff[:, which, k, c:c + 1])
                    ins.then_inc(m.sem("shifted"), 1)
                if k >= 1:
                    act.wait_ge(m.sem("shifted"), k)
                    nc.scalar.activation(m.hH[:, k - 1, :], m.hf[:, (k - 1) % 4, :], ACT.Copy
                                         ).then_inc(m.sem("high"), 1)

        @block.tensor
        def _(pe):
            if first:
                pe.wait_ge(m.sem("bias_rows"), 16)
                nc.tensor.transpose(m.ps[:, 2, 0:48], m.mbr[:, :], m.cst[0:48, K_ID:K_ID + 48]
                                    ).then_inc(m.sem("bias_turned"), 1)
            for k in range(KT):
                if first:
                    mod_slab(nc, pe, m, k, k // 4 + 1, 3 + k // 2).then_inc(m.sem("slab_used"), 1)
                pe.wait_ge(m.sem("squares"), k + 1)
                for n in range(2):
                    last = nc.tensor.matmul(m.ps[:, n, 0:HALF], m.cst[:, K_ONE:K_ONE + P],
                                            m.sq[:, k % 2, n * HALF:(n + 1) * HALF], start=(k == 0), stop=(k == KT - 1))
                last.then_inc(m.sem("summed"), 1)
            if first:
                pe.wait_ge(m.sem("mod_rows"), 2)
                turn_mod(nc, m, 16, 7).then_inc(m.sem("mod_turned"), 1)

        @block.vector
        def _(dve):
            if first:
                order = Signal(m.sem("dve_order"))
                dve.wait_ge(m.sem("small_params"), 9 * 16)
                lp = m.lp[:, :].rearrange("p (a b c) -> p a b c", a=2, b=2)
                done = order.step(nc.vector.tensor_tensor(m.lpw[:, :, :], lp[:, :, 0, :], lp[:, :, 1, :], ALU.mult))
                dve.wait_ge(*done)
                nc.vector.tensor_reduce(m.nlam[:, 2:4], m.lpw[:, :, :], AX.X, ALU.add).then_inc(m.sem("lam_sums"), 2)
                dve.wait_ge(m.sem("lam_exp"), 1)
                done = order.step(nc.vector.tensor_tensor(m.nlam[:, 2:3], m.nlam[:, 3:4], m.nlam[:, 2:3], ALU.subtract))
                dve.wait_ge(*done)
                order.step(nc.vector.tensor_tensor(m.nlam[:, 0:1], m.nlam[:, 2:3], m.nlam[:, 0:1], ALU.add))
                order.step(nc.vector.tensor_scalar(m.subn[:, :], m.subn[:, :], m.nlam[:, 1:2], None, ALU.mult))
                dve.wait_ge(m.sem("bias_turned"), 1)
                done = order.step(nc.vector.tensor_copy(m.mb[:, :], m.ps[:, 2, 0:48]))
                dve.wait_ge(*done)
                dve.wait_ge(m.sem("mod_turned"), 1)
                done = order.step(add_mod_bias(nc, m, 7, 0, 16))
                dve.wait_ge(*done)
                affine(nc, m, dve, order, 0).then_inc(m.sem("mod_ready"), 1)
            dve.wait_ge(m.sem("std"), 1)
            nc.vector.reciprocal(m.rstd[:, :], m.std[:, :]).then_inc(m.sem("rstd"), 1)
            dve.wait_ge(m.sem("rstd"), 1)
            for k in range(KT + 2):
                if k < KT:
                    if k >= 4:
                        dve.wait_ge(m.sem("shifted"), k - 3)
                    nc.vector.tensor_tensor(m.xn[:, k % 4, :], m.xT[:, k, :], m.rstd[:, :], ALU.mult
                                            ).then_inc(m.sem("normed"), 1)
                if k >= 2:
                    dve.wait_ge(m.sem("high"), k - 1)
                    nc.vector.tensor_tensor(m.hL[:, k - 2, :], m.hf[:, (k - 2) % 4, :],
                                            m.hH[:, k - 2, :].bitcast(F32), ALU.subtract).then_inc(m.sem("low"), 1)


def project_gla(nc, m, d, L):
    cols = [C_LV, C_LV + 256, C_LGO, C_LGO + 256, C_LQ, C_LK, C_LR]
    rows, n = 4, len(cols)
    tiles = {4: (0, 1), 5: (0, 1), 6: (0,)}
    done_after = [5, 10, 15, 20, 22, 24, 25]
    with m.block() as block:
        @block.gpsimd
        def _(pool):
            pool.memset(m.g_au[:, :, :], 0.0).then_inc(m.sem("au_zero"), 1)
            pool.memset(m.g_am[:, :, :, :, :], 0.0).then_inc(m.sem("am_zero"), 1)

        @block.sync
        def _(sp):
            took_loads(sp, m)
            for s in range(2, n):
                sp.wait_ge(m.sem("low_ready"), s - 1)
                load_w_in(sp, m, d, L, cols[s], s % 2, m.sem(f"slab_loaded{s % 2}"))
            ld = m.sem("gla_params")
            sp.dma_start(m.g_cst[:, :], d["const_gla"]).then_inc(ld, 16)
            sp.wait_ge(m.sem("au_zero"), 1)
            for z in range(2):
                sp.dma_start(m.g_au[RANK * z:RANK * (z + 1), z, :],
                             d["gla_alpha_up"][ds(L, 1), z, :, :].rearrange("a r c -> (a r) c")).then_inc(ld, 16)
            sp.dma_start(m.g_on[:, :], d["gla_out_norm"][ds(L, 1), :].rearrange("a c -> (a c)").
                         partition_broadcast(P)).then_inc(ld, 16)
            for z in range(2):
                sp.dma_start(m.g_ab[:, z, :], d["gla_alpha_bias"][ds(L, 1), z, :].rearrange("a (h p) -> p (a h)", p=P),
                             allow_slow_non_contiguous=True).then_inc(ld, 16)
            sp.wait_ge(ld, 6 * 16)

        @block.scalar
        def _(act):
            def high(s):
                high_part(nc, m, act, s % 2, 16 * (s // 2 + 1), (m.sem("tile_done"), done_after[s - 2]) if s > 1 else None)

            act.sem_inc(m.sem("high_ready"), 1)
            for s in range(n):
                if s + 1 < n:
                    high(s + 1)
                if s < rows:
                    dst = m.lv if s < 2 else m.lg
                    for tt in range(TT):
                        act.wait_ge(m.sem("tile_done"), 5 * s + tt + 1)
                        nc.scalar.activation(dst[:, tt, (s % 2) * 256:(s % 2 + 1) * 256],
                                             m.ps[:, ROW_BANK[(5 * s + tt) % RING], 0:256], ACT.Copy
                                             ).then_inc(m.sem("tile_copied"), 1)
                else:
                    for col in tiles[s]:
                        t = 2 * (s - rows) + col
                        act.wait_ge(m.sem("tile_done"), 20 + t + 1)
                        nc.scalar.activation(halves(m.lT[:, t, :]), m.ps[:, 2 * (t % 4):2 * (t % 4) + 2, 0:HALF],
                                             ACT.Copy, scale=(HD ** -0.5 if t < 2 else 1.0)
                                             ).then_inc(m.sem("tile_copied"), 1)

        @block.vector
        def _(dve):
            dve.sem_inc(m.sem("low_ready"), 1)
            for s in range(1, n):
                low_part(nc, m, dve, s, s % 2)

        @block.tensor
        def _(pe):
            for s in range(n):
                pe.wait_ge(m.sem("low_ready"), s + 1)
                if s < rows:
                    for tt in range(TT):
                        g = 5 * s + tt
                        back = ROW_BACK[g % RING]
                        if g >= back:
                            pe.wait_ge(m.sem("tile_copied"), g - back + 1)
                        row_tile(nc, m, s % 2, tt, ROW_BANK[g % RING]).then_inc(m.sem("tile_done"), 1)
                else:
                    for col in tiles[s]:
                        t = 2 * (s - rows) + col
                        pe.wait_ge(m.sem("tile_copied"), 20 if t < 4 else 20 + t - 3)
                        transposed_tile(nc, m, s % 2, col * P, W256, KT, m.hH, m.hL, 0, t % 4
                                        ).then_inc(m.sem("tile_done"), 1)


def gla(nc, m, d, L, nxt):
    units = [(hp, dr) for hp in range(2) for dr in range(2)]
    def ds_at(idx, rows=slice(0, P)):
        tt, half = idx // 2, idx % 2
        return m.ps[rows, (2, 0)[half] + tt // 4, (tt % 4) * P:(tt % 4 + 1) * P]

    with m.block() as block:
        @block.sync
        def _(sp):
            for u, (hp, dr) in enumerate(units):
                for j in range(4):
                    if u:
                        sp.wait_ge(m.sem("slab_used"), 4 * u - 3 + j)
                    load_mod(sp, m, d, L, 8 + 4 * u + j)
                if u:
                    sp.wait_ge(m.sem("o_done"), 5 * u)
                sp.dma_start(m.g_s[:, (0, 7)[dr], :],
                             d["state_gla"][0, ds(L, 1), dr, 2 * hp:2 * hp + 2, :, :].
                             rearrange("a h k e -> (a h k) e")).then_inc(m.sem("state_in"), 16)
                if u == 3:
                    for j in range(2):
                        next_load(sp, m, nxt, j, "slab_used", 13 + j)
                sp.wait_ge(m.sem("state_done"), u + 1)
                sp.dma_start(d["new_state_gla"][0, ds(L, 1), dr, 2 * hp:2 * hp + 2, :, :].
                             rearrange("a h k e -> (a h k) e"), m.g_sf[:, :]).then_inc(m.sem("state_out"), 16)
            next_loaded(sp, m, nxt)
            sp.wait_ge(m.sem("state_out"), 16 * len(units))

        @block.scalar
        def _(act):
            order = Signal(m.sem("act_order"))
            done = order.step(nc.scalar.activation(m.lg[:, :, :], m.lg[:, :, :], ACT.Silu))

            def gates(u):
                hp, dr = units[u]
                last = slice(CH - 1, CH) if dr == 0 else slice(0, 1)
                act.wait_ge(m.sem("z_min"), u + 1)
                done = order.step(nc.scalar.activation(halves(m.g_abs[:, :]), m.ps[:, 0:2, 0:HALF], ACT.Abs,
                                                       bias=m.g_ab[:, dr, hp:hp + 1]))
                act.wait_ge(*done)
                done = order.step(nc.scalar.activation(m.g_abs[:, :], m.g_abs[:, :], ACT.Exp, scale=-1.0))
                act.wait_ge(*done)
                nc.scalar.activation(m.g_sp[:, :], m.g_abs[:, :], ACT.Ln, bias=1.0).then_inc(m.sem("softplus"), 1)
                act.wait_ge(m.sem("cum_done"), u + 1)
                if u:
                    act.wait_ge(m.sem("q_decayed"), u)
                    act.wait_ge(m.sem("k_end"), u)
                    act.wait_ge(m.sem("state_done"), u)
                nc.scalar.activation(m.g_eq[:, :], m.g_cum[:, :], ACT.Exp, scale=1.0 / TAU).then_inc(m.sem("exp_q"), 1)
                nc.scalar.activation(m.g_ek[:, :], m.g_cum[:, :], ACT.Exp, scale=-1.0 / TAU).then_inc(m.sem("exp_k"), 1)
                nc.scalar.activation(m.g_dec[:, :], m.g_cum[:, :].rearrange("p (c t) -> p c t", t=CH)[:, :, last].
                                     rearrange("p c t -> p (c t)"), ACT.Exp, scale=1.0 / TAU).then_inc(m.sem("decay"), 1)
                act.wait_ge(m.sem("to_end"), u + 1)
                nc.scalar.activation(m.g_min[:, :], m.g_la[:, :], ACT.Exp, scale=1.0 / TAU).then_inc(m.sem("exp_end"), 1)

            gates(0)
            for u, (hp, dr) in enumerate(units):
                act.wait_ge(m.sem("ke_turned"), u + 1)
                if u:
                    act.wait_ge(m.sem("ds_done"), u)
                nc.scalar.activation(m.g_ker[:, 0:4, :].rearrange("p t c -> p (t c)"), m.ps[:, 0, :], ACT.Copy)
                nc.scalar.activation(m.g_ker[:, 4, :], m.ps[:, 1, 0:P], ACT.Copy).then_inc(m.sem("ke_rows"), 1)
                act.wait_ge(m.sem("slab_used"), 4 * u + 4)
                mod_rows(nc, m, 0, 4).then_inc(m.sem("mod_rows"), 1)
                if u < 3:
                    gates(u + 1)
                else:
                    next_high(nc, m, act, nxt)
                if dr == 1:
                    for tt in range(TT):
                        act.wait_ge(m.sem("o_summed"), 5 * u + tt + 1)
                        for hh in range(2):
                            g = 10 * hp + 2 * tt + hh
                            done = order.step(nc.scalar.activation(
                                m.g_sq[:, hh, :], m.glr[:, tt, (2 * hp + hh) * P:(2 * hp + hh + 1) * P], ACT.Square,
                                accum_out=m.g_st[:, g:g + 1]))
                        act.wait_ge(*done)
                    half = slice(10 * hp, 10 * hp + 10)
                    nc.scalar.activation(m.g_st[:, 20:40][:, half], m.g_st[:, half], ACT.Sqrt, scale=1.0 / P,
                                         bias=m.cst[:, K_LAM + 4:K_LAM + 5]).then_inc(m.sem("o_std"), 1)

        @block.tensor
        def _(pe):
            def z(u):
                hp, dr = units[u]
                for n in range(2):
                    last = nc.tensor.matmul(m.ps[:, n, 0:HALF], m.g_au[0:32, dr, hp * P:(hp + 1) * P],
                                            m.lT[0:32, 4, n * HALF:(n + 1) * HALF], start=True, stop=True)
                last.then_inc(m.sem("z_done"), 1)

            z(0)
            for u, (hp, dr) in enumerate(units):
                if u:
                    pe.wait_ge(m.sem("o_summed"), 5 * u)
                for j in range(3):
                    mod_slab(nc, pe, m, j, u + 1, 4 + j // 2).then_inc(m.sem("slab_used"), 1)
                pe.wait_ge(m.sem("k_end"), u + 1)
                for tt in range(TT):
                    last = nc.tensor.transpose(m.ps[:, tt // 4, (tt % 4) * P:(tt % 4 + 1) * P],
                                               tok(m.g_ke[:, :], tt), m.cst[:, K_ID:K_ID + P])
                last.then_inc(m.sem("ke_turned"), 1)
                def scores(tt):
                    a = 5 * u + tt
                    if a >= 1:
                        pe.wait_ge(m.sem("a_masked"), a)
                    for hh in range(2):
                        h = slice(64 * hh, 64 * hh + 64)
                        last = nc.tensor.matmul(m.ps[:, 6 + hh, 0:P], tok(m.g_ki[h, :], tt),
                                                tok(m.g_qd[h, :], tt), start=True, stop=True)
                    last.then_inc(m.sem("a_done"), 1)

                pe.wait_ge(m.sem("k_inv"), u + 1)
                scores(0)
                pe.wait_ge(m.sem("ke_rows"), u + 1)
                if u:
                    pe.wait_ge(m.sem("mod_copied"), u)
                for idx in range(NCH):
                    tt, half = idx // 2, idx % 2
                    for hh in range(2):
                        last = nc.tensor.matmul(ds_at(idx, slice(64 * hh, 64 * hh + 64)),
                                                m.g_ker[64 * half:64 * half + 64, tt, 64 * hh:64 * hh + 64],
                                                m.lv[64 * half:64 * half + 64, tt, (2 * hp + hh) * P:(2 * hp + hh + 1) * P],
                                                start=True, stop=True)
                last.then_inc(m.sem("ds_done"), 1)

                def outputs(tt):
                    a = 5 * u + tt
                    pe.wait_ge(m.sem("a_masked"), a + 1)
                    if a >= 1:
                        pe.wait_ge(m.sem("o_summed"), a)
                    for hh in range(2):
                        nc.tensor.matmul(m.ps[:, 4 + hh, 0:P], m.g_am[:, dr, a % 2, hh, :],
                                         m.lv[:, tt, (2 * hp + hh) * P:(2 * hp + hh + 1) * P],
                                         start=True, stop=False, skip_group_check=True)
                        for half in range(2):
                            q = chunk_pos(2 * tt + half) * CH
                            last = nc.tensor.matmul(m.ps[64 * half:64 * half + 64, 4 + hh, 0:P],
                                                    m.g_qd[64 * hh:64 * hh + 64, q:q + CH],
                                                    m.g_s[64 * hh:64 * hh + 64, 2 * tt + half, :],
                                                    start=False, stop=True, skip_group_check=True)
                    last.then_inc(m.sem("o_done"), 1)

                mod_slab(nc, pe, m, 3, u + 1, 5).then_inc(m.sem("slab_used"), 1)
                pe.wait_ge(m.sem("state_done"), u + 1)
                if u < 3:
                    z(u + 1)
                pe.wait_ge(m.sem("mod_rows"), u + 1)
                turn_mod(nc, m, 8, 2).then_inc(m.sem("mod_turned"), 1)
                for tt in range(TT):
                    if tt + 1 < TT:
                        scores(tt + 1)
                    outputs(tt)

        @block.vector
        def _(dve):
            order = Signal(m.sem("dve_order"))
            def inverse(hp):
                return order.step(nc.vector.reciprocal(m.g_st[:, 40 + 10 * hp:50 + 10 * hp],
                                                       m.g_st[:, 20 + 10 * hp:30 + 10 * hp]))

            def gate(hp, tt):
                for hh in range(2):
                    c = slice((2 * hp + hh) * P, (2 * hp + hh + 1) * P)
                    g = 40 + 10 * hp + 2 * tt + hh
                    order.step(nc.vector.scalar_tensor_tensor(out=m.glr[:, tt, c], in0=m.glr[:, tt, c],
                                                              scalar=m.g_st[:, g:g + 1], in1=m.lg[:, tt, c],
                                                              op0=ALU.mult, op1=ALU.mult))

            def z_min(u):
                hp, dr = units[u]
                dve.wait_ge(m.sem("z_done"), u + 1)
                nc.vector.tensor_scalar(halves(m.g_min[:, :]), m.ps[:, 0:2, 0:HALF], m.g_ab[:, dr, hp:hp + 1], 0.0,
                                        ALU.add, ALU.min).then_inc(m.sem("z_min"), 1)

            def log_gate(u):
                dve.wait_ge(m.sem("z_min"), u + 1)
                dve.wait_ge(m.sem("softplus"), u + 1)
                nc.vector.tensor_tensor(m.g_la[:, :], m.g_min[:, :], m.g_sp[:, :], ALU.subtract).then_inc(m.sem("la_done"), 1)

            def cumulate(u):
                flip = slice(None, None, -1) if units[u][1] else slice(None)
                dve.wait_ge(m.sem("la_done"), u + 1)
                nc.vector.tensor_tensor_scan(m.g_cum[:, flip], m.g_cst[:, G_CM:G_CM + T], m.g_la[:, flip], 0.0,
                                             ALU.mult, ALU.add).then_inc(m.sem("cum_done"), 1)

            def to_end(u):
                last = slice(CH - 1, CH) if units[u][1] == 0 else slice(0, 1)
                dve.wait_ge(m.sem("cum_done"), u + 1)
                cum = m.g_cum[:, :].rearrange("p (c t) -> p c t", t=CH)
                nc.vector.tensor_tensor(m.g_la[:, :].rearrange("p (c t) -> p c t", t=CH),
                                        cum[:, :, last].broadcast_to([P, NCH, CH]), cum, ALU.subtract
                                        ).then_inc(m.sem("to_end"), 1)

            z_min(0)
            dve.wait_ge(m.sem("act_order"), 1)
            lg = m.lg[:, :, :].rearrange("p t (h c) -> p (t h) c", c=P)
            gated = order.step(nc.vector.tensor_tensor(lg, lg, m.g_on[:, :].unsqueeze(1).broadcast_to([P, 20, P]), ALU.mult))
            dve.wait_ge(*gated)
            log_gate(0)
            cumulate(0)
            to_end(0)
            for u, (hp, dr) in enumerate(units):
                if u:
                    dve.wait_ge(m.sem("o_done"), 5 * u)
                dve.wait_ge(m.sem("exp_q"), u + 1)
                nc.vector.tensor_tensor(m.g_qd[:, :], m.lT[:, hp, :], m.g_eq[:, :], ALU.mult).then_inc(m.sem("q_decayed"), 1)
                dve.wait_ge(m.sem("exp_k"), u + 1)
                nc.vector.tensor_tensor(m.g_ki[:, :], m.lT[:, 2 + hp, :], m.g_ek[:, :], ALU.mult).then_inc(m.sem("k_inv"), 1)
                dve.wait_ge(m.sem("exp_end"), u + 1)
                nc.vector.tensor_tensor(m.g_ke[:, :], m.lT[:, 2 + hp, :], m.g_min[:, :], ALU.mult).then_inc(m.sem("k_end"), 1)
                dve.wait_ge(m.sem("decay"), u + 1)
                dve.wait_ge(m.sem("ds_done"), u + 1)
                dve.wait_ge(m.sem("state_in"), 16 * (u + 1))
                if u:
                    dve.wait_ge(m.sem("state_out"), 16 * u)
                done = order.step(nc.vector.memset(m.g_s[:, (8, 9)[dr], :], 0.0))
                run = list(range(0, 7)) + [8] if dr == 0 else list(range(7, 0, -1)) + [9]
                to = 1 if dr == 0 else -1
                for idx in run:
                    dve.wait_ge(*done)
                    done = order.step(nc.vector.scalar_tensor_tensor(
                        out=m.g_s[:, idx + to, :], in0=m.g_s[:, idx, :],
                        scalar=m.g_dec[:, chunk_pos(idx):chunk_pos(idx) + 1],
                        in1=ds_at(idx), op0=ALU.mult, op1=ALU.add))
                dve.wait_ge(*done)
                idx = 9 if dr == 0 else 8
                nc.vector.scalar_tensor_tensor(
                    out=m.g_sf[:, :], in0=m.g_s[:, idx, :], scalar=m.g_dec[:, chunk_pos(idx):chunk_pos(idx) + 1],
                    in1=ds_at(idx), op0=ALU.mult, op1=ALU.add
                ).then_inc(m.sem("state_done"), 1)

                def mask(tt):
                    a = 5 * u + tt
                    dve.wait_ge(m.sem("a_done"), a + 1)
                    if a >= 2:
                        dve.wait_ge(m.sem("o_done"), a - 1)
                    msk = m.g_cst[:, (G_MF, G_MB)[dr]:(G_MF, G_MB)[dr] + P].bitcast(I32)
                    nc.vector.copy_predicated(m.g_am[:, dr, a % 2, :, :], msk.unsqueeze(1).broadcast_to([P, 2, P]),
                                              m.ps[:, 6:8, 0:P]
                                              ).then_inc(m.sem("a_masked"), 1)

                mask(0)
                dve.wait_ge(m.sem("mod_turned"), u + 1)
                add_mod_bias(nc, m, 2, 16 + 8 * u, 8).then_inc(m.sem("mod_copied"), 1)
                if u < 3:
                    z_min(u + 1)
                if u == 2:
                    dve.wait_ge(m.sem("o_std"), 1)
                    done = inverse(0)
                    dve.wait_ge(*done)
                for tt in range(TT):
                    a = 5 * u + tt
                    if tt + 1 < TT:
                        mask(tt + 1)
                    if u == 2:
                        gate(0, tt)
                    if u < 3 and tt >= 2:
                        (log_gate, cumulate, to_end)[tt - 2](u + 1)
                    dve.wait_ge(m.sem("o_done"), a + 1)
                    dst = m.glr[:, tt, hp * 256:(hp + 1) * 256].rearrange("p (h c) -> p h c", h=2)
                    src = m.ps[:, 4:6, 0:P]
                    if dr == 0:
                        nc.vector.tensor_copy(dst, src).then_inc(m.sem("o_summed"), 1)
                    else:
                        dve.wait_ge(m.sem("o_summed"), a - 4)
                        nc.vector.tensor_tensor(dst, dst, src, ALU.add).then_inc(m.sem("o_summed"), 1)
            dve.wait_ge(m.sem("mod_copied"), 4)
            order.step(affine(nc, m, dve, order, 1))
            next_low(nc.vector, m, dve, nxt)
            dve.wait_ge(m.sem("o_std"), 2)
            done = inverse(1)
            dve.wait_ge(*done)
            for tt in range(TT):
                gate(1, tt)


def project_attention(nc, m, d, L):
    slabs = [(C_GQ, 0), (C_GQ + 256, 0), (C_DQ, 1), (C_DQ + 256, 1), (C_GK, 2), (C_DK, 3), (C_DK + 256, 3),
             (C_DV, None), (C_DV + 256, None)]
    n = len(slabs)

    def place(s):
        if s < 4:
            return m.rq[:, 2 * s:2 * s + 2, :, :]
        b = {4: 8, 5: 0, 6: 2, 7: 4, 8: 6}[s]
        return m.kv[:, b:b + 2, 0:TT, :]

    normed = [s for s in range(n) if slabs[s][1] is not None]
    turns = {s: [] for s in range(n)}
    for s in normed:
        if s < 4:
            turns[s + 2] += [(2 * c, m.rq, 2 * s + c, TT, 0) for c in range(2)]
        elif s == 4:
            turns[s + 2] += [(0, m.kv, 8, TT + 1, 1), (2, m.kv, 10, TT + 1, 1)]
        else:
            turns[s + 2] += [(2 * c, m.kv, 2 * (s - 5) + c, TT + 1, s - 3) for c in range(2)]
    with m.block() as block:
        @block.sync
        def _(sp):
            out = m.sem("kv_stored")
            took_loads(sp, m)
            for s in range(2, n):
                sp.wait_ge(m.sem("low_ready"), s - 1)
                load_w_in(sp, m, d, L, slabs[s][0], s % 2, m.sem(f"slab_loaded{s % 2}"))
                if s == 7:
                    sp.wait_ge(m.sem("normed"), 5)
                    sp.dma_start(d["new_gqa_k"][0, ds(L, 1), :, :, :].rearrange("a t h c -> (a t) (h c)"),
                                 m.kv[:, 8, CTX, :]).then_inc(m.sem("k_stored0"), 16)
            for h in range(2):
                sp.wait_ge(m.sem("normed"), 6 + h)
                sp.dma_start(d["new_diff_k"][0, ds(L, 1), :, 2 * h:2 * h + 2, :, :].rearrange("a t h m c -> (a t) h (m c)"),
                             m.kv[:, 2 * h:2 * h + 2, CTX, :]).then_inc(m.sem(f"k_stored{h + 1}"), 16)
            sp.wait_ge(m.sem("tile_copied"), 5 * n)
            sp.dma_start(d["new_gqa_v"][0, ds(L, 1), :, :, :].rearrange("a t h c -> (a t) (h c)"),
                         m.kv[:, 9, CTX, :]).then_inc(out, 16)
            sp.dma_start(d["new_diff_v"][0, ds(L, 1), :, :, :].rearrange("a t h c -> (a t) h c"),
                         m.kv[:, 4:8, CTX, :]).then_inc(out, 16)
            sp.wait_ge(out, 32)
            sp.wait_ge(m.sem("caches"), 6 * 16)

        @block.gpsimd
        def _(pool):
            pool.wait_ge(m.sem("rope_tables"), 16)
            for kind in range(4):
                w = m.gains[:, kind, :].unsqueeze(1).broadcast_to([P, TT, HD])
                nc.gpsimd.tensor_tensor(m.r_c[:, kind, :, :], m.r_tab[:, 0, :, :], w, ALU.mult).then_inc(m.sem("tables"), 1)
                nc.gpsimd.tensor_tensor(m.r_s[:, kind, :, :], m.r_tab[:, 1, :, :], w, ALU.mult).then_inc(m.sem("tables"), 1)

        @block.scalar
        def _(act):
            act.dma_start(m.r_tab[:, :, :, :], d["const_rope"]).then_inc(m.sem("rope_tables"), 16)
            caches = m.sem("caches")
            act.dma_start(m.kv[:, 0:4, TT, :], d["cache_diff_k"][0, ds(L, 1), :, :, :, :].
                           rearrange("a t h m c -> (a t) h (m c)")).then_inc(caches, 16)
            act.dma_start(m.kv[:, 4:8, TT, :], d["cache_diff_v"][0, ds(L, 1), :, :, :].
                           rearrange("a t h c -> (a t) h c")).then_inc(caches, 16)
            gk = d["cache_gqa_k"][0, ds(L, 1), :, :, :].rearrange("a t h c -> (a t) h c")
            act.dma_start(m.kv[:, 8, TT, :].rearrange("p (h c) -> p h c", h=2), gk).then_inc(caches, 16)
            act.dma_start(m.kv[:, 9, TT, :].rearrange("p (h c) -> p h c", h=2),
                           d["cache_gqa_v"][0, ds(L, 1), :, :, :].rearrange("a t h c -> (a t) h c")).then_inc(caches, 16)
            for h in range(2):
                act.dma_start(m.kv[:, 10, TT, (1 - h) * HD:(2 - h) * HD], gk[:, h, :]).then_inc(caches, 16)
            def high(s):
                high_part(nc, m, act, s % 2, 16 * (s // 2 + 1), (m.sem("tile_done"), 5 * (s - 1)) if s > 1 else None)

            act.sem_inc(m.sem("high_ready"), 1)
            q = turn = 0
            for s in range(n):
                if s + 1 < n:
                    high(s + 1)
                for tt in range(TT):
                    act.wait_ge(m.sem("tile_done"), 5 * s + tt + 1)
                    nc.scalar.activation(place(s)[:, :, tt, :],
                                         m.ps[:, (5 * s + tt) % 6, 0:256].rearrange("p (b c) -> p b c", b=2),
                                         ACT.Copy).then_inc(m.sem("tile_copied"), 1)
                    for after, buf, b, tiles, stored in turns[s]:
                        if after == tt:
                            act.wait_ge(m.sem("turned"), turn + 1)
                            if stored:
                                act.wait_ge(m.sem(f"k_stored{stored - 1}"), 16)
                            nc.scalar.activation(buf[:, b, 0:tiles, :].rearrange("p t c -> p (t c)"),
                                                 m.ps[:, 6:8, :].rearrange("p b c -> p (b c)")[:, 0:tiles * P], ACT.Copy,
                                                 scale=(HD ** -0.5 if turn < 8 else 1.0)
                                                 ).then_inc(m.sem("turned_copied"), 1)
                            turn += 1
                if s in normed:
                    nb = 1 if s == 4 else 2
                    act.wait_ge(m.sem("tile_copied"), 5 * s + 5)
                    if q:
                        act.wait_ge(m.sem("mean_squares"), q)
                    nc.scalar.activation(m.r_sq[:, 0:nb * T].rearrange("p (b t) -> p b t", b=nb),
                                         place(s)[:, 0:nb, :, :].rearrange("p b t c -> p b (t c)"), ACT.Square
                                         ).then_inc(m.sem("squares"), 1)
                    act.wait_ge(m.sem("mean_squares"), q + 1)
                    if q:
                        act.wait_ge(m.sem("normed"), q)
                    nc.scalar.activation(m.r_st[:, 1, 0:10 * nb], m.r_st[:, 0, 0:10 * nb], ACT.Sqrt, scale=1.0 / HD,
                                         bias=m.cst[:, K_LAM + 4:K_LAM + 5]).then_inc(m.sem("head_std"), 1)
                    q += 1

        @block.vector
        def _(dve):
            order = Signal(m.sem("dve_order"))
            dve.sem_inc(m.sem("low_ready"), 1)
            q = 0
            for s, (_, kind) in enumerate(slabs):
                if s + 1 < n:
                    low_part(nc, m, dve, s + 1, (s + 1) % 2)
                if kind is None:
                    continue
                nb = 1 if s == 4 else 2
                x = place(s)
                dve.wait_ge(m.sem("squares"), q + 1)
                nc.vector.tensor_reduce(m.r_st[:, 0, 0:10 * nb],
                                        m.r_sq[:, 0:nb * T].rearrange("p (g c) -> p g c", c=HD), AX.X, ALU.add
                                        ).then_inc(m.sem("mean_squares"), 1)
                dve.wait_ge(m.sem("head_std"), q + 1)
                done = order.step(nc.vector.reciprocal(m.r_st[:, 2, 0:10 * nb], m.r_st[:, 1, 0:10 * nb]))
                if q == 0:
                    dve.wait_ge(m.sem("tables"), 8)
                marks = []
                dve.wait_ge(*done)
                for b in range(nb):
                    xb = x[:, b, :, :].rearrange("p t (h c) -> p (t h) c", c=HD)
                    r = m.r_st[:, 2, 10 * b:10 * b + 10].unsqueeze(2).broadcast_to([P, 10, HD])
                    done = order.step(nc.vector.tensor_tensor(xb, xb, r, ALU.mult))
                dve.wait_ge(*done)
                for b in range(nb):
                    xb = x[:, b, :, :].rearrange("p t (h c) -> p t h c", c=HD)
                    tb = m.r_t[:, b * T:(b + 1) * T].rearrange("p (t h c) -> p t h c", h=2, c=HD)
                    sin = m.r_s[:, kind, :, :].unsqueeze(2).broadcast_to([P, TT, 2, HD])
                    done = order.step(nc.vector.tensor_tensor(tb, xb, sin, ALU.mult))
                dve.wait_ge(*done)
                for b in range(nb):
                    xb = x[:, b, :, :].rearrange("p t (h c) -> p t h c", c=HD)
                    cos = m.r_c[:, kind, :, :].unsqueeze(2).broadcast_to([P, TT, 2, HD])
                    done = order.step(nc.vector.tensor_tensor(xb, xb, cos, ALU.mult))
                dve.wait_ge(*done)
                for b in range(nb):
                    xb = x[:, b, :, :].rearrange("p t (g u f) -> p (t g) u f", u=2, f=16)
                    tb = m.r_t[:, b * T:(b + 1) * T].rearrange("p (g u f) -> p g u f", u=2, f=16)[:, :, ::-1, :]
                    ins = nc.vector.tensor_tensor(xb, xb, tb, ALU.add)
                    if s == 4 or b == 0:
                        done = order.step(ins)
                if s == 4:
                    dve.wait_ge(*done)
                    for h in range(2):
                        ins = nc.vector.tensor_copy(m.kv[:, 10, 0:TT, (1 - h) * HD:(2 - h) * HD],
                                                    m.kv[:, 8, 0:TT, h * HD:(h + 1) * HD])
                ins.then_inc(m.sem("normed"), 1)
                dve.wait_ge(m.sem("normed"), q + 1)
                q += 1

        @block.tensor
        def _(pe):
            turn = 0
            for s in range(n):
                pe.wait_ge(m.sem("low_ready"), s + 1)
                for tt in range(TT):
                    g = 5 * s + tt
                    if g >= 6:
                        pe.wait_ge(m.sem("tile_copied"), g - 5)
                    row_tile(nc, m, s % 2, tt, g % 6).then_inc(m.sem("tile_done"), 1)
                    for after, buf, b, tiles, _ in turns[s]:
                        if after == tt:
                            pe.wait_ge(m.sem("normed"), s - 1)
                            if tiles > TT:
                                pe.wait_ge(m.sem("caches"), 6 * 16)
                            if turn:
                                pe.wait_ge(m.sem("turned_copied"), turn)
                            for t in range(tiles):
                                last = nc.tensor.transpose(m.ps[:, 6 + t // 4, (t % 4) * P:(t % 4 + 1) * P],
                                                           buf[:, b, t, :], m.cst[:, K_ID:K_ID + P])
                            last.then_inc(m.sem("turned"), 1)
                            turn += 1


def attention(nc, m, d, L, nxt):
    def gqa(qt, h):
        return (qt, h // 2, h % 2, 8 if h // 4 == h % 2 else 10, 9, h // 4 * HD, (h % 2) * HD, None)

    def quad(j):
        return (CTX, 2 * j, None, None, None, None, None, "gqa" if j < 2 else "diff")

    items = []
    for qt in range(CTX):
        items += [(qt, 4 + h, mp, h, 4 + h, 0, 0, mp) for h in range(4) for mp in range(2)]
        items += [quad(qt)] + [gqa(qt, h) for h in range(8)]
    units = [i for i, it in enumerate(items) if it[7] != 0]
    unit_of = {i: u for u, i in enumerate(units)}

    def blocks(i):
        return {"gqa": 4, "diff": 2}.get(items[i][7], TT)

    def mixes(upto):
        return sum(items[j][7] in (1, "diff") for j in units[:upto + 1])

    keys = [0, 1, 2, 3, TT]

    def pair(i, n):
        return m.ps[:, 2 * (i % 3):2 * (i % 3) + 2, :].rearrange("p b c -> p (b c)")[:, 0:n * P]

    def quad_scores(i):
        return m.ps[:, 2 * (i % 3):2 * (i % 3) + 2, 0:2 * P].rearrange("p b (j c) -> p b j c", c=P)

    def quad_st(i):
        return m.a_q[:, items[i][1] // 2, :]

    with m.block() as block:
        @block.sync
        def _(sp):
            for j in range(2):
                next_load(sp, m, nxt, j)
            next_loaded(sp, m, nxt)

        @block.tensor
        def _(pe):
            def scores(i):
                qt, qb, half, kb, *_ = items[i]
                j = i - 3
                if j in unit_of:
                    pe.wait_ge(m.sem("p_copied"), unit_of[j] + 1)
                elif j >= 0:
                    pe.wait_ge(m.sem("exp_done"), j + 1)
                b = 2 * (i % 3)
                if qt < CTX:
                    h = slice(64 * half, 64 * half + 64)
                    q = m.rq[h, qb, qt, :]
                    nc.tensor.matmul(m.ps[:, b, :], q, m.kv[h, kb, 0:4, :].rearrange("p t c -> p (t c)"),
                                     start=True, stop=True)
                    last = nc.tensor.matmul(m.ps[:, b + 1, 0:P], q, m.kv[h, kb, TT, :], start=True, stop=True)
                else:
                    for half in range(2):
                        for j in range(2):
                            h = slice(64 * half, 64 * half + 64)
                            kb = gqa(qt, 2 * (qb + j) + half)[3] if qb < 4 else qb - 4 + j
                            last = nc.tensor.matmul(m.ps[:, b + half, j * P:(j + 1) * P], m.rq[h, qb + j, qt, :],
                                                    m.kv[h, kb, CTX, :], start=True, stop=True)
                last.then_inc(m.sem("scores"), 1)

            def weigh(u):
                i = units[u]
                mp = items[i][7]
                slot = (i - 1) % 4 if mp == 1 else i % 4
                pe.wait_ge(m.sem("exp_done"), i + 1)
                if mp in (1, "diff"):
                    pe.wait_ge(m.sem("mixed"), mixes(u))
                for n in range(blocks(i)):
                    last = nc.tensor.transpose(m.ps[:, 2 * (i % 3) + n // 4, (n % 4) * P:(n % 4 + 1) * P],
                                               m.e[:, slot, n * P:(n + 1) * P], m.cst[:, K_ID:K_ID + P])
                last.then_inc(m.sem("p_turned"), 1)

            def values(u):
                qt, qb, _, _, vb, vc, _, mp = items[units[u]]
                pe.wait_ge(m.sem("p_copied"), u + 1)
                if u >= 2:
                    pe.wait_ge(m.sem("o_copied"), u - 1)
                if qt < CTX:
                    w = HD if mp is None else P
                    for n, kt in enumerate(keys):
                        last = nc.tensor.matmul(m.ps[:, 6 + u % 2, 0:w], m.eT[:, u % 2, n, :], m.kv[:, vb, kt, vc:vc + w],
                                                start=(n == 0), stop=(n == len(keys) - 1))
                else:
                    for n in range(blocks(units[u])):
                        v = m.kv[:, 9, CTX, qb // 2 * HD:(qb // 2 + 1) * HD] if mp == "gqa" else m.kv[:, qb + n, CTX, :]
                        w = HD if mp == "gqa" else P
                        last = nc.tensor.matmul(m.ps[:, 6 + u % 2, n * w:(n + 1) * w], m.eT[:, u % 2, n, :], v,
                                                start=True, stop=True)
                last.then_inc(m.sem("o_done"), 1)

            scores(0)
            scores(1)
            for i in range(len(items)):
                if i + 2 < len(items):
                    scores(i + 2)
                if i in unit_of:
                    weigh(unit_of[i])
                    if unit_of[i] >= 1:
                        values(unit_of[i] - 1)
            values(len(units) - 1)

        @block.gpsimd
        def _(pool):
            done = 0
            for u, i in enumerate(units):
                qt, qb, *_, mp = items[i]
                if mp in (1, "diff"):
                    done += 1
                    pool.wait_ge(m.sem("o_squared"), done)
                    for j in range(1 if mp == 1 else 2):
                        o = m.rq[:, qb + j, qt, :]
                        nc.gpsimd.tensor_tensor(o, o, m.subn[:, :], ALU.mult).then_inc(m.sem("pool_order"), 1)

        @block.scalar
        def _(act):
            def exp(i):
                act.wait_ge(m.sem("maximum"), i + 1)
                old = [u for u, j in enumerate(units) if j <= i - 4 or (items[j][7] == 1 and j - 1 <= i - 4)]
                if old:
                    act.wait_ge(m.sem("p_turned"), old[-1] + 1)
                if items[i][0] < CTX:
                    ins = nc.scalar.activation(m.e[:, i % 4, :], pair(i, TT), ACT.Exp, bias=m.a_st[:, i % 32, 0:1],
                                               accum_out=m.a_st[:, i % 32, 1:2])
                else:
                    for n in range(4):
                        ins = nc.scalar.activation(m.e[:, i % 4, n * P:(n + 1) * P], quad_scores(i)[:, n // 2, n % 2, :],
                                                   ACT.Exp, bias=quad_st(i)[:, n:n + 1], accum_out=quad_st(i)[:, 4 + n:5 + n])
                ins.then_inc(m.sem("exp_done"), 1)

            def copy(u):
                i = units[u]
                n = blocks(i)
                act.wait_ge(m.sem("p_turned"), u + 1)
                if u >= 2:
                    act.wait_ge(m.sem("o_done"), u - 1)
                nc.scalar.activation(m.eT[:, u % 2, 0:n, :].rearrange("p t c -> p (t c)"), pair(i, n), ACT.Copy
                                     ).then_inc(m.sem("p_copied"), 1)

            def square(u):
                qt, qb, *_, mp = items[units[u]]
                if mp in (1, "diff"):
                    act.wait_ge(m.sem("o_copied"), u + 1)
                    if mixes(u) > 2:
                        act.wait_ge(m.sem("o_squared"), mixes(u) - 2)
                    for j in range(1 if mp == 1 else 2):
                        g = (qb + j - 4) * TT + qt
                        ins = nc.scalar.activation(m.o_sq[:, mixes(u) % 2, j, :], m.rq[:, qb + j, qt, :], ACT.Square,
                                                   accum_out=m.sml[:, g:g + 1])
                    ins.then_inc(m.sem("o_squared"), 1)

            exp(0)
            for i in range(len(items)):
                if i + 1 < len(items):
                    exp(i + 1)
                if i in unit_of:
                    copy(unit_of[i])
                    if unit_of[i] >= 2:
                        square(unit_of[i] - 2)
                if i == 4:
                    next_high(nc, m, act, nxt)
            square(len(units) - 2)
            square(len(units) - 1)

        @block.vector
        def _(dve):
            order = Signal(m.sem("dve_order"))

            def maximum(i):
                dve.wait_ge(m.sem("scores"), i + 1)
                if items[i][0] < CTX:
                    ins = nc.vector.tensor_reduce(m.a_st[:, i % 32, 0:1], pair(i, TT), AX.X, ALU.max, negate=True)
                else:
                    ins = nc.vector.tensor_reduce(quad_st(i)[:, 0:4].rearrange("p (b j) -> p b j", b=2), quad_scores(i),
                                                  AX.X, ALU.max, negate=True)
                ins.then_inc(m.sem("maximum"), 1)

            def inverse(u):
                i = units[u]
                dve.wait_ge(m.sem("exp_done"), i + 1)
                if items[i][0] == CTX:
                    a = quad_st(i)
                    done = order.step(nc.vector.reciprocal(a[:, 8:12], a[:, 4:8]))
                    if items[i][7] == "diff":
                        dve.wait_ge(*done)
                        done = order.step(nc.vector.scalar_tensor_tensor(out=a[:, 12:14], in0=a[:, 4:6],
                                                                         scalar=m.nlam[:, 0:1], in1=a[:, 10:12],
                                                                         op0=ALU.mult, op1=ALU.mult))
                        dve.wait_ge(*done)
                        for j in range(2):
                            first, second = [m.e[:, i % 4, n * P:(n + 1) * P] for n in (j, 2 + j)]
                            ins = nc.vector.scalar_tensor_tensor(out=first, in0=second, scalar=a[:, 12 + j:13 + j],
                                                                 in1=first, op0=ALU.mult, op1=ALU.add)
                        ins.then_inc(m.sem("mixed"), 1)
                    return done
                n = TT * P
                a = m.a_st[:, i % 32, :]
                done = order.step(nc.vector.reciprocal(a[:, 2:3], a[:, 1:2]))
                if items[i][7] == 1:
                    b = m.a_st[:, (i - 1) % 32, :]
                    dve.wait_ge(*done)
                    done = order.step(nc.vector.scalar_tensor_tensor(out=a[:, 3:4], in0=b[:, 1:2], scalar=m.nlam[:, 0:1],
                                                                     in1=a[:, 2:3], op0=ALU.mult, op1=ALU.mult))
                    dve.wait_ge(*done)
                    nc.vector.scalar_tensor_tensor(out=m.e[:, (i - 1) % 4, 0:n], in0=m.e[:, i % 4, 0:n],
                                                   scalar=a[:, 3:4], in1=m.e[:, (i - 1) % 4, 0:n],
                                                   op0=ALU.mult, op1=ALU.add).then_inc(m.sem("mixed"), 1)
                    done = order.step(nc.vector.reciprocal(a[:, 2:3], b[:, 1:2]))
                return done

            def out(u, done):
                i = units[u]
                qt, qb, half, _, _, _, oc, mp = items[i]
                dve.wait_ge(*done)
                dve.wait_ge(m.sem("o_done"), u + 1)
                if qt == CTX:
                    a = quad_st(i)
                    if mp == "gqa":
                        dst = m.rq[:, qb:qb + 2, qt, :].rearrange("p j (h c) -> p h j c", h=2)
                        src = m.ps[:, 6 + u % 2, 0:4 * HD].rearrange("p (h j c) -> p h j c", h=2, j=2)
                        inv = a[:, 8:12].rearrange("p (h j) -> p h j", h=2).unsqueeze(3).broadcast_to([P, 2, 2, HD])
                    else:
                        dst = m.rq[:, qb:qb + 2, qt, :]
                        src = m.ps[:, 6 + u % 2, 0:2 * P].rearrange("p (j c) -> p j c", j=2)
                        inv = a[:, 8:10].unsqueeze(2).broadcast_to([P, 2, P])
                    nc.vector.tensor_tensor(dst, src, inv, ALU.mult).then_inc(m.sem("o_copied"), 1)
                    return
                if mp is None and half == 0:
                    dve.wait_ge(m.sem("scores"), i + 2)
                w = HD if mp is None else P
                nc.vector.tensor_scalar(m.rq[:, qb, qt, oc:oc + w], m.ps[:, 6 + u % 2, 0:w], m.a_st[:, i % 32, 2:3],
                                        None, ALU.mult).then_inc(m.sem("o_copied"), 1)

            maximum(0)
            maximum(1)
            marks = []
            for i in range(len(items)):
                if i in unit_of and items[i][7] != 1:
                    marks.append(inverse(unit_of[i]))
                elif items[i][7] == 0:
                    marks.append(inverse(unit_of[i + 1]))
                if i + 2 < len(items):
                    maximum(i + 2)
                if i in unit_of and unit_of[i] >= 1:
                    out(unit_of[i] - 1, marks[unit_of[i] - 1])
                if i == 6:
                    next_low(nc.vector, m, dve, nxt)
            out(len(units) - 1, marks[-1])


def merge(nc, m, d, L, nxt):
    rows = [m.rq[:, b, :, :] for b in range(4)] + \
           [m.glr[:, :, b * P:(b + 1) * P] for b in range(4)] + [m.rq[:, 4 + b, :, :] for b in range(4)]
    pairs = KT // 2

    with m.block() as block:
        @block.sync
        def _(sp):
            took_loads(sp, m)

            def loads(dp, first=0):
                for i in range(first, 3):
                    for kind in range(2):
                        sp.wait_ge(m.sem("low_ready"), dp * 6 + 2 * i + kind + 1)
                        load_merge(sp, m, d, L, dp, i, kind, m.sem(f"slab_loaded{kind}"))

            loads(0, 1)
            with sp.Fori(1, pairs) as dp:
                loads(dp)
            for j in range(2):
                next_load(sp, m, nxt, j, "low_ready", 6 * pairs + j + 1)
            next_loaded(sp, m, nxt)

        @block.scalar
        def _(act):
            act.sem_inc(m.sem("gates_ready"), 2)
            act.sem_inc(m.sem("high_ready"), 1)
            nc.scalar.activation(m.sml[:, 20:40], m.sml[:, 0:20], ACT.Sqrt, scale=1.0 / P,
                                 bias=m.cst[:, K_LAM + 4:K_LAM + 5]).then_inc(m.sem("o_std"), 1)

            def high(dp, s):
                slot = s % 2
                act.wait_ge(m.sem(f"slab_loaded{slot}"), dp * 48 + 16 * (s // 2 + 1))
                act.wait_ge(m.sem("tile_done"), dp * 12 + 2 * s + 2)
                n = SLAB if slot == 0 else 1024
                nc.scalar.activation(m.wH[:, slot, 0:n], m.raw[:, slot, 0:n], ACT.Copy).then_inc(m.sem("high_ready"), 1)

            for t in range(12):
                act.wait_ge(m.sem("turned"), t + 1)
                pair = 2 + t % 2
                nc.scalar.activation(halves(m.oH[:, t, :]), m.ps[:, 2 * pair:2 * pair + 2, 0:HALF], ACT.Copy
                                     ).then_inc(m.sem("turned_high"), 1)
                if t == 8:
                    high(0, 1)

            def split(ks):
                for k in ks:
                    act.wait_ge(m.sem("mixed"), 4 * (k // 2 + 1))
                    nc.scalar.activation(m.hH[:, k, :], m.mix[:, k, :], ACT.Copy).then_inc(m.sem("mix_high"), 1)

            def round_(dp, first, last):
                for i in range(3):
                    if not (first and i == 0):
                        high(dp, 2 * i + 1)
                    for c in range(2):
                        act.wait_ge(m.sem("tile_done"), dp * 12 + 4 * i + c + 1 + 4)
                        act.wait_ge(m.sem("gated"), dp * 6 + 2 * i + c + 1)
                        nc.scalar.activation(halves(m.gate[:, c, :]), m.ps[:, 2 * c:2 * c + 2, 0:HALF], ACT.Sigmoid
                                             ).then_inc(m.sem("gates_ready"), 1)
                    if last and i == 2:
                        next_high(nc, m, act, nxt, "tile_done", 12 * pairs + 2)
                        split(range(6))
                    else:
                        high(dp, 2 * i + 2)

            round_(0, True, False)
            with act.Fori(1, pairs - 1) as dp:
                round_(dp, False, False)
            round_(pairs - 1, False, True)
            split((6, 7))

        @block.vector
        def _(dve):
            order = Signal(m.sem("dve_order"))
            dve.sem_inc(m.sem("low_ready"), 3)
            dve.sem_inc(m.sem("gated"), 2)
            dve.wait_ge(m.sem("o_std"), 1)
            done = order.step(nc.vector.reciprocal(m.sml[:, 40:60], m.sml[:, 20:40]))
            dve.wait_ge(*done)
            def low(dp, s):
                slot = s % 2
                n = SLAB if slot == 0 else 1024
                dve.wait_ge(m.sem("high_ready"), dp * 6 + s + 1)
                nc.vector.tensor_tensor(m.wL[:, slot, 0:n], m.raw[:, slot, 0:n], m.wH[:, slot, 0:n].bitcast(F32),
                                        ALU.subtract).then_inc(m.sem("low_ready"), 1)

            for t in range(12):
                dve.wait_ge(m.sem("turned_high"), t + 1)
                pair = 2 + t % 2
                nc.vector.tensor_tensor(halves(m.oL[:, t, :]), m.ps[:, 2 * pair:2 * pair + 2, 0:HALF],
                                        halves(m.oH[:, t, :]).bitcast(F32), ALU.subtract).then_inc(m.sem("turned_low"), 1)
                if 1 <= t < 5:
                    o = m.rq[:, 3 + t, :, :]
                    inv = m.sml[:, 40 + TT * (t - 1):40 + TT * t].unsqueeze(2).broadcast_to([P, TT, P])
                    nc.vector.tensor_tensor(o, o, inv, ALU.mult).then_inc(m.sem("o_normed"), 1)
                if t == 8:
                    low(0, 1)

            def split(ks):
                for k in ks:
                    dve.wait_ge(m.sem("mix_high"), k + 1)
                    order.step(nc.vector.tensor_tensor(m.hL[:, k, :], m.mix[:, k, :], m.hH[:, k, :].bitcast(F32),
                                                       ALU.subtract))

            def round_(dp, first, last):
                for i in range(3):
                    if not (first and i == 0):
                        low(dp, 2 * i + 1)
                    if last and i == 2:
                        next_low(nc.vector, m, dve, nxt)
                        split(range(6))
                    else:
                        low(dp, 2 * i + 2)
                    for c in range(2):
                        dve.wait_ge(m.sem("tile_done"), dp * 12 + 4 * i + 2 + c + 1 + 4)
                        dve.wait_ge(m.sem("gates_ready"), dp * 6 + 2 * i + c + 1 + 2)
                        mix = m.mix[:, ds(dp * 2 + c, 1), :].rearrange("p a t -> p (a t)")
                        y = m.gy[:, c, :] if i else mix
                        nc.vector.tensor_tensor(halves(y), halves(m.gate[:, c, :]), m.ps[:, 4 + 2 * c:6 + 2 * c, 0:HALF],
                                                ALU.mult).then_inc(m.sem("gated"), 1)
                        dve.wait_ge(m.sem("gated"), dp * 6 + 2 * i + c + 1 + 2)
                        if i:
                            nc.vector.tensor_tensor(mix, mix, y, ALU.add).then_inc(m.sem("mixed"), 1)
                            dve.wait_ge(m.sem("mixed"), dp * 4 + 2 * i + c - 1)

            round_(0, True, False)
            with dve.Fori(1, pairs - 1) as dp:
                round_(dp, False, False)
            round_(pairs - 1, False, True)
            split((6, 7))

        @block.tensor
        def _(pe):
            pe.sem_inc(m.sem("tile_done"), 4)
            steps = [(c, k) for c in range(2) for k in range(KT)]
            for t in range(12):
                if t >= 2:
                    pe.wait_ge(m.sem("turned_low"), t - 1)
                if t >= 8:
                    pe.wait_ge(m.sem("o_normed"), t - 7)
                b = 2 * (2 + t % 2)
                for tt in range(CTX):
                    c = (tt % 2) * P + CH * (tt // 2)
                    nc.tensor.transpose(m.ps[:, b + tt // 2, c:c + P], rows[t][:, tt, :], m.cst[:, K_ID:K_ID + P])
                for h in range(2):
                    r = slice(CH * h, CH * h + CH)
                    c = 256 * (1 - h)
                    last = nc.tensor.transpose(m.ps[:, b + h, c:c + CH], rows[t][r, CTX, :],
                                               m.cst[r, K_ID + CH * h:K_ID + CH * h + CH])
                last.then_inc(m.sem("turned"), 1)
                for c, k in steps[4 * t // 3:4 * (t + 1) // 3]:
                    last = transposed_tile(nc, m, 0, c * P, W256, KT, m.hH, m.hL, 0, c, [k])
                    if k == KT - 1:
                        last.then_inc(m.sem("tile_done"), 1)
            pe.wait_ge(m.sem("turned_low"), 12)

            def round_(dp, first):
                for i in range(3):
                    if not (first and i == 0):
                        pe.wait_ge(m.sem("low_ready"), dp * 6 + 2 * i + 3)
                        for c in range(2):
                            pe.wait_ge(m.sem("gates_ready"), dp * 6 + 2 * i + c + 1)
                            transposed_tile(nc, m, 0, c * P, W256, KT, m.hH, m.hL, 0, c).then_inc(m.sem("tile_done"), 1)
                    pe.wait_ge(m.sem("low_ready"), dp * 6 + 2 * i + 4)
                    for c in range(2):
                        pe.wait_ge(m.sem("gated"), dp * 6 + 2 * i + c + 1)
                        transposed_tile(nc, m, 1, c * P, W256, 4, m.oH, m.oL, 4 * i, 2 + c).then_inc(m.sem("tile_done"), 1)

            round_(0, True)
            with pe.Fori(1, pairs) as dp:
                round_(dp, False)


def add_gated(nc, m, k, gate_col, pair, signal):
    x = m.xT[:, ds(k, 1), :].rearrange("p a t -> p (a t)")
    src = psum_segments(m.ps, pair)
    for c, seg in enumerate(segments(x)):
        g = m.mod[:, ds(k + gate_col, 1), c:c + 1].rearrange("p a b -> p (a b)")
        ins = nc.vector.scalar_tensor_tensor(out=seg, in0=src[c], scalar=g, in1=seg, op0=ALU.mult, op1=ALU.add)
    ins.then_inc(signal, 1)


def project_out(nc, m, d, L, w, gate_col, k0, nk, cols, aH, aL, nxt=None):
    per = cols // P
    slabs = D // cols
    rounds = slabs // 2
    n = nk * cols

    with m.block() as block:
        @block.sync
        def _(sp):
            took_loads(sp, m)
            with sp.Fori(1, rounds) as r:
                for slot in range(2):
                    sp.wait_ge(m.sem("low_ready"), r * 2 + slot + 1)
                    load_out(sp, m, w, L, r * 2 + slot, k0, nk, cols, slot, m.sem(f"slab_loaded{slot}"))
            if nxt:
                for j in range(2):
                    next_load(sp, m, nxt, j, "low_ready", slabs + j + 1)
                next_loaded(sp, m, nxt)

        @block.scalar
        def _(act):
            def high(r, slot):
                act.wait_ge(m.sem(f"slab_loaded{slot}"), r * 16 + 16)
                act.wait_ge(m.sem("tile_done"), r * (2 * per) + slot * per + per)
                nc.scalar.activation(m.wH[:, slot, 0:n], m.raw[:, slot, 0:n], ACT.Copy).then_inc(m.sem("high_ready"), 1)

            act.sem_inc(m.sem("high_ready"), 1)
            with act.Fori(0, rounds - 1) as r:
                high(r, 1)
                high(r + 1, 0)
            high(rounds - 1, 1)
            if nxt:
                next_high(nc, m, act, nxt, "tile_done", slabs * per + per)

        @block.vector
        def _(dve):
            dve.sem_inc(m.sem("low_ready"), 3)
            dve.sem_inc(m.sem("added"), 4)

            def low(s, slot):
                dve.wait_ge(m.sem("high_ready"), s + 1)
                nc.vector.tensor_tensor(m.wL[:, slot, 0:n], m.raw[:, slot, 0:n], m.wH[:, slot, 0:n].bitcast(F32),
                                        ALU.subtract).then_inc(m.sem("low_ready"), 1)

            def add(s, slot):
                for c in range(per):
                    dve.wait_ge(m.sem("tile_done"), s * per + c + 1 + 2 * per)
                    add_gated(nc, m, s * per + c, gate_col, (slot * per + c) % 4, m.sem("added"))

            with dve.Fori(0, rounds - 1) as r:
                for slot in range(2):
                    low(2 * r + slot + 1, 1 - slot)
                    add(2 * r + slot, slot)
            low(2 * rounds - 1, 1)
            add(2 * rounds - 2, 0)
            if nxt:
                next_low(nc.vector, m, dve, nxt)
            add(2 * rounds - 1, 1)

        @block.tensor
        def _(pe):
            pe.sem_inc(m.sem("tile_done"), 2 * per)
            with pe.Fori(0, rounds) as r:
                for slot in range(2):
                    pe.wait_ge(m.sem("low_ready"), 2 * r + slot + 3)
                    for c in range(per):
                        pe.wait_ge(m.sem("added"), r * (2 * per) + slot * per + c + 1 + 4 - 2 * per)
                        transposed_tile(nc, m, slot, c * P, cols, nk, aH, aL, 0, slot * per + c
                                        ).then_inc(m.sem("tile_done"), 1)


def ffn_in(nc, m, d, L, f0, nf, nxt):
    rounds = nf // 2

    with m.block() as block:
        @block.sync
        def _(sp):
            took_loads(sp, m, 32)
            with sp.Fori(1, rounds) as r:
                for slot in range(2):
                    sp.wait_ge(m.sem("low_ready"), 2 * r + slot + 1)
                    load_ffn(sp, m, d, L, f0, 2 * r + slot, slot, m.sem(f"slab_loaded{slot}"))
            for j in range(2):
                next_load(sp, m, nxt, j, "low_ready", nf + j + 1)
            next_loaded(sp, m, nxt)

        @block.scalar
        def _(act):
            def high(s, slot):
                act.wait_ge(m.sem(f"slab_loaded{slot}"), s * 16 - slot * 16 + 32)
                act.wait_ge(m.sem("tile_done"), 2 * s + 2)
                nc.scalar.activation(m.wH[:, slot, :], m.raw[:, slot, :], ACT.Copy).then_inc(m.sem("high_ready"), 1)

            def silu(s, slot):
                act.wait_ge(m.sem("tile_done"), 2 * s + 5)
                act.wait_ge(m.sem("multiplied"), s + 1)
                nc.scalar.activation(halves(m.act[:, slot, :]), m.ps[:, 4 * slot:4 * slot + 2, 0:HALF], ACT.Silu
                                     ).then_inc(m.sem("silu"), 1)

            def split(s, slot):
                act.wait_ge(m.sem("multiplied"), s + 3)
                nc.scalar.activation(m.gH[:, ds(s, 1), :].rearrange("p a t -> p (a t)"), m.gf[:, slot, :], ACT.Copy
                                     ).then_inc(m.sem("g_high"), 1)

            def both(s, slot, more=True):
                if more:
                    high(s + 1, 1 - slot)
                else:
                    next_high(nc, m, act, nxt, "tile_done", 2 * nf + 2)
                silu(s, slot)
                split(s, slot)

            act.sem_inc(m.sem("high_ready"), 1)
            with act.Fori(0, rounds - 1) as r:
                for slot in range(2):
                    both(2 * r + slot, slot)
            both(nf - 2, 0)
            both(nf - 1, 1, False)

        @block.vector
        def _(dve):
            dve.sem_inc(m.sem("low_ready"), 3)
            dve.sem_inc(m.sem("multiplied"), 2)

            def low(s, slot):
                dve.wait_ge(m.sem("high_ready"), s + 1)
                nc.vector.tensor_tensor(m.wL[:, slot, :], m.raw[:, slot, :], m.wH[:, slot, :].bitcast(F32), ALU.subtract
                                        ).then_inc(m.sem("low_ready"), 1)

            def g(s, slot):
                dve.wait_ge(m.sem("silu"), s + 1)
                dve.wait_ge(m.sem("tile_done"), 2 * s + 6)
                nc.vector.tensor_tensor(halves(m.gf[:, slot, :]), halves(m.act[:, slot, :]),
                                        m.ps[:, 4 * slot + 2:4 * slot + 4, 0:HALF], ALU.mult).then_inc(m.sem("multiplied"), 1)
                dve.wait_ge(m.sem("g_high"), s + 1)
                hi = m.gH[:, ds(s, 1), :].rearrange("p a t -> p (a t)").bitcast(F32)
                nc.vector.tensor_tensor(m.gL[:, ds(s, 1), :].rearrange("p a t -> p (a t)"), m.gf[:, slot, :], hi,
                                        ALU.subtract).then_inc(m.sem("g_low"), 1)

            with dve.Fori(0, rounds - 1) as r:
                for slot in range(2):
                    low(2 * r + slot + 1, 1 - slot)
                    g(2 * r + slot, slot)
            low(nf - 1, 1)
            g(nf - 2, 0)
            next_low(nc.vector, m, dve, nxt)
            g(nf - 1, 1)

        @block.tensor
        def _(pe):
            pe.sem_inc(m.sem("tile_done"), 4)
            with pe.Fori(0, rounds) as r:
                for slot in range(2):
                    pe.wait_ge(m.sem("low_ready"), 2 * r + slot + 3)
                    pe.wait_ge(m.sem("multiplied"), 2 * r + slot + 1)
                    for c in range(2):
                        transposed_tile(nc, m, slot, c * P, W256, KT, m.hH, m.hL, 0, 2 * slot + c
                                        ).then_inc(m.sem("tile_done"), 1)


def last_stage(nc, m, d):
    with m.block() as block:
        @block.tensor
        def _(pe):
            for tt in range(TT):
                if tt >= 4:
                    pe.wait_ge(m.sem("copied"), tt - 3)
                for k in range(KT):
                    b = 2 * (tt % 4) + k // 4
                    last = nc.tensor.transpose(m.ps[:, b, (k % 4) * P:(k % 4 + 1) * P], tok(m.xT[:, k, :], tt),
                                               m.cst[:, K_ID:K_ID + P])
                last.then_inc(m.sem("turned"), 1)

        @block.vector
        def _(dve):
            for tt in range(TT):
                dve.wait_ge(m.sem("turned"), tt + 1)
                if tt >= 2:
                    dve.wait_ge(m.sem(f"stored{tt % 2}"), 16 * (tt // 2))
                b = 2 * (tt % 4)
                nc.vector.tensor_copy(m.xrow[:, tt % 2, :], m.ps[:, b:b + 2, :].rearrange("p b c -> p (b c)")
                                      ).then_inc(m.sem("copied"), 1)

        @block.sync
        def _(sp):
            for tt in range(TT):
                sp.wait_ge(m.sem("copied"), tt + 1)
                dst = d["y_sample"][0, tt * P:(tt + 1) * P, :] if tt < CTX else d["y_prompt"][0, :, :]
                sp.dma_start(dst, m.xrow[:, tt % 2, :]).then_inc(m.sem(f"stored{tt % 2}"), 16)
            sp.wait_ge(m.sem("stored0"), 16 * 3)
            sp.wait_ge(m.sem("stored1"), 16 * 2)


def program(nc, d):
    with ExitStack() as ctx:
        m = Stages(nc, ctx)
        first_stage(nc, m, d)
        with nc.Fori(0, DEPTH) as L:
            def out_slabs(w, k0, nk, cols):
                return nk * cols, lambda sp, j, sem: load_out(sp, m, w, L, j, k0, nk, cols, j, sem), 16

            def ffn_slabs(f0):
                return SLAB, lambda sp, j, sem: load_ffn(sp, m, d, L, f0, j, j, sem), 32

            norm(nc, m, d, L, 0, (SLAB, lambda sp, j, sem: load_w_in(sp, m, d, L, C_LV + W256 * j, j, sem), 16))
            project_gla(nc, m, d, L)
            gla(nc, m, d, L, (SLAB, lambda sp, j, sem: load_w_in(sp, m, d, L, C_GQ + W256 * j, j, sem), 16))
            project_attention(nc, m, d, L)
            attention(nc, m, d, L, (SLAB, lambda sp, j, sem: load_merge(sp, m, d, L, 0, 0, j, sem), 16))
            merge(nc, m, d, L, out_slabs(d["w_out"], 0, KT, W256))
            project_out(nc, m, d, L, d["w_out"], 16, 0, KT, W256, m.hH, m.hL)
            norm(nc, m, d, L, 1, ffn_slabs(0))
            for f0, nf in ((0, 12), (12, 10)):
                ffn_in(nc, m, d, L, f0, nf, out_slabs(d["w_ffn_out"], f0, nf, P))
                project_out(nc, m, d, L, d["w_ffn_out"], 40, f0, nf, P, m.gH, m.gL, ffn_slabs(12) if f0 == 0 else None)
        last_stage(nc, m, d)


def constants():
    all_ = np.zeros((P, K_COLS), np.float32)
    all_[:, K_ID:K_ID + P] = np.eye(P)
    all_[:, K_ONE:K_ONE + P] = 1.0 / D
    all_[:, K_LAM + 4] = EPS
    lam = np.array([[-(0.8 - 0.6 * math.exp(-0.3 * l)), 1.0 - (0.8 - 0.6 * math.exp(-0.3 * l))]
                    for l in range(DEPTH)], np.float32)
    g = np.zeros((P, G_COLS), np.float32)
    j, i = np.meshgrid(np.arange(P), np.arange(P), indexing="ij")
    same = j // CH == i // CH
    g[:, G_MF:G_MF + P] = same & (j <= i)
    g[:, G_MB:G_MB + P] = same & (j >= i)
    g[:, G_CM:G_CM + T] = (np.arange(T) % CH != 0)
    t = np.arange(DEC)
    f = np.float32(10000.0) ** (-np.arange(16, dtype=np.float32) / np.float32(16))
    rope = np.zeros((P, 2, TT, HD), np.float32)
    rope[:, 0] = 1.0
    for half, pos in enumerate((t // 64, t % 64)):
        ang = (pos.astype(np.float32)[:, None] * f).reshape(4, P, 16).transpose(1, 0, 2)
        c = half * 32
        rope[:, 0, 0:4, c:c + 16] = rope[:, 0, 0:4, c + 16:c + 32] = np.cos(ang)
        rope[:, 1, 0:4, c:c + 16] = np.sin(ang)
        rope[:, 1, 0:4, c + 16:c + 32] = -np.sin(ang)
    return {"const_all": all_, "const_lam": lam, "const_gla": g, "const_rope": rope}


OUTS = [("y_prompt", (1, SEQ, D)), ("y_sample", (1, DEC, D)), ("new_gqa_k", (1, DEPTH, SEQ, 2, HD)),
        ("new_gqa_v", (1, DEPTH, SEQ, 2, HD)), ("new_state_gla", (1, DEPTH, 2, 4, HD, P)),
        ("new_diff_k", (1, DEPTH, SEQ, 4, 2, HD)), ("new_diff_v", (1, DEPTH, SEQ, 4, P))]


def kernel(**inputs):
    import concourse.bacc as bacc
    from concourse.bass_utils import run_bass_kernel_spmd

    nc = bacc.Bacc("TRN2", target_bir_lowering=False, num_devices=1)
    arrays, d = {}, {}
    for name, a in {**inputs, **constants()}.items():
        a = np.ascontiguousarray(a)
        arrays[f"in_{name}"] = a
        d[name] = nc.dram_tensor(f"in_{name}", a.shape, F32, kind="ExternalInput").ap()
    for name, shape in OUTS:
        d[name] = nc.dram_tensor(f"out_{name}", shape, F32, kind="ExternalOutput").ap()
    program(nc, d)
    r = run_bass_kernel_spmd(nc, [arrays], core_ids=[0])
    return tuple(r.results[0][f"out_{name}"] for name, _ in OUTS)
```
